# Optimizing a Trainium2 kernel written in Bass

```python
import jax
import jax.numpy as jnp
from jax import lax
import numpy as np

D_MODEL = 1024
BATCH = 1
SEQ = 256
DEPTH = 1
DEC_BATCH = 8
DEC_SEQ = 8
PAST_LEN = 2048
PAGE_SIZE = 128

N_META = 16
HA_HEADS = 4
HA_DK = 128
HA_DV = 128
HA_QK = HA_HEADS * HA_DK
HA_WIDTH = HA_HEADS * HA_DV
HA_IN = 2 * HA_QK + 2 * HA_WIDTH
HA_CHUNK = 64
HB_HEADS = 8
HB_HEAD = 64
HB_WIDTH = HB_HEADS * HB_HEAD
LORA_W = 64
LORA_A = 64
LORA_G = 128
RWKV_IN = 3 * HB_WIDTH + LORA_W + LORA_A + LORA_G
D_IN = HA_IN + RWKV_IN
MIX_WIDTH = HA_WIDTH + HB_WIDTH
PEER_HEADS = 8
N_KEYS = 128
N_EXPERTS = N_KEYS * N_KEYS
D_KEY = 256
PEER_TOPK = 16
PEER_BLOCK = 256
EPS = 1e-6
GN_EPS = 64e-5

kernel_name = 'hymba_hgrn2_rwkv7_peer_step'

def rmsnorm(x, g):
    xf = x.astype(jnp.float32)
    y = xf * lax.rsqrt(jnp.mean(xf * xf, axis=-1, keepdims=True) + EPS)
    return (y * g.astype(jnp.float32)).astype(x.dtype)

def hgrn2_chunked(q, k, v, logf, s0, chunk):
    b_, l_, h_, _ = q.shape
    n = l_ // chunk

    def to_chunks(t):
        return t.reshape(b_, n, chunk, h_, t.shape[-1]).transpose(1, 0, 3, 2, 4)

    causal = jnp.tril(jnp.ones((chunk, chunk), dtype=bool))[:, :, None]

    def step(s, inp):
        qc, kc, vc, gc = inp
        cum = jnp.cumsum(gc, axis=2)
        rel = jnp.where(causal, cum[:, :, :, None, :] - cum[:, :, None, :, :], -jnp.inf)
        scores = jnp.einsum('bhtd,bhsd,bhtsd->bhts', qc, kc, jnp.exp(rel))
        o = (jnp.einsum('bhts,bhse->bhte', scores, vc)
             + jnp.einsum('bhtd,bhde->bhte', qc * jnp.exp(cum), s))
        last = cum[:, :, -1:, :]
        s_new = (jnp.exp(last[:, :, 0, :])[..., None] * s
                 + jnp.einsum('bhsd,bhse->bhde', kc * jnp.exp(last - cum), vc))
        return s_new, o

    s_fin, o = lax.scan(step, s0, (to_chunks(q), to_chunks(k), to_chunks(v), to_chunks(logf)))
    return o.transpose(1, 0, 3, 2, 4).reshape(b_, l_, h_, v.shape[-1]), s_fin

def rwkv7_scan(r, w, k, v, kk, a, s0):
    def step(s, inp):
        rt, wt, kt, vt, kkt, at = inp
        sa = jnp.einsum('bhvk,bhk->bhv', s, -kkt)
        s = (s * wt[:, :, None, :] + sa[..., None] * (kkt * at)[:, :, None, :]
             + vt[..., None] * kt[:, :, None, :])
        return s, jnp.einsum('bhvk,bhk->bhv', s, rt)

    xs = tuple(t.transpose(1, 0, 2, 3) for t in (r, w, k, v, kk, a))
    s_fin, y = lax.scan(step, s0, xs)
    return y.transpose(1, 0, 2, 3), s_fin

def time_mix(h, shift_prev, s_hgrn, s_rwkv, segments, lb, w_in, hgrn_norm, mu_shift,
             w0, w_w2, a0, a_w2, g_w2, k_k, k_a, r_k, ln_w, ln_b, w_out):
    f32 = jnp.float32
    bsz, seq, _ = h.shape
    z = h @ w_in
    za, zb = z[..., :HA_IN], z[..., HA_IN:]

    zq, zf, zi, zo = jnp.split(za, [HA_QK, 2 * HA_QK, 2 * HA_QK + HA_WIDTH], axis=-1)
    zf = zf.astype(f32)
    logf = jnp.log(lb + (1.0 - lb) * jax.nn.sigmoid(zf))
    kin = (1.0 - lb) * jax.nn.sigmoid(-zf)
    qa = jax.nn.silu(zq.astype(f32)).reshape(bsz, seq, HA_HEADS, HA_DK)
    ia = zi.astype(f32).reshape(bsz, seq, HA_HEADS, HA_DV)
    kin = kin.reshape(bsz, seq, HA_HEADS, HA_DK)
    logf = logf.reshape(bsz, seq, HA_HEADS, HA_DK)
    outs = []
    s_a = s_hgrn
    start = 0
    for length, chunk in segments:
        sl = slice(start, start + length)
        o_seg, s_a = hgrn2_chunked(qa[:, sl], kin[:, sl], ia[:, sl], logf[:, sl], s_a, chunk)
        outs.append(o_seg)
        start += length
    oa = jnp.concatenate(outs, axis=1)
    oa = oa * lax.rsqrt(jnp.mean(oa * oa, axis=-1, keepdims=True) + EPS)
    oa = (oa * hgrn_norm.astype(f32).reshape(HA_HEADS, HA_DV)).reshape(bsz, seq, HA_WIDTH)
    oa = oa * jax.nn.silu(zo.astype(f32))

    prev = jnp.concatenate([shift_prev[:, None].astype(zb.dtype), zb[:, :-1]], axis=1)
    zm = zb + (prev - zb) * mu_shift
    new_shift = zb[:, -1]
    r, k, v, dw, da, dg = (t.astype(f32) for t in jnp.split(
        zm, [HB_WIDTH, 2 * HB_WIDTH, 3 * HB_WIDTH, 3 * HB_WIDTH + LORA_W,
             3 * HB_WIDTH + LORA_W + LORA_A], axis=-1))
    w_raw = w0 + jnp.tanh(dw) @ w_w2
    decay = jnp.exp(-jnp.exp(-jax.nn.softplus(-w_raw) - 0.5))
    a = jax.nn.sigmoid(a0 + da @ a_w2)
    g = jax.nn.sigmoid(dg) @ g_w2
    hd = lambda t: t.reshape(bsz, seq, HB_HEADS, HB_HEAD)
    kk = hd(k * k_k)
    kk = kk / jnp.maximum(jnp.sqrt(jnp.sum(kk * kk, axis=-1, keepdims=True)), 1e-12)
    k = k * (1.0 + (a - 1.0) * k_a)
    rh, kh, vh = hd(r), hd(k), hd(v)
    y, s_b = rwkv7_scan(rh, hd(decay), kh, vh, kk, hd(a), s_rwkv)
    mu = jnp.mean(y, axis=-1, keepdims=True)
    var = jnp.mean(jnp.square(y - mu), axis=-1, keepdims=True)
    yn = ((y - mu) * lax.rsqrt(var + GN_EPS) * ln_w.astype(f32).reshape(HB_HEADS, HB_HEAD)
          + ln_b.astype(f32).reshape(HB_HEADS, HB_HEAD))
    bonus = jnp.sum(rh * kh * r_k.astype(f32).reshape(HB_HEADS, HB_HEAD), axis=-1, keepdims=True) * vh
    ob = (yn + bonus).reshape(bsz, seq, HB_WIDTH) * g

    out = jnp.concatenate([oa, ob], axis=-1).astype(h.dtype) @ w_out
    return out, s_a, s_b, new_shift

def peer(h, w_q, sub_keys, u_tab, v_tab):
    bsz, seq, d = h.shape
    n_tok = bsz * seq
    n_blk = -(-n_tok // PEER_BLOCK)
    t = jnp.pad(h.reshape(n_tok, d), ((0, n_blk * PEER_BLOCK - n_tok), (0, 0)))
    t = t.reshape(n_blk, PEER_BLOCK, d)

    def block(xb):
        q = (xb @ w_q).reshape(PEER_BLOCK, PEER_HEADS, 2, D_KEY // 2)
        s = jnp.einsum('thpc,pnc->thpn', q, sub_keys).astype(jnp.float32)
        sv, si = lax.top_k(s, PEER_TOPK)
        cand = (sv[:, :, 0, :, None] + sv[:, :, 1, None, :]).reshape(
            PEER_BLOCK, PEER_HEADS, PEER_TOPK * PEER_TOPK)
        best, flat = lax.top_k(cand, PEER_TOPK)
        i1 = jnp.take_along_axis(si[:, :, 0], flat // PEER_TOPK, axis=-1)
        i2 = jnp.take_along_axis(si[:, :, 1], flat % PEER_TOPK, axis=-1)
        idx = i1 * N_KEYS + i2
        gate = jax.nn.softmax(best, axis=-1)
        act = jax.nn.gelu(jnp.einsum('thkd,td->thk', u_tab[idx], xb).astype(jnp.float32),
                          approximate=False)
        coef = (gate * act).astype(xb.dtype)
        return jnp.einsum('thk,thkd->td', coef, v_tab[idx])

    out = lax.map(block, t).reshape(n_blk * PEER_BLOCK, d)[:n_tok]
    return out.reshape(bsz, seq, d)

def trunk(x, st_hgrn, st_rwkv, st_shift, segments, norm1, w_in, lb_theta, hgrn_norm, mu_shift,
          w0, w_w2, a0, a_w2, g_w2, k_k, k_a, r_k, ln_w, ln_b, w_out, norm2,
          peer_wq, peer_keys, peer_u, peer_v, norm_f):
    lb_all = jnp.cumsum(jax.nn.softmax(lb_theta.astype(jnp.float32), axis=0), axis=0)
    new_h, new_r, new_s = [], [], []
    for l in range(DEPTH):
        mix, sh, sr, ss = time_mix(
            rmsnorm(x, norm1[l]), st_shift[l], st_hgrn[l].astype(jnp.float32),
            st_rwkv[l].astype(jnp.float32), segments, lb_all[l], w_in[l], hgrn_norm[l],
            mu_shift[l], w0[l], w_w2[l], a0[l], a_w2[l], g_w2[l], k_k[l], k_a[l], r_k[l],
            ln_w[l], ln_b[l], w_out[l])
        x = x + mix
        x = x + peer(rmsnorm(x, norm2[l]), peer_wq[l], peer_keys[l], peer_u[l], peer_v[l])
        new_h.append(sh)
        new_r.append(sr)
        new_s.append(ss)
    return rmsnorm(x, norm_f), jnp.stack(new_h), jnp.stack(new_r), jnp.stack(new_s)

def setup_inputs(seed: int = 0) -> dict:
    key = jax.random.key(seed)
    ks = iter(jax.random.split(key, 40))
    nrm = lambda shape, scale: scale * jax.random.normal(next(ks), shape, jnp.float32)
    return {
        'x_prompt': nrm((BATCH, SEQ, D_MODEL), 1.0),
        'x_sample': nrm((DEC_BATCH, DEC_SEQ, D_MODEL), 1.0),
        'state_hgrn': nrm((DEPTH, DEC_BATCH, HA_HEADS, HA_DK, HA_DV), 0.5),
        'state_rwkv': nrm((DEPTH, DEC_BATCH, HB_HEADS, HB_HEAD, HB_HEAD), 0.3),
        'state_shift': nrm((DEPTH, DEC_BATCH, RWKV_IN), 1.0),
        'meta_tokens': nrm((N_META, D_MODEL), 1.0),
        'norm1': 1.0 + nrm((DEPTH, D_MODEL), 0.02),
        'w_in': nrm((DEPTH, D_MODEL, D_IN), D_MODEL ** -0.5),
        'lb_theta': nrm((DEPTH + 1, HA_QK), 0.3),
        'hgrn_norm': 1.0 + nrm((DEPTH, HA_WIDTH), 0.02),
        'mu_shift': jax.random.uniform(next(ks), (DEPTH, RWKV_IN), jnp.float32),
        'w0': jax.random.uniform(next(ks), (DEPTH, HB_WIDTH), jnp.float32, -5.0, 0.5),
        'w_w2': nrm((DEPTH, LORA_W, HB_WIDTH), 0.05),
        'a0': nrm((DEPTH, HB_WIDTH), 0.1),
        'a_w2': nrm((DEPTH, LORA_A, HB_WIDTH), 0.05),
        'g_w2': nrm((DEPTH, LORA_G, HB_WIDTH), LORA_G ** -0.5),
        'k_k': 0.85 + nrm((DEPTH, HB_WIDTH), 0.05),
        'k_a': 1.0 + nrm((DEPTH, HB_WIDTH), 0.05),
        'r_k': nrm((DEPTH, HB_WIDTH), 0.1),
        'ln_w': 1.0 + nrm((DEPTH, HB_WIDTH), 0.02),
        'ln_b': nrm((DEPTH, HB_WIDTH), 0.01),
        'w_out': nrm((DEPTH, MIX_WIDTH, D_MODEL), 0.5 * MIX_WIDTH ** -0.5),
        'norm2': 1.0 + nrm((DEPTH, D_MODEL), 0.02),
        'peer_wq': nrm((DEPTH, D_MODEL, PEER_HEADS * D_KEY), D_MODEL ** -0.5),
        'peer_keys': nrm((DEPTH, 2, N_KEYS, D_KEY // 2), (D_KEY // 2) ** -0.5),
        'peer_u': nrm((DEPTH, N_EXPERTS, D_MODEL), D_MODEL ** -0.5),
        'peer_v': nrm((DEPTH, N_EXPERTS, D_MODEL), 0.5),
        'norm_f': 1.0 + nrm((D_MODEL,), 0.02),
    }

def reference(x_prompt, x_sample, state_hgrn, state_rwkv, state_shift, meta_tokens, norm1, w_in,
              lb_theta, hgrn_norm, mu_shift, w0, w_w2, a0, a_w2, g_w2, k_k, k_a, r_k, ln_w, ln_b,
              w_out, norm2, peer_wq, peer_keys, peer_u, peer_v, norm_f):
    f32 = jnp.float32
    bp, sp, d = x_prompt.shape
    bs, ss = x_sample.shape[0], x_sample.shape[1]

    xp = jnp.concatenate([jnp.broadcast_to(meta_tokens[None].astype(x_prompt.dtype), (bp, N_META, d)),
                          x_prompt], axis=1)
    yp, hgrn_p, rwkv_p, shift_p = trunk(
        xp, jnp.zeros((DEPTH, bp, HA_HEADS, HA_DK, HA_DV), f32),
        jnp.zeros((DEPTH, bp, HB_HEADS, HB_HEAD, HB_HEAD), f32),
        jnp.zeros((DEPTH, bp, RWKV_IN), x_prompt.dtype),
        ((N_META, N_META), (sp, min(HA_CHUNK, sp))),
        norm1, w_in, lb_theta, hgrn_norm, mu_shift, w0, w_w2, a0, a_w2, g_w2, k_k, k_a, r_k,
        ln_w, ln_b, w_out, norm2, peer_wq, peer_keys, peer_u, peer_v, norm_f)
    y_prompt = yp[:, N_META:]

    y_sample, hgrn_s, rwkv_s, shift_s = trunk(
        x_sample, state_hgrn, state_rwkv, state_shift, ((ss, ss),),
        norm1, w_in, lb_theta, hgrn_norm, mu_shift, w0, w_w2, a0, a_w2, g_w2, k_k, k_a, r_k,
        ln_w, ln_b, w_out, norm2, peer_wq, peer_keys, peer_u, peer_v, norm_f)

    return (y_prompt, y_sample,
            hgrn_p.astype(state_hgrn.dtype), rwkv_p.astype(state_rwkv.dtype),
            shift_p.astype(state_shift.dtype),
            hgrn_s.astype(state_hgrn.dtype), rwkv_s.astype(state_rwkv.dtype),
            shift_s.astype(state_shift.dtype))


_drawn_inputs = setup_inputs


def setup_inputs(seed=0):
    import zlib

    import numpy as np

    out = dict(_drawn_inputs(seed))
    spreads = {}
    factors = {'hgrn_norm': 3.094, 'ln_w': 3.539, 'ln_b': 15.288, 'norm_f': 9.692}
    for name, (base, spread) in spreads.items():
        noise = np.random.default_rng([zlib.crc32(name.encode()), seed]).standard_normal(out[name].shape)
        drawn = base * np.exp(spread * noise) if base else spread * noise
        out[name] = jnp.asarray(drawn.astype(out[name].dtype))
    for name, factor in factors.items():
        out[name] = (out[name] * factor).astype(out[name].dtype)
    return out
```

```python
from contextlib import ExitStack

import numpy as np

import concourse.bass as bass
from concourse import mybir

ALU = mybir.AluOpType
ACT = mybir.ActivationFunctionType
AX = mybir.AxisListType.X
F32 = mybir.dt.float32
F32R = mybir.dt.float32r
U32 = mybir.dt.uint32

P = 128
D = 1024
KD = D // P
META, SEQ, NS, LS = 16, 256, 8, 8
PROMPT = META + SEQ
SAMP0 = 288
C = SAMP0 + NS * LS
TW = [128, 128, C - 256]
HA, HB, HN = 4, 8, 64
FB = 14
EPS, GN_EPS = 1e-6, 64e-5
NT = SEQ + NS * LS
PT = [(0, 128), (128, 128), (256, 64)]
PH, NK, TOPK = 8, 128, 16
NBLK = NK
NMASK = 12
(M_ID, M_BU, M_BL, M_EU, M_SU, M_IU, M_TBU, M_TBL, M_TIU, M_HI, M_HO, M_B64) = range(NMASK)


def shape_constants():
    s, t = np.arange(P)[:, None], np.arange(P)[None, :]
    blk = lambda n: s // n == t // n
    seq = np.where(np.arange(P) < 16, 100, np.where(np.arange(P) < 32, 101, np.arange(P) // 8))
    same = seq[:, None] == seq[None, :]
    m = np.zeros((P, NMASK, P), np.float32)
    m[:, M_ID] = s == t
    m[:, M_BU] = blk(16) & (s < t)
    m[:, M_BL] = blk(16) & (s > t)
    m[:, M_EU] = blk(64) & ~blk(16) & (s < t)
    m[:, M_SU] = blk(64) & (s < t)
    m[:, M_IU] = blk(64) & (s <= t)
    m[:, M_TBU] = same & (s < t)
    m[:, M_TBL] = same & (s > t)
    m[:, M_TIU] = same & (s <= t)
    m[:, M_HI] = blk(16) & (s <= t)
    m[:, M_HO] = blk(32) & ~blk(16) & (s < t)
    m[:, M_B64] = blk(64)
    col = np.arange(C)
    start = np.where(col < PROMPT, col % 64 == 0, np.where(col < SAMP0, col == PROMPT, col % 8 == 0))
    restart = np.broadcast_to(np.where(start, 0.0, 1.0), (P, C)).astype(np.float32)
    seq9 = np.zeros((P, 9), np.float32)
    seq9[:16, 8] = 1
    for n in range(NS):
        seq9[32 + 8 * n:40 + 8 * n, n] = 1
    x = np.arange(144)
    pat = np.stack([x % 16 == 0, x % 8 == 0]).astype(np.float32)
    misc = np.concatenate([restart, seq9, np.broadcast_to(np.arange(P, dtype=np.float32), (P, P)),
                           np.broadcast_to(pat.reshape(1, 288), (P, 288)), np.ones((P, P), np.float32)], axis=1)
    return m, np.ascontiguousarray(misc.astype(np.float32))


NMISC = C + 9 + P + 288 + P


def build_program(nc, inp, out):
    with ExitStack() as whole:
        names = [0]

        def sem(name):
            names[0] += 1
            return whole.enter_context(nc.semaphore(f"{name}_{names[0]}"))

        def linker(eng, s):
            n = [0]

            def link(ins):
                n[0] += 1
                ins.then_inc(s, 1)
                eng.wait_ge(s, n[0])
            return link

        class Mem:
            def __init__(self):
                self.ctx = ExitStack()

            def sb(self, name, shape, dt=F32):
                names[0] += 1
                return self.ctx.enter_context(nc.sbuf_tensor(f"{name}_{names[0]}", shape, dt))

            def ps(self, name, shape):
                names[0] += 1
                return self.ctx.enter_context(nc.psum_tensor(f"{name}_{names[0]}", shape, F32))

            def free(self):
                self.ctx.close()

        base = Mem()
        ident = base.sb("identity", [P, P])
        iota = base.sb("iota", [P, P])
        feat = base.sb("feat", [P, NFEAT])
        epsc = base.sb("epsc", [P, 4])
        xh = base.sb("xh", [P, KD, NT], F32R)
        xl = base.sb("xl", [P, KD, NT], F32R)
        mask_mem = Mem()
        masks = mask_mem.sb("masks", [P, NMASK, P])
        misc = mask_mem.sb("misc", [P, NMISC])
        restart = misc[:, 0:C]
        seq9 = misc[:, C:C + 9]
        pat16 = misc[:, C + 9 + P:C + 9 + P + 144]
        pat8 = misc[:, C + 9 + P + 144:C + 9 + P + 288]
        ones = misc[:, C + 9 + P + 288:C + 9 + P + 288 + P]
        x1_dram = nc.dram_tensor("x1_scratch", [NT, D], F32).ap()
        rt_dram = nc.dram_tensor("rt_scratch", [P, 3, NT], F32).ap()

        def col(name, i=0, n=1):
            return feat[:, FEAT[name] + i:FEAT[name] + i + n]

        mix_mem = Mem()
        mixT = mix_mem.sb("mixT", [P, 8, C])
        zb_mem = Mem()
        zbT = zb_mem.sb("zbT", [P, FB, 289 + 9 * NS])
        za_mem = Mem()
        qT = za_mem.sb("qT", [P, HA, C])
        fT = za_mem.sb("fT", [P, HA, C])
        kT = za_mem.sb("kT", [P, HA, C])
        zoT = za_mem.sb("zoT", [P, HA, C])
        vtok = za_mem.sb("vtok", [P, 3, HA, P])
        in_mem = Mem()
        xnT = in_mem.sb("xnT", [P, KD, C])
        wslot = in_mem.sb("wslot", [P, 4, KD, P])
        wzi = in_mem.sb("wzi", [P, KD, 512])
        sig = in_mem.sb("sig", [P, 2, 2, C])
        shift0 = in_mem.sb("shift0", [P, FB, NS])
        lbt = in_mem.sb("lbt", [P, 6, HA])
        t1 = Mem()
        x = t1.sb("x", [P, 3, D])
        sq = t1.sb("sq", [P, D])
        rs = t1.sb("rs", [P, 16])
        pst = t1.ps("pst", [P, 2, 4, P])

        x_in, c_in = sem("x_in"), sem("c_in")
        sq_done, rt_done, rstd_done, xn_done, dv1 = (sem(n) for n in ("sq", "rt", "rstd", "xn", "dv1"))
        tr_full, tr_free = sem("tr_full"), sem("tr_free")
        const_ready = sem("const_ready")
        with nc.Block() as block:
            @block.sync
            def _(sp):
                sp.dma_start(x[:], inp["x_rows"].rearrange("k p d -> p k d")).then_inc(x_in, 16)
                sp.dma_start(masks[:], inp["masks"]).then_inc(c_in, 16)
                sp.dma_start(misc[:], inp["misc"]).then_inc(c_in, 16)
                sp.dma_start(feat[:], inp["feat"]).then_inc(c_in, 16)
                sp.dma_start(ident[:], inp["masks"][:, M_ID]).then_inc(c_in, 16)
                sp.dma_start(iota[:], inp["misc"][:, C + 9:C + 9 + P]).then_inc(c_in, 16)

            @block.gpsimd
            def _(pool):
                pool.memset(epsc[:, 0:1], EPS).then_inc(const_ready, 1)
                pool.memset(epsc[:, 1:2], GN_EPS).then_inc(const_ready, 1)
                pool.memset(epsc[:, 2:3], 0.0).then_inc(const_ready, 1)
                pool.memset(zbT[:, :, 0:1], 0.0).then_inc(const_ready, 1)

            @block.scalar
            def _(act):
                act.wait_ge(x_in, 16)
                act.wait_ge(const_ready, 4)
                for i in range(3):
                    if i:
                        act.wait_ge(sq_done, i)
                    act.activation(sq[:], x[:, i], ACT.Square, accum_out=rs[:, i:i + 1]).then_inc(sq_done, 1)
                act.wait_ge(sq_done, 3)
                act.activation(rs[:, 3:6], rs[:, 0:3], ACT.Sqrt, bias=epsc[:, 0:1], scale=1.0 / D).then_inc(rt_done, 1)

            @block.vector
            def _(dve):
                dve.wait_ge(rt_done, 1)
                dve.reciprocal(rs[:, 6:9], rs[:, 3:6]).then_inc(rstd_done, 1)
                dve.wait_ge(rstd_done, 1)
                for i in range(3):
                    dve.tensor_scalar(x[:, i], x[:, i], rs[:, 6 + i:7 + i], None, ALU.mult).then_inc(xn_done, 1)
                dve.wait_ge(c_in, 80)
                for i in range(3):
                    for j in range(KD):
                        n = KD * i + j
                        if n % 4 == 0:
                            dve.wait_ge(tr_full, n // 4 + 1)
                        w = TW[i]
                        ins = dve.tensor_scalar(xnT[:, j, P * i:P * i + w], pst[:, n // 4 % 2, n % 4, 0:w],
                                                col("norm1", j), None, ALU.mult)
                        if n % 4 == 3:
                            ins.then_inc(tr_free, 1)

            @block.tensor
            def _(pe):
                pe.wait_ge(c_in, 80)
                for n in range(3 * KD):
                    i, j = divmod(n, KD)
                    if j == 0:
                        pe.wait_ge(xn_done, i + 1)
                    if n % 4 == 0 and n >= 8:
                        pe.wait_ge(tr_free, n // 4 - 1)
                    ins = pe.transpose(pst[:, n // 4 % 2, n % 4, :], x[:, i, P * j:P * j + P], ident[:])
                    if n % 4 == 3:
                        ins.then_inc(tr_full, 1)
        t1.free()

        tiles = [("q", i) for i in range(4)] + [("f", i) for i in range(4)] + [("o", i) for i in range(4)] + \
                [("b", i) for i in range(FB)]
        NF = len(tiles)
        t2 = Mem()
        pz = t2.ps("pz", [P, 8, 512])
        w_in_slot = [sem(f"w_in_slot{i}") for i in range(4)]
        zi_in, sh_in = sem("zi_in"), sem("sh_in")
        z_full, z_act, z_dve, z_tok, dv2, a2, shift_copied = (
            sem(n) for n in ("z_full", "z_act", "z_dve", "z_tok", "dv2", "a2", "shift_copied"))
        with nc.Block() as block:
            @block.sync
            def _(sp):
                sp.dma_start(wzi[:], inp["w_zi"]).then_inc(zi_in, 16)
                sp.dma_start(shift0[:], inp["shift0"]).then_inc(sh_in, 16)
                for n in range(NF):
                    if n >= 4:
                        sp.wait_ge(z_full, 3 + n - 3)
                    sp.dma_start(wslot[:, n % 4], inp["w_tiles"][n]).then_inc(w_in_slot[n % 4], 16)

            @block.tensor
            def _(pe):
                pe.wait_ge(zi_in, 16)
                for i in range(3):
                    for k in range(KD):
                        ins = pe.matmul(pz[0:TW[i], i, :], xnT[:, k, P * i:P * i + TW[i]], wzi[:, k, :],
                                        start=k == 0, stop=k == KD - 1)
                    ins.then_inc(z_full, 1)
                for n in range(NF):
                    bank = (n + 3) % 8
                    if n >= 5:
                        m = n - 8
                        if m < 0:
                            pe.wait_ge(z_tok, n - 4)
                        elif m < 12:
                            pe.wait_ge(z_dve, m + 1)
                        else:
                            pe.wait_ge(z_act, m + 1)
                    pe.wait_ge(w_in_slot[n % 4], 16 * (n // 4 + 1))
                    for k in range(KD):
                        ins = pe.matmul(pz[:, bank, 0:C], wslot[:, n % 4, k], xnT[:, k],
                                        start=k == 0, stop=k == KD - 1)
                    ins.then_inc(z_full, 1)

            @block.scalar
            def _(act):
                act.wait_ge(a2, 1)
                act.activation(lbt[:, 2:4], lbt[:, 0:2], ACT.Exp).then_inc(a2, 1)
                for n, (kind, i) in enumerate(tiles):
                    bank = (n + 3) % 8
                    act.wait_ge(z_full, 4 + n)
                    if kind in "qfo" and n >= 2:
                        act.wait_ge(z_dve, n - 1)
                    if kind in "qo":
                        act.activation(sig[:, n % 2, 0], pz[:, bank, 0:C], ACT.Sigmoid).then_inc(z_act, 1)
                    elif kind == "f":
                        act.activation(sig[:, n % 2, 0], pz[:, bank, 0:C], ACT.Sigmoid)
                        act.activation(sig[:, n % 2, 1], pz[:, bank, 0:C], ACT.Sigmoid, scale=-1.0).then_inc(z_act, 1)
                    else:
                        act.activation(zbT[:, i, 1:289], pz[:, bank, 0:288], ACT.Copy)
                        act.activation(zbT[:, i, 289:361].rearrange("p (s l) -> p s l", l=9)[:, :, 1:9],
                                       pz[:, bank, 288:C].rearrange("p (s l) -> p s l", l=8),
                                       ACT.Copy).then_inc(z_act, 1)

            @block.vector
            def _(dve):
                link = linker(dve, dv2)
                th0, th1 = col("theta0", 0, 4), col("theta1", 0, 4)
                link(dve.tensor_tensor(lbt[:, 0], th0, th1, ALU.max))
                dve.tensor_tensor(lbt[:, 1], th0, lbt[:, 0], ALU.subtract)
                link(dve.tensor_tensor(lbt[:, 2], th1, lbt[:, 0], ALU.subtract))
                link(dve.tensor_copy(lbt[:, 0], lbt[:, 1]))
                dve.tensor_copy(lbt[:, 1], lbt[:, 2]).then_inc(a2, 1)
                dve.wait_ge(sh_in, 16)
                dve.tensor_copy(zbT[:, :, 289:361].rearrange("p f (s l) -> p f s l", l=9)[:, :, :, 0],
                                shift0[:]).then_inc(shift_copied, 1)
                dve.wait_ge(a2, 2)
                link(dve.tensor_tensor(lbt[:, 4], lbt[:, 2], lbt[:, 3], ALU.add))
                link(dve.reciprocal(lbt[:, 5], lbt[:, 4]))
                link(dve.tensor_tensor(lbt[:, 0], lbt[:, 2], lbt[:, 5], ALU.mult))
                link(dve.tensor_scalar(lbt[:, 1], lbt[:, 0], -1.0, 1.0, ALU.mult, ALU.add))
                for i in range(3):
                    dve.wait_ge(z_full, i + 1)
                    dve.tensor_copy(vtok[0:TW[i], i], pz[0:TW[i], i, :].rearrange("p (h e) -> p h e", e=P)) \
                        .then_inc(z_tok, 1)
                for n, (kind, i) in enumerate(tiles[:12]):
                    bank = (n + 3) % 8
                    dve.wait_ge(z_act, n + 1)
                    if kind in "qo":
                        dst = qT if kind == "q" else zoT
                        dve.tensor_tensor(dst[:, i], pz[:, bank, 0:C], sig[:, n % 2, 0], ALU.mult).then_inc(z_dve, 1)
                    else:
                        dve.tensor_scalar(fT[:, i], sig[:, n % 2, 0], lbt[:, 1, i:i + 1], lbt[:, 0, i:i + 1],
                                          ALU.mult, ALU.add)
                        dve.tensor_scalar(kT[:, i], sig[:, n % 2, 1], lbt[:, 1, i:i + 1], None,
                                          ALU.mult).then_inc(z_dve, 1)
        t2.free()
        in_mem.free()
        NB = SAMP0 // 16
        h_mem = Mem()
        scT = h_mem.sb("scT", [P, 3, HA, P])
        q2 = h_mem.sb("q2", [P, HA, C])
        k2h = h_mem.sb("k2h", [P, HA, C])
        ktok = h_mem.sb("ktok", [P, 3, HA, P])
        f16 = h_mem.sb("f16", [P, HA, NB])
        f8 = h_mem.sb("f8", [P, HA, NS])
        f32c = h_mem.sb("f32c", [P, HA, NB // 2])
        hp_mem = Mem()
        prod16 = hp_mem.sb("prod16", [P, 2, HA, NB, 16])
        prod8 = hp_mem.sb("prod8", [P, 2, HA, NS, LS])
        suf16 = hp_mem.sb("suf16", [P, HA, NB, 16])
        suf8 = hp_mem.sb("suf8", [P, HA, NS, LS])
        offm = hp_mem.sb("offm", [P, 2, HA, P])
        ps_h = Mem()
        psI = ps_h.ps("psI", [P, HA, 512])
        psS = ps_h.ps("psS", [P, 512])
        psO = ps_h.ps("psO", [P, 2, HA, P])
        psK = ps_h.ps("psK", [P, HA, P])
        prod_zero, prod_ready, prod_used, dv3, q_decayed, off_full, kt_full, kt_free, sc_done = (
            sem(n) for n in ("prod_zero", "prod_ready", "prod_used", "dv3", "q_decayed", "off_full", "kt_full",
                             "kt_free", "sc_done"))
        blocks16 = lambda a: a[:, :, 0:SAMP0].rearrange("p h (c j) -> p h c j", j=16)
        blocks8 = lambda a: a[:, :, SAMP0:C].rearrange("p h (c j) -> p h c j", j=8)
        with nc.Block() as block:
            @block.gpsimd
            def _(pool):
                pool.memset(prod16[:], 0.0).then_inc(prod_zero, 1)
                pool.memset(prod8[:], 0.0).then_inc(prod_zero, 1)
                pool.memset(suf16[:], 1.0).then_inc(prod_zero, 1)
                pool.memset(suf8[:], 1.0).then_inc(prod_zero, 1)

            @block.vector
            def _(dve):
                link = linker(dve, dv3)
                q16, f16v, k16 = blocks16(qT), blocks16(fT), blocks16(kT)
                q8, f8v, k8 = blocks8(qT), blocks8(fT), blocks8(kT)
                dve.wait_ge(prod_zero, 4)
                for n in range(16):
                    i, j = 15 - n, 7 - n
                    if n:
                        r16 = q16[:, :, :, i + 1:16]
                        ins = dve.tensor_tensor(r16, r16, f16v[:, :, :, i + 1:i + 2].to_broadcast([P, HA, NB, n]), ALU.mult)
                        if 0 < n < 8:
                            r8 = q8[:, :, :, j + 1:8]
                            ins = dve.tensor_tensor(r8, r8, f8v[:, :, :, j + 1:j + 2].to_broadcast([P, HA, NS, n]), ALU.mult)
                        link(ins)
                    if n >= 2:
                        dve.wait_ge(prod_used, n - 1)
                    ins = dve.tensor_tensor(prod16[:, n % 2, :, :, i:16], q16[:, :, :, i:16],
                                            k16[:, :, :, i:i + 1].to_broadcast([P, HA, NB, n + 1]), ALU.mult)
                    if n < 8:
                        ins = dve.tensor_tensor(prod8[:, n % 2, :, :, j:8], q8[:, :, :, j:8],
                                                k8[:, :, :, j:j + 1].to_broadcast([P, HA, NS, n + 1]), ALU.mult)
                    ins.then_inc(prod_ready, 1)
                dve.tensor_tensor(q16, q16, f16v[:, :, :, 0:1].to_broadcast([P, HA, NB, 16]), ALU.mult)
                link(dve.tensor_tensor(q8, q8, f8v[:, :, :, 0:1].to_broadcast([P, HA, NS, 8]), ALU.mult))
                for i in range(14, -1, -1):
                    ins = dve.tensor_tensor(suf16[:, :, :, i:i + 1], suf16[:, :, :, i + 1:i + 2],
                                            f16v[:, :, :, i + 1:i + 2], ALU.mult)
                    if i < 7:
                        ins = dve.tensor_tensor(suf8[:, :, :, i:i + 1], suf8[:, :, :, i + 1:i + 2],
                                                f8v[:, :, :, i + 1:i + 2], ALU.mult)
                    link(ins)
                dve.tensor_tensor(k16, k16, suf16[:], ALU.mult)
                dve.tensor_tensor(k8, k8, suf8[:], ALU.mult)
                dve.tensor_tensor(f16[:], suf16[:, :, :, 0], f16v[:, :, :, 0], ALU.mult)
                dve.tensor_tensor(f8[:], suf8[:, :, :, 0], f8v[:, :, :, 0], ALU.mult).then_inc(q_decayed, 1)
                dve.wait_ge(q_decayed, 1)
                dve.tensor_copy(q2[:], qT[:])
                link(dve.tensor_copy(k2h[:], kT[:]))
                pairs = lambda a: a[:, :, 0:256].rearrange("p h (c b j) -> p h c b j", b=2, j=16)
                fe = f16[:, :, 0:16].rearrange("p h (c b) -> p h c b", b=2)
                for h in range(HA):
                    dve.tensor_tensor(pairs(q2)[:, h, :, 1], pairs(qT)[:, h, :, 1],
                                      fe[:, h, :, 0:1].to_broadcast([P, 8, 16]), ALU.mult)
                    dve.tensor_tensor(pairs(k2h)[:, h, :, 0], pairs(kT)[:, h, :, 0],
                                      fe[:, h, :, 1:2].to_broadcast([P, 8, 16]), ALU.mult)
                dve.tensor_copy(f32c[:, :, 8:9], f16[:, :, 16:17])
                dve.tensor_tensor(f32c[:, :, 0:8], fe[:, :, :, 0], fe[:, :, :, 1], ALU.mult).then_inc(q_decayed, 1)
                dve.wait_ge(off_full, 1)
                dve.wait_ge(prod_used, 16)
                mask = lambda m, n, w: masks[0:n, m:m + 1, 0:w].to_broadcast([n, HA, w])
                for i in range(2):
                    dve.tensor_tensor(offm[:, i], psO[:, i], mask(M_HO, P, P), ALU.mult)
                    dve.tensor_tensor(scT[:, i], psI[:, :, P * i:P * i + P], mask(M_HI, P, P), ALU.mult)
                dve.tensor_tensor(scT[0:96, 2, :, 0:32], psI[0:96, :, 256:288], mask(M_HI, 96, 32), ALU.mult)
                link(dve.tensor_tensor(scT[0:96, 2, :, 32:96], psS[0:96, 0:256].rearrange("p (h t) -> p h t", h=HA),
                                       masks[0:96, M_TIU:M_TIU + 1, 32:96].to_broadcast([96, HA, 64]), ALU.mult))
                dve.tensor_tensor(scT[:, 0:2], scT[:, 0:2], offm[:], ALU.add).then_inc(sc_done, 1)

            @block.tensor
            def _(pe):
                for n in range(16):
                    i, j = 15 - n, 7 - n
                    pe.wait_ge(prod_ready, n + 1)
                    for h in range(HA):
                        ins = pe.matmul(psI[:, h, 0:SAMP0], pat16[:, 16 - i:144 - i],
                                        prod16[:, n % 2, h].rearrange("p c j -> p (c j)"), start=n == 0, stop=n == 15)
                    if n < 8:
                        ins = pe.matmul(psS[:, 0:256], pat8[:, 8 - j:136 - j],
                                        prod8[:, n % 2].rearrange("p h c j -> p (h c j)"), start=n == 0, stop=n == 7)
                    ins.then_inc(prod_used, 1)
                pe.wait_ge(q_decayed, 1)
                for i in range(2):
                    for h in range(HA):
                        ins = pe.matmul(psO[:, i, h], kT[:, h, P * i:P * i + P], qT[:, h, P * i:P * i + P],
                                        start=True, stop=True)
                ins.then_inc(off_full, 1)
                pe.wait_ge(q_decayed, 2)
                for i in range(3):
                    if i:
                        pe.wait_ge(kt_free, i)
                    for h in range(HA):
                        ins = pe.transpose(psK[0:TW[i], h], k2h[:, h, P * i:P * i + TW[i]], ident[:])
                    ins.then_inc(kt_full, 1)

            @block.scalar
            def _(act):
                for i in range(3):
                    act.wait_ge(kt_full, i + 1)
                    act.activation(ktok[0:TW[i], i], psK[0:TW[i]], ACT.Copy).then_inc(kt_free, 1)
        ps_h.free()
        hp_mem.free()

        NCH = 9
        s_mem = Mem()
        sts = s_mem.sb("sts", [P, NCH, HA, P])
        sth = s_mem.sb("sth", [P, NS, HA, P])
        stn = s_mem.sb("stn", [P, NS, HA, P])
        vexp = s_mem.sb("vexp", [P, 2, NS, P])
        osq = s_mem.sb("osq", [P, HA, C])
        rsh = s_mem.sb("rsh", [P, 2, HA, C])
        ps4 = Mem()
        kv = ps4.ps("kv", [P, 4, 512])
        po = ps4.ps("po", [P, HA, 512])
        hs_in, vexp_ready, vexp_used, kv_full, kv_free, st_ready, o_full, sq_ready, ms_full, rt_h, dv4, hst_out = (
            sem(n) for n in ("hs_in", "vexp_ready", "vexp_used", "kv_full", "kv_free", "st_ready", "o_full",
                             "sq_ready", "ms_full", "rt_h", "dv4", "hst_out"))
        with nc.Block() as block:
            @block.sync
            def _(sp):
                sp.dma_start(sth[:], inp["state_h"]).then_inc(hs_in, 16)
                sp.wait_ge(st_ready, NCH)
                sp.dma_start(out["hgrn_p"], sts[:, NCH - 1]).then_inc(hst_out, 16)
                sp.wait_ge(st_ready, NCH + 2 * HA)
                sp.dma_start(out["hgrn_s"], stn[:]).then_inc(hst_out, 16)
                sp.wait_ge(hst_out, 32)

            @block.tensor
            def _(pe):
                for c in range(NCH):
                    if c >= 4:
                        pe.wait_ge(kv_free, c - 3)
                    b, w = 32 * c % P, 32 if c < 8 else 16
                    for h in range(HA):
                        ins = pe.matmul(kv[:, c % 4, P * h:P * h + P], ktok[b:b + w, c // 4, h], vtok[b:b + w, c // 4, h],
                                        start=True, stop=True)
                    ins.then_inc(kv_full, 1)
                for h in range(HA):
                    pe.wait_ge(vexp_ready, h + 1)
                    for g in range(2):
                        n = NCH + 2 * h + g
                        pe.wait_ge(kv_free, n - 3)
                        ins = pe.matmul(kv[:, n % 4, :], ktok[0:96, 2, h],
                                        vexp[0:96, h % 2, 4 * g:4 * g + 4].rearrange("p s e -> p (s e)"),
                                        start=True, stop=True)
                        ins.then_inc(kv_full, 1)
                pe.wait_ge(hs_in, 16)
                pe.wait_ge(st_ready, NCH)
                for h in range(HA):
                    for i in range(3):
                        pe.matmul(po[:, h, P * i:P * i + TW[i]], vtok[0:TW[i], i, h], scT[0:TW[i], i, h, 0:TW[i]],
                                  start=i == 0, stop=False, skip_group_check=True)
                    for c in range(1, NCH):
                        w = 32 if c < 8 else 16
                        pe.matmul(po[:, h, 32 * c:32 * c + w], sts[:, c - 1, h], q2[:, h, 32 * c:32 * c + w],
                                  start=False, stop=False, skip_group_check=True)
                    for s in range(NS):
                        t = SAMP0 + LS * s
                        ins = pe.matmul(po[:, h, t:t + LS], sth[:, s, h], q2[:, h, t:t + LS],
                                        start=False, stop=s == NS - 1, skip_group_check=True)
                    ins.then_inc(o_full, 1)
                for h in range(HA):
                    if h == 0:
                        pe.wait_ge(kv_free, NCH + 2 * HA)
                    pe.wait_ge(sq_ready, h + 1)
                    pe.matmul(kv[:, h, 0:C], ones, osq[:, h], start=True, stop=True).then_inc(ms_full, 1)

            @block.gpsimd
            def _(pool):
                for h in range(HA):
                    if h >= 2:
                        pool.wait_ge(kv_full, NCH + 2 * (h - 1))
                    pool.tensor_tensor(vexp[0:96, h % 2], vtok[0:96, 2, h:h + 1, :].to_broadcast([96, NS, P]),
                                       seq9[0:96, 0:NS].unsqueeze(2).to_broadcast([96, NS, P]), ALU.mult) \
                        .then_inc(vexp_ready, 1)

            @block.vector
            def _(dve):
                for c in range(NCH):
                    dve.wait_ge(kv_full, c + 1)
                    kvc = kv[:, c % 4, :].rearrange("p (h e) -> p h e", h=HA)
                    if c == 0:
                        ins = dve.tensor_copy(sts[:, 0], kvc)
                    else:
                        dve.wait_ge(st_ready, c)
                        for h in range(HA):
                            ins = dve.scalar_tensor_tensor(out=sts[:, c, h], in0=sts[:, c - 1, h], scalar=f32c[:, h, c:c + 1],
                                                           in1=kvc[:, h], op0=ALU.mult, op1=ALU.add)
                    ins.then_inc(st_ready, 1)
                    dve.wait_ge(st_ready, c + 1)
                    dve.sem_inc(kv_free, 1)
                dve.wait_ge(hs_in, 16)
                for h in range(HA):
                    for g in range(2):
                        n = NCH + 2 * h + g
                        dve.wait_ge(kv_full, n + 1)
                        for s in range(4):
                            ins = dve.scalar_tensor_tensor(out=stn[:, 4 * g + s, h], in0=sth[:, 4 * g + s, h],
                                                           scalar=f8[:, h, 4 * g + s:4 * g + s + 1],
                                                           in1=kv[:, n % 4, P * s:P * s + P], op0=ALU.mult, op1=ALU.add)
                        ins.then_inc(st_ready, 1)
                        dve.wait_ge(st_ready, n + 1)
                        dve.sem_inc(kv_free, 1)
                link = linker(dve, dv4)
                for h in range(HA):
                    dve.wait_ge(rt_h, h + 1)
                    link(dve.reciprocal(rsh[:, 1, h], rsh[:, 0, h]))
                    link(dve.scalar_tensor_tensor(out=rsh[:, 0, h], in0=po[:, h, 0:C], scalar=col("hgrn_norm", h),
                                                  in1=rsh[:, 1, h], op0=ALU.mult, op1=ALU.mult))
                    link(dve.tensor_tensor(mixT[:, h], rsh[:, 0, h], zoT[:, h], ALU.mult))

            @block.scalar
            def _(act):
                for h in range(HA):
                    act.wait_ge(o_full, h + 1)
                    act.activation(osq[:, h], po[:, h, 0:C], ACT.Square).then_inc(sq_ready, 1)
                for h in range(HA):
                    act.wait_ge(ms_full, h + 1)
                    act.activation(rsh[:, 0, h], kv[:, h, 0:C], ACT.Sqrt, bias=epsc[:, 0:1], scale=1.0 / P).then_inc(rt_h, 1)
        ps4.free()
        s_mem.free()
        h_mem.free()
        za_mem.free()
        CEXP = float(np.exp(-0.5))
        y_mem = Mem()
        gT = y_mem.sb("gT", [P, 4, C])
        bonusT = y_mem.sb("bonusT", [P, 4, C])
        ARx = y_mem.sb("ARx", [P, 4, 4, C])
        Bt = y_mem.sb("Bt", [P, 4, C])
        Kt = y_mem.sb("Kt", [P, 4, C])
        pinc = y_mem.sb("pinc", [P, 4, C])
        vr = y_mem.sb("vr", [P, 3, 512])
        bk = y_mem.sb("bk", [P, 2, 5, 512])
        w5 = Mem()
        zm = w5.sb("zm", [P, FB, C])
        lora = w5.sb("lora", [P, 2, 512])
        aT = w5.sb("aT", [P, 4, C])
        Lw = w5.sb("Lw", [P, 4, C])
        cum = w5.sb("cum", [P, 4, C])
        tmpa = w5.sb("tmpa", [P, 4, C])
        kkn = w5.sb("kkn", [P, 4, C])
        k7 = w5.sb("k7", [P, 4, C])
        ex = w5.sb("ex", [P, 4, C])
        At = w5.sb("At", [P, 4, C])
        Bh, Kh = aT, Lw
        sh_out = w5.sb("sh_out", [P, FB, 1 + NS])
        ps5 = Mem()
        psl = ps5.ps("psl", [P, 8, 512])
        lora_in, shout, zm_done, tanh_done, lo_full, lo_used, dv5, kk_sq, kk_full, kk_rt, cum_done, to_exp, exps, zeroed, \
            rk_ready, rk_full, tok_src, tok_full, tok_free, sh_done = (
                sem(n) for n in ("lora_in", "shout", "zm_done", "tanh_done", "lo_full", "lo_used", "dv5", "kk_sq",
                                 "kk_full", "kk_rt", "cum_done", "to_exp", "exps", "zeroed", "rk_ready", "rk_full", "tok_src",
                                 "tok_full", "tok_free", "sh_done"))
        order = [12, 13, 4, 5, 6, 7, 0, 1, 2, 3, 8, 9, 10, 11]
        samp = lambda a: a[:, :, 289:361].rearrange("p f (s l) -> p f s l", l=9)
        zs8 = lambda a: a[:, :, SAMP0:C].rearrange("p f (s l) -> p f s l", l=8)
        with nc.Block() as block:
            @block.sync
            def _(sp):
                sp.dma_start(lora[:], inp["lora"].rearrange("p (a f) -> p a f", a=2)).then_inc(lora_in, 16)
                sp.wait_ge(sh_done, 2)
                sp.dma_start(out["shift"], sh_out[:]).then_inc(shout, 16)
                sp.wait_ge(shout, 16)

            @block.gpsimd
            def _(pool):
                pool.memset(ARx[64:128, :, 0::2], 0.0).then_inc(zeroed, 1)
                pool.wait_ge(zeroed, 1)
                pool.memset(ARx[0:64, :, 1::2], 0.0).then_inc(zeroed, 1)
                pool.wait_ge(zeroed, 2)
                pool.memset(bk[:], 0.0).then_inc(zeroed, 1)
                pool.memset(vr[:], 0.0).then_inc(zeroed, 1)
                pool.tensor_copy(sh_out[:, :, 0:1], zbT[:, :, PROMPT:PROMPT + 1]).then_inc(sh_done, 1)
                pool.tensor_copy(sh_out[:, :, 1:1 + NS], samp(zbT)[:, :, :, 8]).then_inc(sh_done, 1)

            @block.tensor
            def _(pe):
                pe.wait_ge(lora_in, 16)
                pe.wait_ge(tanh_done, 1)
                pe.wait_ge(zm_done, 1)
                for i in range(4):
                    pe.matmul(psl[:, i, 0:C], lora[0:64, 0, P * i:P * i + P], zm[0:64, 12], start=True, stop=True)
                    pe.matmul(psl[:, 4 + i, 0:C], lora[64:128, 0, P * i:P * i + P], zm[64:128, 12],
                              start=True, stop=True).then_inc(lo_full, 1)
                pe.wait_ge(tanh_done, 2)
                for i in range(4):
                    pe.wait_ge(lo_used, i + 1)
                    pe.matmul(psl[:, i, 0:C], lora[:, 1, P * i:P * i + P], zm[:, 13], start=True,
                              stop=True).then_inc(lo_full, 1)
                pe.wait_ge(lo_used, 4)
                for i in range(4):
                    pe.wait_ge(kk_sq, 1)
                    pe.matmul(psl[:, 4 + i, 0:C], masks[:, M_B64], tmpa[:, i], start=True, stop=True).then_inc(kk_full, 1)
                pe.wait_ge(lo_used, 8)
                for i in range(4):
                    pe.wait_ge(rk_ready, 1)
                    pe.matmul(psl[:, i, 0:C], masks[:, M_B64], ex[:, i], start=True, stop=True).then_inc(rk_full, 1)
                for n in range(9):
                    what, i = divmod(n, 3)
                    if what == 0:
                        pe.wait_ge(zm_done, FB)
                    else:
                        pe.wait_ge(tok_src, what)
                    if n >= 2:
                        pe.wait_ge(tok_free, n - 1)
                    else:
                        pe.wait_ge(kk_rt, 4)
                    src = zm[:, 8:12] if what == 0 else (Bh, Kh)[what - 1]
                    for j in range(4):
                        ins = pe.transpose(psl[0:TW[i], 4 + n % 2, P * j:P * j + P], src[:, j, P * i:P * i + TW[i]], ident[:])
                    ins.then_inc(tok_full, 1)

            @block.scalar
            def _(act):
                act.wait_ge(zm_done, 1)
                act.activation(zm[0:64, 12], zm[0:64, 12], ACT.Tanh).then_inc(tanh_done, 1)
                act.wait_ge(zm_done, 2)
                act.activation(zm[:, 13], zm[:, 13], ACT.Sigmoid).then_inc(tanh_done, 1)
                for i in range(4):
                    act.wait_ge(lo_full, i + 1)
                    act.activation(Lw[:, i], psl[:, i, 0:C], ACT.Sigmoid, bias=col("w0", i))
                    act.activation(aT[:, i], psl[:, 4 + i, 0:C], ACT.Sigmoid, bias=col("a0", i)).then_inc(lo_used, 1)
                for i in range(4):
                    act.wait_ge(lo_full, 5 + i)
                    act.activation(gT[:, i], psl[:, i, 0:C], ACT.Copy).then_inc(lo_used, 1)
                for i in range(4):
                    act.wait_ge(kk_full, i + 1)
                    act.activation(ex[:, i], psl[:, 4 + i, 0:C], ACT.Sqrt).then_inc(kk_rt, 1)
                act.wait_ge(cum_done, 1)
                act.activation(pinc[:], cum[:], ACT.Exp).then_inc(exps, 1)
                act.activation(Bt[:], cum[:], ACT.Exp, scale=-1.0).then_inc(exps, 1)
                act.wait_ge(to_exp, 1)
                act.activation(At[:], At[:], ACT.Exp).then_inc(exps, 1)
                act.wait_ge(to_exp, 2)
                act.activation(Kt[:], Kt[:], ACT.Exp).then_inc(exps, 1)
                act.wait_ge(zeroed, 4)
                for n in range(9):
                    what, i = divmod(n, 3)
                    act.wait_ge(tok_full, n + 1)
                    src = psl[:, 4 + n % 2, :]
                    if what == 0:
                        ins = act.activation(vr[0:TW[i], i], src[0:TW[i]], ACT.Copy)
                    elif i == 2:
                        ins = act.activation(bk[0:96, what - 1, 4], src[0:96], ACT.Copy)
                    else:
                        act.activation(bk[0:64, what - 1, 2 * i], src[0:64], ACT.Copy)
                        ins = act.activation(bk[64:128, what - 1, 2 * i + 1], src[64:128], ACT.Copy)
                    ins.then_inc(tok_free, 1)

            @block.vector
            def _(dve):
                link = linker(dve, dv5)
                dve.tensor_tensor(zm[:, :, 0:SAMP0], zbT[:, :, 0:288], zbT[:, :, 1:289], ALU.subtract)
                for s in range(NS):
                    ins = dve.tensor_tensor(zm[:, :, SAMP0 + 8 * s:SAMP0 + 8 * s + 8], samp(zbT)[:, :, s, 0:8],
                                            samp(zbT)[:, :, s, 1:9], ALU.subtract)
                link(ins)
                for f in order:
                    dve.scalar_tensor_tensor(out=zm[:, f, 0:SAMP0], in0=zm[:, f, 0:SAMP0], scalar=col("mu", f),
                                             in1=zbT[:, f, 1:289], op0=ALU.mult, op1=ALU.add)
                    dve.scalar_tensor_tensor(out=zs8(zm)[:, f], in0=zs8(zm)[:, f], scalar=col("mu", f),
                                             in1=samp(zbT)[:, f, :, 1:9], op0=ALU.mult, op1=ALU.add).then_inc(zm_done, 1)
                dve.wait_ge(zm_done, FB)
                r, k, v = zm[:, 0:4], zm[:, 4:8], zm[:, 8:12]
                for i in range(4):
                    ins = dve.tensor_scalar(kkn[:, i], k[:, i], col("k_k", i), None, ALU.mult)
                link(ins)
                dve.tensor_tensor(tmpa[:], kkn[:], kkn[:], ALU.mult).then_inc(kk_sq, 1)
                dve.wait_ge(lo_used, 4)
                link(dve.tensor_scalar(Lw[:], Lw[:], -CEXP, None, ALU.mult))
                for i in range(4):
                    ins = dve.tensor_tensor_scan(cum[:, i], restart, Lw[:, i], 0.0, ALU.mult, ALU.add)
                ins.then_inc(cum_done, 1)
                dve.wait_ge(cum_done, 1)
                link(dve.tensor_tensor(At[:], cum[:], Lw[:], ALU.subtract))
                dve.sem_inc(to_exp, 1)
                pc = lambda a: a[:, :, 0:256].rearrange("p f (c j) -> p f c j", j=64)
                pe2 = lambda a: a[:, :, 256:288].rearrange("p f (c j) -> p f c j", j=16)
                dve.tensor_tensor(pc(Kt), pc(cum)[:, :, :, 63:64].to_broadcast([P, 4, 4, 64]), pc(cum), ALU.subtract)
                dve.tensor_tensor(pe2(Kt), pe2(cum)[:, :, :, 15:16].to_broadcast([P, 4, 2, 16]), pe2(cum), ALU.subtract)
                dve.tensor_tensor(zs8(Kt), zs8(cum)[:, :, :, 7:8].to_broadcast([P, 4, NS, 8]), zs8(cum),
                                  ALU.subtract).then_inc(to_exp, 1)
                for i in range(4):
                    ins = dve.tensor_scalar(k7[:, i], aT[:, i], -1.0, col("k_a", i), ALU.add, ALU.mult)
                link(ins)
                link(dve.scalar_tensor_tensor(out=k7[:], in0=k7[:], scalar=1.0, in1=k, op0=ALU.add, op1=ALU.mult))
                dve.wait_ge(kk_rt, 4)
                link(dve.tensor_scalar(tmpa[:], ex[:], 1e-12, None, ALU.max))
                link(dve.reciprocal(tmpa[:], tmpa[:]))
                link(dve.tensor_tensor(kkn[:], kkn[:], tmpa[:], ALU.mult))
                link(dve.tensor_tensor(tmpa[:], kkn[:], aT[:], ALU.mult))
                for i in range(4):
                    ins = dve.scalar_tensor_tensor(out=ex[:, i], in0=r[:, i], scalar=col("r_k", i), in1=k7[:, i],
                                                   op0=ALU.mult, op1=ALU.mult)
                ins.then_inc(rk_ready, 1)
                dve.wait_ge(exps, 4)
                dve.tensor_tensor(Bh[:], tmpa[:], Kt[:], ALU.mult).then_inc(tok_src, 1)
                dve.tensor_tensor(Kh[:], k7[:], Kt[:], ALU.mult).then_inc(tok_src, 1)
                dve.wait_ge(tok_src, 2)
                dve.wait_ge(zeroed, 2)
                for g in range(2):
                    half = slice(64 * g, 64 * g + 64)
                    dve.scalar_tensor_tensor(out=ARx[half, :, g], in0=At[half], scalar=-1.0, in1=kkn[half],
                                             op0=ALU.mult, op1=ALU.mult)
                    dve.tensor_tensor(ARx[half, :, 2 + g], zm[half, 0:4], pinc[half], ALU.mult)
                link(dve.tensor_tensor(Kt[:], k7[:], Bt[:], ALU.mult))
                dve.tensor_tensor(Bt[:], tmpa[:], Bt[:], ALU.mult)
                for i in range(4):
                    dve.wait_ge(rk_full, i + 1)
                    dve.tensor_tensor(bonusT[:, i], psl[:, i, 0:C], v[:, i], ALU.mult)
        ps5.free()
        w5.free()
        m6 = Mem()
        TT = m6.sb("TT", [P, 3, HB, P])
        Aak = m6.sb("Aak", [P, 3, HB, P])
        Arb = m6.sb("Arb", [P, 3, HB, P])
        Ark = m6.sb("Ark", [P, 3, HB, P])
        t6 = Mem()
        pwt = t6.sb("pwt", [P, HB, P])
        pw = t6.sb("pw", [P, HB, P])
        qwt = t6.sb("qwt", [P, HB, P])
        qw = t6.sb("qw", [P, HB, P])
        Et = t6.sb("Et", [P, HB, P])
        ps6 = Mem()
        pb6 = ps6.ps("pb6", [P, 8, 4, P])
        sc_full, sc_free, mm_full, by_act, by_dve, tt_first = (
            sem(n) for n in ("sc_full", "sc_free", "mm_full", "by_act", "by_dve", "tt_first"))
        def solve_steps(i):
            s = [("N2", pwt, pw, qwt, "a"), ("N2t", pw, pwt, qw, "a"), ("R1", qwt, "TT", "TT", "d"),
                 ("N4", qw, qwt, pw, "a"), ("N4t", qwt, qw, pwt, "a"), ("R2", pw, "TT", "TT", "d"),
                 ("N8", pwt, pw, qwt, "a"), ("R3", qwt, "TT", "TT", "d")]
            if i < 2:
                s += [("R", "TT", "ident", qw, "a"), ("F", Et, qw, pwt, "a"), ("Ft", qw, Et, pw, "a"),
                      ("Z1", pwt, "TT", "TT", "d"), ("F2", pw, pwt, qwt, "a"), ("Z2", qwt, "TT", "TT", "d")]
            return s
        reads = {"N2": [], "N2t": [], "R1": ["N2"], "N4": ["N2", "N2t"], "N4t": ["N2", "N2t"], "R2": ["N4", "R1"],
                 "N8": ["N4", "N4t"], "R3": ["N8", "R2"], "R": ["R3"], "F": ["R"], "Ft": ["R"], "Z1": ["F", "R3"],
                 "F2": ["F", "Ft"], "Z2": ["F2", "Z1"]}
        ops = [(i, q) + step for i in range(3) for step in solve_steps(i) for q in range(2)]
        taken = {}
        n_by = {"a": 0, "d": 0}
        for i, q, name, _, _, _, who in ops:
            n_by[who] += 1
            taken[i, q, name] = (by_act if who == "a" else by_dve, n_by[who])
        order6 = [(i, q, name) for i, q, name, *_ in ops]
        NSC = 10
        with nc.Block() as block:
            @block.tensor
            def _(pe):
                for i in range(3):
                    w, cs = TW[i], slice(P * i, P * i + TW[i])
                    first = order6.index((i, 0, "N2"))
                    for n in range(NSC):
                        if i and n < 8:
                            for q in range(2):
                                pe.wait_ge(*taken[i - 1, q, "Z2"])
                                pe.wait_ge(*taken[i - 1, q, "F2"])
                        if n >= 8:
                            pe.wait_ge(sc_free, NSC * i + n - 7)
                        bank = pb6[:, n % 8]
                        if n < 8:
                            j, kind = divmod(n, 2)
                            lhs = (Bt, Kt)[kind]
                            ins = pe.matmul(bank[0:w, :, 0:w], lhs[:, j, cs], ARx[:, j, :, cs], start=True, stop=True)
                        else:
                            for m in range(4):
                                h = 4 * (n - 8) + m
                                ins = pe.matmul(bank[0:w, m, 0:w], ARx[:, h // 2, h % 2, cs], Bt[:, h // 2, cs],
                                                start=True, stop=True)
                        ins.then_inc(sc_full, 1)
                    for n, (_, q, name, lhs, rhs, dst, who) in enumerate(o for o in ops if o[0] == i):
                        if n < 8:
                            pe.wait_ge(sc_free, NSC * (i + 1))
                        else:
                            pe.wait_ge(*taken[order6[first + n - 8]])
                        for r in reads[name]:
                            pe.wait_ge(*taken[i, q, r])
                        if name == "R1":
                            pe.wait_ge(tt_first, i + 1)
                        for m in range(4):
                            h = 4 * q + m
                            pick = lambda a: TT[0:w, i, h, 0:w] if a == "TT" else ident[0:w, 0:w] if a == "ident" \
                                else a[0:w, h, 0:w]
                            if name == "R":
                                ins = pe.transpose(pb6[0:w, n % 8, m, 0:w], pick(lhs), pick(rhs))
                            else:
                                ins = pe.matmul(pb6[0:w, n % 8, m, 0:w], pick(lhs), pick(rhs), start=True, stop=True)
                        ins.then_inc(mm_full, 1)

            @block.vector
            def _(dve):
                dn = 0
                for i in range(3):
                    w = TW[i]
                    first = order6.index((i, 0, "N2"))
                    msk = lambda m, k: masks[0:w, m:m + 1, 0:w].to_broadcast([w, k, w])
                    if i:
                        dve.wait_ge(mm_full, first)
                    bu, bl, su, iu = (M_BU, M_BL, M_SU, M_IU) if i < 2 else (M_TBU, M_TBL, M_TBU, M_TIU)
                    for n in range(NSC):
                        dve.wait_ge(sc_full, NSC * i + n + 1)
                        bank = pb6[0:w, n % 8, :, 0:w]
                        j, kind = divmod(n, 2)
                        hs = slice(2 * j, 2 * j + 2)
                        if n >= 8:
                            ins = dve.tensor_tensor(pw[0:w, 4 * n - 32:4 * n - 28, 0:w], bank, msk(bl, 4), ALU.mult)
                        elif kind == 0:
                            dve.tensor_tensor(pwt[0:w, hs, 0:w], bank[:, 0:2], msk(bu, 2), ALU.mult)
                            if i < 2:
                                dve.tensor_tensor(Et[0:w, hs, 0:w], bank[:, 0:2], msk(M_EU, 2), ALU.mult)
                            ins = dve.tensor_tensor(Arb[0:w, i, hs, 0:w], bank[:, 2:4], msk(iu, 2), ALU.mult)
                        else:
                            dve.tensor_tensor(Aak[0:w, i, hs, 0:w], bank[:, 0:2], msk(su, 2), ALU.mult)
                            ins = dve.tensor_tensor(Ark[0:w, i, hs, 0:w], bank[:, 2:4], msk(iu, 2), ALU.mult)
                        ins.then_inc(sc_free, 1)
                    dve.wait_ge(sc_free, NSC * (i + 1))
                    dve.tensor_tensor(TT[0:w, i, :, 0:w], pwt[0:w, :, 0:w], msk(M_ID, HB), ALU.add).then_inc(tt_first, 1)
                    dve.wait_ge(tt_first, i + 1)
                    for n, (_, q, name, lhs, rhs, dst, who) in enumerate(o for o in ops if o[0] == i):
                        if who == "d":
                            dve.wait_ge(mm_full, first + n + 1)
                            if dn >= 2:
                                dve.wait_ge(by_dve, dn - 1)
                            acc = TT[0:w, i, 4 * q:4 * q + 4, 0:w]
                            dve.tensor_tensor(acc, acc, pb6[0:w, n % 8, :, 0:w], ALU.add).then_inc(by_dve, 1)
                            dn += 1

            @block.scalar
            def _(act):
                for i in range(3):
                    w = TW[i]
                    first = order6.index((i, 0, "N2"))
                    for n, (_, q, name, lhs, rhs, dst, who) in enumerate(o for o in ops if o[0] == i):
                        if who == "a":
                            act.wait_ge(mm_full, first + n + 1)
                            if name == "N4t":
                                act.wait_ge(tt_first, i + 1)
                            act.activation(dst[0:w, 4 * q:4 * q + 4, 0:w], pb6[0:w, n % 8, :, 0:w], ACT.Copy) \
                                .then_inc(by_act, 1)
        ps6.free()
        t6.free()

        m7 = Mem()
        st = m7.sb("st", [P, 2, 4, HN])
        std = m7.sb("std", [P, 4, HN])
        xb = m7.sb("xb", [P, 512])
        ub = m7.sb("ub", [P, 512])
        ss = m7.sb("ss", [P, 4, NS, HN])
        xm = m7.sb("xm", [P, NS, HN])
        xs = m7.sb("xs", [P, HB, HN])
        uv = zbT[:].rearrange("p f c -> p (f c)")[:, 0:36 * HN].rearrange("p (a b s v) -> p a b s v", a=2, b=2, s=9)
        yT = mixT[:, 4:8]
        ps7 = Mem()
        psX = ps7.ps("psX", [P, 512])
        psU = ps7.ps("psU", [P, 512])
        psSt = ps7.ps("psSt", [P, 512])
        psY = ps7.ps("psY", [P, 512])
        ps2 = ps7.ps("ps2", [P, 4, 512])
        (rs_in, z7, x_full, x_ready, u_full, u_ready, st_full, st_done, std_done, y_full, y_taken, x0_full, x0_free,
         xs_ready, spread, spread_used, ns_full, ns_free, rst_out, spread_u, ns_mul) = (sem(n) for n in (
             "rs_in", "z7", "x_full", "x_ready", "u_full", "u_ready", "st_full", "st_done", "std_done", "y_full",
             "y_taken", "x0_full", "x0_free", "xs_ready", "spread", "spread_used", "ns_full", "ns_free", "rst_out",
             "spread_u", "ns_mul"))
        hv = lambda h: slice(HN * h, HN * h + HN)
        with nc.Block() as block:
            @block.sync
            def _(sp):
                sp.dma_start(ss[:], inp["state_r"]).then_inc(rs_in, 16)
                sp.wait_ge(st_done, 5)
                sp.dma_start(out["rwkv_p"], st[:, 0]).then_inc(rst_out, 16)
                sp.wait_ge(ns_free, 4)
                sp.dma_start(out["rwkv_s"], ss[:]).then_inc(rst_out, 16)
                sp.wait_ge(rst_out, 32)

            @block.gpsimd
            def _(pool):
                pool.memset(xb[:], 0.0).then_inc(z7, 1)
                pool.memset(ub[:], 0.0).then_inc(z7, 1)
                for h in range(HB):
                    if h >= 2:
                        pool.wait_ge(spread_used, h - 1)
                    pool.tensor_tensor(uv[0:96, h % 2, 1], vr[0:96, 2, hv(h)].unsqueeze(1).to_broadcast([96, 9, HN]),
                                       seq9[0:96].unsqueeze(2).to_broadcast([96, 9, HN]), ALU.mult).then_inc(spread, 1)

            @block.tensor
            def _(pe):
                pe.wait_ge(z7, 2)
                for c in range(4):
                    i, pb, col0 = c // 2, 64 * (c % 2), 64 * c
                    rows, ts = slice(pb, pb + 64), slice(64 * c, 64 * c + 64)
                    tl = slice(pb, pb + 64)
                    if c:
                        pe.wait_ge(st_done, c)
                        pe.wait_ge(x_ready, c)
                    for h in range(HB):
                        j, g = divmod(h, 2)
                        ins = pe.matmul(psX[rows, hv(h)], Aak[:, i, h, tl], vr[:, i, hv(h)], start=True, stop=c == 0,
                                        skip_group_check=True)
                        if c:
                            ins = pe.matmul(psX[rows, hv(h)], ARx[:, j, g, ts], st[:, (c - 1) % 2, j], start=False, stop=True,
                                      skip_group_check=True)
                    ins.then_inc(x_full, 1)
                    pe.wait_ge(x_ready, c + 1)
                    if c:
                        pe.wait_ge(u_ready, c)
                    for h in range(HB):
                        ins = pe.matmul(psU[rows, hv(h)], TT[:, i, h, tl], xb[:, hv(h)], start=True, stop=True)
                    ins.then_inc(u_full, 1)
                    pe.wait_ge(u_ready, c + 1)
                    for h in range(HB):
                        j, g = divmod(h, 2)
                        o = psSt[64 * g:64 * g + 64, hv(j)]
                        pe.matmul(o, bk[:, 0, c, hv(h)], ub[:, hv(h)], start=True, stop=False)
                        ins = pe.matmul(o, bk[:, 1, c, hv(h)], vr[:, i, hv(h)], start=False, stop=True)
                    ins.then_inc(st_full, 1)
                    if c:
                        pe.wait_ge(y_taken, c)
                    for h in range(HB):
                        j, g = divmod(h, 2)
                        o = psY[64 * g:64 * g + 64, hv(j)]
                        pe.matmul(o, ub[:, hv(h)], Arb[:, i, h, tl], start=True, stop=False)
                        ins = pe.matmul(o, vr[:, i, hv(h)], Ark[:, i, h, tl], start=False, stop=c == 0)
                        if c:
                            ins = pe.matmul(o, st[:, (c - 1) % 2, j], ARx[:, j, 2 + g, ts], start=False, stop=True)
                    ins.then_inc(y_full, 1)
                t2c = slice(256, C)
                pe.wait_ge(rs_in, 16)
                for h in range(HB):
                    j, g = divmod(h, 2)
                    if h >= 4:
                        pe.wait_ge(x0_free, h - 3)
                    pe.matmul(ps2[0:96, h % 4, :], ARx[:, j, g, t2c], ss[:, j].rearrange("p s v -> p (s v)"),
                              start=True, stop=True).then_inc(x0_full, 1)
                pe.wait_ge(st_done, 4)
                pe.wait_ge(u_ready, 4)
                for h in range(HB):
                    j, g = divmod(h, 2)
                    pe.matmul(psX[0:96, hv(h)], ARx[:, j, g, t2c], st[:, 1, j], start=True, stop=True)
                    ins = pe.matmul(psU[0:96, hv(h)], Aak[0:96, 2, h, 0:96], vr[0:96, 2, hv(h)], start=True, stop=True)
                ins.then_inc(x_full, 1)
                pe.wait_ge(x_ready, 5)
                for h in range(HB):
                    ins = pe.matmul(psU[0:96, hv(h)], TT[0:96, 2, h, 0:96], xb[0:96, hv(h)], start=True, stop=True)
                ins.then_inc(u_full, 1)
                pe.wait_ge(u_ready, 5)
                pe.wait_ge(y_taken, 4)
                yb = psY[:, 0:384].rearrange("p (j t) -> p j t", j=4)
                for h in range(HB):
                    j, g = divmod(h, 2)
                    o = yb[64 * g:64 * g + 64, j]
                    pe.matmul(o, ub[0:96, hv(h)], Arb[0:96, 2, h, 0:96], start=j == 0, stop=False, skip_group_check=True)
                    pe.matmul(o, vr[0:96, 2, hv(h)], Ark[0:96, 2, h, 0:96], start=False, stop=False, skip_group_check=True)
                    pe.matmul(o[:, 0:16], st[:, 1, j], ARx[:, j, 2 + g, 256:272], start=False, stop=False,
                              skip_group_check=True)
                    for s in range(NS):
                        t = 32 + 8 * s
                        ins = pe.matmul(o[:, t:t + 8], ss[:, j, s], ARx[:, j, 2 + g, 256 + t:264 + t], start=False,
                                        stop=s == NS - 1, skip_group_check=True)
                ins.then_inc(y_full, 1)
                pe.wait_ge(x0_free, 8)
                for h in range(HB):
                    j, g = divmod(h, 2)
                    pe.wait_ge(spread, h + 1)
                    pe.wait_ge(spread_u, h + 1)
                    lhs = [bk[0:96, k, 4, hv(h)] for k in range(2)]
                    half = slice(64 * g, 64 * g + 64)
                    for k in range(2):
                        pe.matmul(ps2[half, j, :], lhs[k], uv[0:96, h % 2, k, 0:8].rearrange("p s v -> p (s v)"),
                                  start=k == 0, stop=k == 1)
                    for k in range(2):
                        ins = pe.matmul(psSt[half, hv(j)], lhs[k], uv[0:96, h % 2, k, 8], start=k == 0, stop=k == 1)
                    ins.then_inc(spread_used, 1)

            @block.vector
            def _(dve):
                pend = lambda c: pinc[:, :, c:c + 1].to_broadcast([P, 4, HN])
                for c in range(4):
                    pb = 64 * (c % 2)
                    dve.wait_ge(x_full, c + 1)
                    if c == 0:
                        dve.wait_ge(z7, 2)
                    dve.tensor_copy(xb[pb:pb + 64], psX[pb:pb + 64]).then_inc(x_ready, 1)
                    if c:
                        dve.tensor_tensor(std[:], st[:, (c - 1) % 2], pend(64 * c + 63), ALU.mult).then_inc(std_done, 1)
                        dve.wait_ge(std_done, c)
                    dve.wait_ge(st_full, c + 1)
                    src = psSt[:, 0:256].rearrange("p (j v) -> p j v", j=4)
                    if c:
                        dve.tensor_tensor(st[:, c % 2], src, std[:], ALU.add).then_inc(st_done, 1)
                    else:
                        dve.tensor_copy(st[:, 0], src).then_inc(st_done, 1)
                dve.wait_ge(st_done, 4)
                for h in range(HB):
                    dve.wait_ge(x0_full, h + 1)
                    if h:
                        dve.wait_ge(xs_ready, h)
                    dve.tensor_tensor(xm[0:96], ps2[0:96, h % 4, :].rearrange("p (s v) -> p s v", s=NS),
                                      seq9[0:96, 0:8].unsqueeze(2).to_broadcast([96, NS, HN]), ALU.mult).then_inc(x0_free, 1)
                    dve.wait_ge(x0_free, h + 1)
                    dve.tensor_reduce(xs[0:96, h], xm[0:96].rearrange("p s v -> p v s"), AX, ALU.add).then_inc(xs_ready, 1)
                dve.wait_ge(xs_ready, 8)
                dve.wait_ge(x_full, 5)
                xsf = xs[0:96].rearrange("p h v -> p (h v)")
                dve.scalar_tensor_tensor(out=xsf, in0=psX[0:96], scalar=seq9[0:96, 8:9], in1=xsf, op0=ALU.mult,
                                         op1=ALU.add).then_inc(xs_ready, 1)
                dve.wait_ge(xs_ready, 9)
                dve.tensor_tensor(xb[0:96], psU[0:96], xsf, ALU.add).then_inc(x_ready, 1)
                dve.wait_ge(u_ready, 5)
                for h in range(HB):
                    if h >= 2:
                        dve.wait_ge(spread_used, h - 1)
                    dve.tensor_tensor(uv[0:96, h % 2, 0], ub[0:96, hv(h)].unsqueeze(1).to_broadcast([96, 9, HN]),
                                      seq9[0:96].unsqueeze(2).to_broadcast([96, 9, HN]), ALU.mult).then_inc(spread_u, 1)
                dve.wait_ge(y_full, 5)
                for j in range(4):
                    last = pinc[:, j, SAMP0:C].rearrange("p (s l) -> p s l", l=8)[:, :, 7:8]
                    dve.tensor_tensor(ss[:, j], ss[:, j], last.to_broadcast([P, NS, HN]), ALU.mult).then_inc(ns_mul, 1)
                dve.tensor_tensor(std[:], st[:, 1], pend(PROMPT - 1), ALU.mult).then_inc(ns_mul, 1)
                dve.wait_ge(ns_mul, 5)
                for j in range(4):
                    dve.wait_ge(spread_used, 2 * j + 2)
                    dve.tensor_tensor(ss[:, j], ss[:, j], ps2[:, j, :].rearrange("p (s v) -> p s v", s=NS),
                                      ALU.add).then_inc(ns_free, 1)
                dve.tensor_tensor(st[:, 0], psSt[:, 0:256].rearrange("p (j v) -> p j v", j=4), std[:],
                                  ALU.add).then_inc(st_done, 1)

            @block.scalar
            def _(act):
                for c in range(4):
                    pb = 64 * (c % 2)
                    act.wait_ge(u_full, c + 1)
                    act.activation(ub[pb:pb + 64], psU[pb:pb + 64], ACT.Copy).then_inc(u_ready, 1)
                    act.wait_ge(y_full, c + 1)
                    act.activation(yT[:, :, 64 * c:64 * c + 64], psY[:, 0:256].rearrange("p (j t) -> p j t", j=4),
                                   ACT.Copy).then_inc(y_taken, 1)
                act.wait_ge(u_full, 5)
                act.activation(ub[0:96], psU[0:96], ACT.Copy).then_inc(u_ready, 1)
                act.wait_ge(y_full, 5)
                act.activation(yT[:, :, 256:C], psY[:, 0:384].rearrange("p (j t) -> p j t", j=4), ACT.Copy).then_inc(y_taken, 1)
        ps7.free()

        yc, ysq, sd = Bt, Kt, pinc
        ps8 = Mem()
        pmu = ps8.ps("pmu", [P, 4, 512])
        pvar = ps8.ps("pvar", [P, 4, 512])
        mu_full, c_ready, ysq_ready, var_full, sd_ready, dv8 = (
            sem(n) for n in ("mu_full", "c_ready", "ysq_ready", "var_full", "sd_ready", "dv8"))
        with nc.Block() as block:
            @block.tensor
            def _(pe):
                for j in range(4):
                    pe.matmul(pmu[:, j, 0:C], masks[:, M_B64], yT[:, j], start=True, stop=True).then_inc(mu_full, 1)
                for j in range(4):
                    pe.wait_ge(ysq_ready, j + 1)
                    pe.matmul(pvar[:, j, 0:C], masks[:, M_B64], ysq[:, j], start=True, stop=True).then_inc(var_full, 1)

            @block.scalar
            def _(act):
                for j in range(4):
                    act.wait_ge(c_ready, j + 1)
                    act.activation(ysq[:, j], yc[:, j], ACT.Square).then_inc(ysq_ready, 1)
                for j in range(4):
                    act.wait_ge(var_full, j + 1)
                    act.activation(sd[:, j], pvar[:, j, 0:C], ACT.Sqrt, bias=epsc[:, 1:2], scale=1.0 / HN).then_inc(sd_ready, 1)

            @block.vector
            def _(dve):
                link = linker(dve, dv8)
                for j in range(4):
                    dve.wait_ge(mu_full, j + 1)
                    dve.scalar_tensor_tensor(out=yc[:, j], in0=pmu[:, j, 0:C], scalar=-1.0 / HN, in1=yT[:, j],
                                             op0=ALU.mult, op1=ALU.add).then_inc(c_ready, 1)
                dve.wait_ge(c_ready, 4)
                for j in range(4):
                    dve.wait_ge(sd_ready, j + 1)
                    link(dve.reciprocal(sd[:, j], sd[:, j]))
                    link(dve.tensor_tensor(yc[:, j], yc[:, j], sd[:, j], ALU.mult))
                    link(dve.tensor_scalar(yc[:, j], yc[:, j], col("ln_w", j), col("ln_b", j), ALU.mult, ALU.add))
                    link(dve.tensor_tensor(yc[:, j], yc[:, j], bonusT[:, j], ALU.add))
                    link(dve.tensor_tensor(mixT[:, 4 + j], yc[:, j], gT[:, j], ALU.mult))
        ps8.free()
        m7.free()
        m6.free()
        y_mem.free()
        zb_mem.free()
        rt_mem = Mem()
        RT = rt_mem.sb("RT", [P, 3, NT])
        m9 = Mem()
        x2T = m9.sb("x2T", [P, KD, NT])
        wo = m9.sb("wo", [P, 8, D])
        x1 = m9.sb("x1", [P, 3, D])
        sq9 = m9.sb("sq9", [P, D])
        rs9 = m9.sb("rs9", [P, 16])
        ps9 = Mem()
        pmix = ps9.ps("pmix", [P, 6, 512])
        ptr = ps9.ps("ptr", [P, 2, 4, P])
        x1_in, wo_in, mix_full, x1_ready, sq9d, rt9, rc9, rn9, tr9_full, tr9_free, x1_saved = (
            sem(n) for n in ("x1_in", "wo_in", "mix_full", "x1_ready", "sq9d", "rt9", "rc9", "rn9", "tr9_full", "tr9_free",
                             "x1_saved"))
        KEEP = [[(META, P, 0)], [(0, P, P - META)], [(0, 16, 240), (32, 96, 256)]]
        with nc.Block() as block:
            @block.sync
            def _(sp):
                sp.dma_start(wo[:], inp["w_out"]).then_inc(wo_in, 16)
                sp.dma_start(x1[:], inp["x_rows"].rearrange("k p d -> p k d")).then_inc(x1_in, 16)
                for i in range(3):
                    sp.wait_ge(x1_ready, i + 1)
                    for a, b, c0 in KEEP[i]:
                        sp.dma_start(x1_dram[c0:c0 + b - a], x1[a:b, i]).then_inc(x1_saved, 16)
                sp.wait_ge(x1_saved, 64)

            @block.tensor
            def _(pe):
                pe.wait_ge(wo_in, 16)
                for i in range(3):
                    for g in range(2):
                        for f in range(8):
                            ins = pe.matmul(pmix[0:TW[i], 2 * i + g], mixT[:, f, P * i:P * i + TW[i]],
                                            wo[:, f, 512 * g:512 * g + 512], start=f == 0, stop=f == 7)
                    ins.then_inc(mix_full, 1)
                for n in range(3 * KD):
                    i, j = divmod(n, KD)
                    if j == 0:
                        pe.wait_ge(rn9, i + 1)
                    if n % 4 == 0 and n >= 8:
                        pe.wait_ge(tr9_free, n // 4 - 1)
                    w = TW[i]
                    ins = pe.transpose(ptr[:, n // 4 % 2, n % 4, 0:w], x1[0:w, i, P * j:P * j + P], ident[0:w, 0:w])
                    if n % 4 == 3:
                        ins.then_inc(tr9_full, 1)

            @block.scalar
            def _(act):
                for i in range(3):
                    act.wait_ge(x1_ready, i + 1)
                    if i:
                        act.wait_ge(sq9d, i)
                    w = TW[i]
                    act.activation(sq9[0:w], x1[0:w, i], ACT.Square, accum_out=rs9[0:w, i:i + 1]).then_inc(sq9d, 1)
                    act.wait_ge(sq9d, i + 1)
                    act.activation(rs9[0:w, 3 + i:4 + i], rs9[0:w, i:i + 1], ACT.Sqrt, bias=epsc[0:w, 0:1],
                                   scale=1.0 / D).then_inc(rt9, 1)

            @block.vector
            def _(dve):
                dve.wait_ge(x1_in, 16)
                for i in range(3):
                    dve.wait_ge(mix_full, i + 1)
                    w = TW[i]
                    dve.tensor_tensor(x1[0:w, i], x1[0:w, i], pmix[0:w, 2 * i:2 * i + 2].rearrange("p a b -> p (a b)"),
                                      ALU.add).then_inc(x1_ready, 1)
                dve.wait_ge(x1_saved, 64)
                for i in range(3):
                    w = TW[i]
                    dve.wait_ge(rt9, i + 1)
                    dve.reciprocal(rs9[0:w, 6 + i:7 + i], rs9[0:w, 3 + i:4 + i]).then_inc(rc9, 1)
                dve.wait_ge(rc9, 3)
                for i in range(3):
                    w = TW[i]
                    dve.tensor_scalar(x1[0:w, i], x1[0:w, i], rs9[0:w, 6 + i:7 + i], None, ALU.mult).then_inc(rn9, 1)
                for n in range(3 * KD):
                    i, j = divmod(n, KD)
                    if n % 4 == 0:
                        dve.wait_ge(tr9_full, n // 4 + 1)
                    for a, b, c0 in KEEP[i]:
                        ins = dve.tensor_scalar(x2T[:, j, c0:c0 + b - a], ptr[:, n // 4 % 2, n % 4, a:b],
                                                col("norm2", j), None, ALU.mult)
                    if n % 4 == 3:
                        ins.then_inc(tr9_free, 1)
        ps9.free()

        m10 = Mem()
        sc = m10.sb("sc", [P, 3, 16, NK])
        wqs = m10.sb("wqs", [P, 3, KD, P])
        qpT = m10.sb("qpT", [P, 2, NT])
        keysT = m10.sb("keysT", [P, 2, NK])
        top = m10.sb("top", [P, 16, TOPK])
        topi = m10.sb("topi", [P, 16, TOPK], U32)
        topf = m10.sb("topf", [P, 16, TOPK])
        cand = m10.sb("cand", [P, PH, TOPK, TOPK])
        best = m10.sb("best", [P, PH, TOPK])
        flat = m10.sb("flat", [P, PH, TOPK], U32)
        rank = m10.sb("rank", [P, 2, PH, TOPK], U32)
        rankf = m10.sb("rankf", [P, 2, PH, TOPK])
        pick = m10.sb("pick", [P, PH, TOPK, TOPK])
        picked = m10.sb("picked", [P, 3, 3, P])
        gsum = m10.sb("gsum", [P, 2, PH])
        ps10 = Mem()
        pq = ps10.ps("pq", [P, 2, 512])
        pss = ps10.ps("pss", [P, 2, 4, P])
        ptp = ps10.ps("ptp", [P, 3, 512])
        wq_in = [sem(f"wq_in{i}") for i in range(3)]
        keys_in, q_full, q_ready, s_full, s_ready, dv10, e10, pk_ready, pt_full, rt_ready, split_ready, rt_saved = (
            sem(n) for n in ("keys_in", "q_full", "q_ready", "s_full", "s_ready", "dv10", "e10", "pk_ready", "pt_full",
                             "rt_ready", "split_ready", "rt_saved"))
        NEG = -3.0e38
        with nc.Block() as block:
            @block.sync
            def _(sp):
                sp.dma_start(keysT[:], inp["keysT"]).then_inc(keys_in, 16)
                for n in range(16):
                    if n >= 3:
                        sp.wait_ge(q_full, n - 2)
                    sp.dma_start(wqs[:, n % 3], inp["w_q"][n]).then_inc(wq_in[n % 3], 16)
                sp.wait_ge(rt_ready, 3)
                sp.dma_start(rt_dram, RT[:]).then_inc(rt_saved, 16)
                sp.wait_ge(rt_saved, 16)

            @block.tensor
            def _(pe):
                for n in range(17):
                    if n < 16:
                        pe.wait_ge(wq_in[n % 3], 16 * (n // 3 + 1))
                        if n >= 2:
                            pe.wait_ge(q_ready, n - 1)
                        for k in range(KD):
                            ins = pe.matmul(pq[:, n % 2, 0:NT], wqs[:, n % 3, k], x2T[:, k], start=k == 0, stop=k == KD - 1)
                        ins.then_inc(q_full, 1)
                    if n:
                        m = n - 1
                        if m == 0:
                            pe.wait_ge(keys_in, 16)
                        pe.wait_ge(q_ready, m + 1)
                        if m >= 2:
                            pe.wait_ge(s_ready, m - 1)
                        for i, (c0, w) in enumerate(PT):
                            ins = pe.matmul(pss[0:w, m % 2, i], qpT[:, m % 2, c0:c0 + w], keysT[:, m % 2], start=True,
                                            stop=True)
                        ins.then_inc(s_full, 1)
                for i, (c0, w) in enumerate(PT):
                    pe.wait_ge(pk_ready, i + 1)
                    for k in range(3):
                        ins = pe.transpose(ptp[:, k, c0:c0 + w], picked[0:w, i, k], ident[0:w, 0:w])
                    ins.then_inc(pt_full, 1)

            @block.scalar
            def _(act):
                for n in range(17):
                    if n < 16:
                        act.wait_ge(q_full, n + 1)
                        if n >= 2:
                            act.wait_ge(s_full, n - 1)
                        act.activation(qpT[:, n % 2], pq[:, n % 2, 0:NT], ACT.Copy).then_inc(q_ready, 1)
                    if n:
                        m = n - 1
                        act.wait_ge(s_full, m + 1)
                        act.activation(sc[:, 0:2, m], pss[:, m % 2, 0:2], ACT.Copy)
                        act.activation(sc[0:64, 2, m], pss[0:64, m % 2, 2], ACT.Copy).then_inc(s_ready, 1)
                act.activation(xh[:], x2T[:], ACT.Copy).then_inc(split_ready, 1)
                for i, (c0, w) in enumerate(PT):
                    act.wait_ge(e10, 2 * i + 1)
                    act.activation(best[0:w], best[0:w], ACT.Exp).then_inc(e10, 1)

            @block.vector
            def _(dve):
                link = linker(dve, dv10)
                dve.wait_ge(s_ready, 16)
                dve.wait_ge(split_ready, 1)
                dve.tensor_tensor(xl[:], x2T[:], xh[:], ALU.subtract)

                def top16(values, index, source, groups):
                    for half in range(2):
                        e = slice(8 * half, 8 * half + 8)
                        for g in range(groups):
                            ins = dve.max(values(g)[:, e], source(g))
                        link(ins)
                        for g in range(groups):
                            ins = dve.max_index(index(g)[:, e], values(g)[:, e], source(g))
                        link(ins)
                        if half == 0:
                            for g in range(groups):
                                ins = dve.match_replace(out=source(g), in_to_replace=values(g)[:, e], in_values=source(g),
                                                        imm_value=NEG)
                            link(ins)

                for i, (c0, w) in enumerate(PT):
                    top16(lambda g: top[0:w, g], lambda g: topi[0:w, g], lambda g: sc[0:w, i, g], 16)
                    dve.tensor_copy(topf[0:w], topi[0:w])
                    pairs = top[0:w].rearrange("p (h a) k -> p h a k", a=2)
                    link(dve.tensor_tensor(cand[0:w], pairs[:, :, 0, :].unsqueeze(3).to_broadcast([w, PH, TOPK, TOPK]),
                                           pairs[:, :, 1, :].unsqueeze(2).to_broadcast([w, PH, TOPK, TOPK]), ALU.add))
                    top16(lambda g: best[0:w, g], lambda g: flat[0:w, g],
                          lambda g: cand[0:w, g].rearrange("p a b -> p (a b)"), PH)
                    link(dve.tensor_copy(gsum[0:w, 0], best[0:w, :, 0]))
                    dve.tensor_tensor(best[0:w], best[0:w], gsum[0:w, 0].unsqueeze(2).to_broadcast([w, PH, TOPK]),
                                      ALU.subtract).then_inc(e10, 1)
                    dve.tensor_single_scalar(rank[0:w, 0], flat[0:w], 4, ALU.logical_shift_right)
                    link(dve.tensor_single_scalar(rank[0:w, 1], flat[0:w], TOPK - 1, ALU.bitwise_and))
                    link(dve.tensor_copy(rankf[0:w], rank[0:w]))
                    for a in range(2):
                        keys = topf[0:w].rearrange("p (h a) k -> p h a k", a=2)[:, :, a, :].unsqueeze(2)
                        link(dve.tensor_tensor(pick[0:w], rankf[0:w, a].unsqueeze(3).to_broadcast([w, PH, TOPK, TOPK]),
                                               iota[0:w, 0:TOPK].unsqueeze(1).unsqueeze(1).to_broadcast([w, PH, TOPK, TOPK]),
                                               ALU.is_equal))
                        link(dve.tensor_tensor(pick[0:w], pick[0:w], keys.to_broadcast([w, PH, TOPK, TOPK]), ALU.mult))
                        link(dve.tensor_reduce(picked[0:w, i, a].rearrange("p (h k) -> p h k", h=PH), pick[0:w], AX, ALU.add))
                    dve.wait_ge(e10, 2 * i + 2)
                    link(dve.tensor_reduce(gsum[0:w, 0], best[0:w], AX, ALU.add))
                    link(dve.reciprocal(gsum[0:w, 1], gsum[0:w, 0]))
                    dve.tensor_tensor(picked[0:w, i, 2].rearrange("p (h k) -> p h k", h=PH), best[0:w],
                                      gsum[0:w, 1].unsqueeze(2).to_broadcast([w, PH, TOPK]), ALU.mult).then_inc(pk_ready, 1)
                    dve.wait_ge(pk_ready, i + 1)
                dve.wait_ge(pt_full, 3)
                for k in range(3):
                    dve.tensor_copy(RT[:, k], ptp[:, k, 0:NT]).then_inc(rt_ready, 1)
        ps10.free()
        m10.free()
        m9.free()
        rt_mem.free()
        mix_mem.free()
        mask_mem.free()

        big_mem = Mem()
        hid = big_mem.sb("hid", [P, NBLK, NT])
        ring = Mem()
        raw = [ring.sb(f"raw{u}", [P, 512]) for u in range(4)]
        hi = [ring.sb(f"hi{u}", [P, 4, P], F32R) for u in range(4)]
        lo = [ring.sb(f"lo{u}", [P, 4, P], F32R) for u in range(4)]
        wide = lambda a: a[:].rearrange("p k n -> p (k n)")
        ps11 = Mem()
        ph = ps11.ps("ph", [P, 2, 512])
        u_in = [sem(f"u_in{u}") for u in range(4)]
        u_hi, u_lo, u_mm, h_done = (sem(n) for n in ("u_hi", "u_lo", "u_mm", "h_done"))
        STEPS = NBLK // 2
        with nc.Block() as block:
            @block.sync
            def _(sp):
                def step(i, first):
                    for u in range(4):
                        if not first:
                            sp.wait_ge(u_lo, 4 * i + (u - 3))
                        src = inp["uT"][bass.ds(2 * i + u // 2, 1), :, 4 * (u % 2):4 * (u % 2) + 4, :]
                        sp.dma_start(raw[u][:], src.rearrange("b p k n -> p (b k n)")).then_inc(u_in[u], 16)
                step(0, True)
                with sp.Fori(1, STEPS) as i:
                    step(i, False)

            @block.scalar
            def _(act):
                def gelu(b, bank, count):
                    act.wait_ge(u_mm, count)
                    act.activation(hid[:, bass.ds(b, 1), :].rearrange("p b t -> p (b t)"), ph[:, bank, 0:NT],
                                   ACT.Gelu).then_inc(h_done, 1)

                def step(i, first):
                    for u in range(4):
                        act.wait_ge(u_in[u], 16 * i + 16)
                        if not first:
                            act.wait_ge(u_mm, 4 * i + (u - 3))
                        act.activation(wide(hi[u]), raw[u][:], ACT.Copy).then_inc(u_hi, 1)
                        if u == 1 and not first:
                            gelu(2 * i - 1, 1, 4 * i)
                        if u == 3:
                            gelu(2 * i, 0, 4 * i + 2)
                step(0, True)
                with act.Fori(1, STEPS) as i:
                    step(i, False)
                gelu(NBLK - 1, 1, 2 * NBLK)

            @block.vector
            def _(dve):
                def step(i):
                    for u in range(4):
                        dve.wait_ge(u_hi, 4 * i + (u + 1))
                        dve.tensor_tensor(wide(lo[u]), raw[u][:], wide(hi[u]), ALU.subtract).then_inc(u_lo, 1)
                with dve.Fori(0, STEPS) as i:
                    step(i)

            @block.tensor
            def _(pe):
                def step(i, first):
                    for u in range(4):
                        if u % 2 == 0 and not first:
                            pe.wait_ge(h_done, 2 * i + (u // 2 - 1))
                        pe.wait_ge(u_lo, 4 * i + (u + 1))
                        for k in range(4):
                            o, c = ph[:, u // 2, 0:NT], 4 * (u % 2) + k
                            begin, end = c == 0, c == KD - 1
                            pe.matmul(o, hi[u][:, k], xh[:, c], start=begin, stop=False)
                            pe.matmul(o, hi[u][:, k], xl[:, c], start=False, stop=False)
                            ins = pe.matmul(o, lo[u][:, k], xh[:, c], start=False, stop=end)
                        ins.then_inc(u_mm, 1)
                step(0, True)
                with pe.Fori(1, STEPS) as i:
                    step(i, False)
        ps11.free()
        ring.free()

        m12 = Mem()
        RT = m12.sb("RT2", [P, 3, NT])
        oh1 = [m12.sb(f"oh1_{s}", [P, 4, NK]) for s in range(2)]
        oh2 = [m12.sb(f"oh2_{s}", [P, 4, NK]) for s in range(2)]
        ps12 = Mem()
        pg = ps12.ps("pg", [P, 2, 4, NK])
        r_in, oh_ready, g_full, g_used = (sem(n) for n in ("r_in", "oh_ready", "g_full", "g_used"))
        GROUPS = NT // 4
        with nc.Block() as block:
            @block.sync
            def _(sp):
                sp.dma_start(RT[:], rt_dram).then_inc(r_in, 16)

            @block.vector
            def _(dve):
                dve.wait_ge(r_in, 16)

                def times(t0, s, count):
                    dve.wait_ge(g_full, count)
                    h = hid[:, :, bass.ds(t0, 4)]
                    dve.tensor_tensor(h, h, pg[:, s].rearrange("p t k -> p k t"), ALU.mult).then_inc(g_used, 1)

                def step(i, first):
                    for s in range(2):
                        if not first:
                            dve.wait_ge(g_full, 2 * i + (s - 1))
                        for t in range(4):
                            at = 8 * i + 4 * s + t
                            dve.tensor_scalar(oh1[s][:, t], iota[:], RT[:, 0, bass.ds(at, 1)], RT[:, 2, bass.ds(at, 1)],
                                                    ALU.is_equal, ALU.mult)
                        keys = RT[:, 1, bass.ds(8 * i + 4 * s, 4)]
                        dve.tensor_tensor(oh2[s][:], iota[:].unsqueeze(1).to_broadcast([P, 4, NK]),
                                          keys.unsqueeze(2).to_broadcast([P, 4, NK]), ALU.is_equal).then_inc(oh_ready, 1)
                        if s == 1:
                            times(8 * i, 0, 2 * i + 1)
                        elif not first:
                            times(8 * i - 4, 1, 2 * i)
                step(0, True)
                with dve.Fori(1, GROUPS // 2) as i:
                    step(i, False)
                times(NT - 4, 1, GROUPS)

            @block.tensor
            def _(pe):
                def step(i, first):
                    for s in range(2):
                        pe.wait_ge(oh_ready, 2 * i + (s + 1))
                        if not first:
                            pe.wait_ge(g_used, 2 * i + (s - 1))
                        for t in range(4):
                            ins = pe.matmul(pg[:, s, t], oh2[s][:, t], oh1[s][:, t], start=True, stop=True)
                        ins.then_inc(g_full, 1)
                step(0, True)
                with pe.Fori(1, GROUPS // 2) as i:
                    step(i, False)
        ps12.free()
        m12.free()

        ring = Mem()
        raw = [ring.sb(f"raw{u}", [P, 512]) for u in range(4)]
        hi = [ring.sb(f"hi{u}", [P, 4, P], F32R) for u in range(4)]
        lo = [ring.sb(f"lo{u}", [P, 4, P], F32R) for u in range(4)]
        ch = [xh[:, s] for s in range(2)]
        cl = [xl[:, s] for s in range(2)]
        ps13 = Mem()
        acc = ps13.ps("acc", [P, KD, 512])
        v_in = [sem(f"v_in{u}") for u in range(4)]
        v_hi, v_lo, v_mm, c_hi, c_lo = (sem(n) for n in ("v_hi", "v_lo", "v_mm", "c_hi", "c_lo"))
        with nc.Block() as block:
            @block.sync
            def _(sp):
                def step(i, first):
                    for u in range(4):
                        if not first:
                            sp.wait_ge(v_lo, 4 * i + (u - 3))
                        src = inp["v"][bass.ds(2 * i + u // 2, 1), :, 512 * (u % 2):512 * (u % 2) + 512]
                        sp.dma_start(raw[u][:], src.rearrange("b p n -> p (b n)")).then_inc(v_in[u], 16)
                step(0, True)
                with sp.Fori(1, STEPS) as i:
                    step(i, False)

            @block.scalar
            def _(act):
                def step(i, first):
                    for u in range(4):
                        act.wait_ge(v_in[u], 16 * i + 16)
                        if not first:
                            act.wait_ge(v_mm, 4 * i + (u - 2 if u % 2 == 0 else u - 3))
                        if u % 2 == 0:
                            act.activation(ch[u // 2], hid[:, bass.ds(2 * i + u // 2, 1), :].rearrange("p b t -> p (b t)"),
                                           ACT.Copy).then_inc(c_hi, 1)
                        act.activation(wide(hi[u]), raw[u][:], ACT.Copy).then_inc(v_hi, 1)
                step(0, True)
                with act.Fori(1, STEPS) as i:
                    step(i, False)

            @block.vector
            def _(dve):
                def step(i):
                    for u in range(4):
                        if u % 2 == 0:
                            dve.wait_ge(c_hi, 2 * i + (u // 2 + 1))
                            dve.tensor_tensor(cl[u // 2], hid[:, bass.ds(2 * i + u // 2, 1), :].rearrange("p b t -> p (b t)"),
                                              ch[u // 2], ALU.subtract).then_inc(c_lo, 1)
                        dve.wait_ge(v_hi, 4 * i + (u + 1))
                        dve.tensor_tensor(wide(lo[u]), raw[u][:], wide(hi[u]), ALU.subtract).then_inc(v_lo, 1)
                with dve.Fori(0, STEPS) as i:
                    step(i)

            @block.tensor
            def _(pe):
                def step(i, first, last):
                    for u in range(4):
                        if u % 2 == 0:
                            pe.wait_ge(c_lo, 2 * i + (u // 2 + 1))
                        pe.wait_ge(v_lo, 4 * i + (u + 1))
                        begin, end = first and u < 2, last and u >= 2
                        for k in range(4):
                            o, s = acc[:, 4 * (u % 2) + k, 0:NT], u // 2
                            pe.matmul(o, hi[u][:, k], ch[s], start=begin, stop=False)
                            pe.matmul(o, hi[u][:, k], cl[s], start=False, stop=False)
                            ins = pe.matmul(o, lo[u][:, k], ch[s], start=False, stop=end)
                        ins.then_inc(v_mm, 1)
                step(0, True, False)
                with pe.Fori(1, STEPS - 1) as i:
                    step(i, False, False)
                step(STEPS - 1, False, True)
        ring.free()
        big_mem.free()

        m14 = Mem()
        oT = m14.sb("oT", [P, KD, NT])
        x2 = m14.sb("x2", [P, 3, D])
        nf = m14.sb("nf", [P, D])
        sq14 = m14.sb("sq14", [P, D])
        rs14 = m14.sb("rs14", [P, 16])
        x2_in, o_taken, y_full14, y_sum, sq14d, rt14, dv14, y_done, y_out = (
            sem(n) for n in ("x2_in", "o_taken", "y_full14", "y_sum", "sq14d", "rt14", "dv14", "y_done", "y_out"))
        with nc.Block() as block:
            @block.sync
            def _(sp):
                for i, (c0, w) in enumerate(PT):
                    sp.dma_start(x2[0:w, i], x1_dram[c0:c0 + w]).then_inc(x2_in, 16)
                sp.dma_start(nf[:], inp["norm_f"].to_broadcast([P, D])).then_inc(x2_in, 16)
                for i, (c0, w) in enumerate(PT):
                    sp.wait_ge(y_done, i + 1)
                    sp.dma_start(out["y"][c0:c0 + w], x2[0:w, i]).then_inc(y_out, 16)
                sp.wait_ge(y_out, 48)

            @block.scalar
            def _(act):
                for j in range(KD):
                    act.activation(oT[:, j], acc[:, j, 0:NT], ACT.Copy).then_inc(o_taken, 1)
                for i, (c0, w) in enumerate(PT):
                    act.wait_ge(y_sum, i + 1)
                    if i:
                        act.wait_ge(sq14d, i)
                    act.activation(sq14[0:w], x2[0:w, i], ACT.Square, accum_out=rs14[0:w, i:i + 1]).then_inc(sq14d, 1)
                    act.wait_ge(sq14d, i + 1)
                    act.activation(rs14[0:w, 3 + i:4 + i], rs14[0:w, i:i + 1], ACT.Sqrt, bias=epsc[0:w, 0:1],
                                   scale=1.0 / D).then_inc(rt14, 1)

            @block.tensor
            def _(pe):
                pe.wait_ge(o_taken, KD)
                for i, (c0, w) in enumerate(PT):
                    for j in range(KD):
                        ins = pe.transpose(acc[0:w, 2 * i + j // 4, P * (j % 4):P * (j % 4) + P], oT[:, j, c0:c0 + w], ident[:])
                    ins.then_inc(y_full14, 1)

            @block.vector
            def _(dve):
                link = linker(dve, dv14)
                dve.wait_ge(x2_in, 64)
                for i, (c0, w) in enumerate(PT):
                    dve.wait_ge(y_full14, i + 1)
                    dve.tensor_tensor(x2[0:w, i], x2[0:w, i], acc[0:w, 2 * i:2 * i + 2].rearrange("p a b -> p (a b)"),
                                      ALU.add).then_inc(y_sum, 1)
                for i, (c0, w) in enumerate(PT):
                    dve.wait_ge(rt14, i + 1)
                    link(dve.reciprocal(rs14[0:w, 6 + i:7 + i], rs14[0:w, 3 + i:4 + i]))
                    dve.scalar_tensor_tensor(out=x2[0:w, i], in0=x2[0:w, i], scalar=rs14[0:w, 6 + i:7 + i], in1=nf[0:w],
                                             op0=ALU.mult, op1=ALU.mult).then_inc(y_done, 1)
        ps13.free()
        m14.free()
        base.free()


_LAYOUT = [("norm1", 8), ("norm2", 8), ("theta0", 4), ("theta1", 4), ("hgrn_norm", 4), ("mu", FB), ("w0", 4),
           ("a0", 4), ("k_k", 4), ("k_a", 4), ("r_k", 4), ("ln_w", 4), ("ln_b", 4)]
FEAT, NFEAT = {}, 0
for _name, _n in _LAYOUT:
    FEAT[_name] = NFEAT
    NFEAT += _n

_OUTS = {
    "y": (NT, D),
    "hgrn_p": (P, HA, P),
    "hgrn_s": (P, NS, HA, P),
    "rwkv_p": (P, 4, HN),
    "rwkv_s": (P, 4, NS, HN),
    "shift": (P, FB, 1 + NS),
}


def layout(inputs):
    a = {k: np.asarray(v) for k, v in inputs.items()}
    f32 = np.float32
    rows = np.concatenate([a["meta_tokens"], a["x_prompt"][0], np.zeros((SAMP0 - PROMPT, D), f32),
                           a["x_sample"].reshape(-1, D), np.zeros((3 * P - C, D), f32)])
    w_in = a["w_in"][0].reshape(KD, P, 30, P).transpose(2, 1, 0, 3)
    cols = lambda v: v.reshape(-1, P).T
    parts = {"norm1": a["norm1"][0], "norm2": a["norm2"][0], "theta0": a["lb_theta"][0], "theta1": a["lb_theta"][1],
             "hgrn_norm": a["hgrn_norm"][0], "mu": a["mu_shift"][0], "w0": a["w0"][0], "a0": a["a0"][0],
             "k_k": a["k_k"][0], "k_a": a["k_a"][0], "r_k": a["r_k"][0], "ln_w": a["ln_w"][0], "ln_b": a["ln_b"][0]}
    masks, misc = shape_constants()
    wq = a["peer_wq"][0].reshape(KD, P, 16, P).transpose(2, 1, 0, 3)
    out = {
        "x_rows": rows.reshape(3, P, D),
        "masks": masks,
        "misc": misc,
        "feat": np.concatenate([cols(parts[n]) for n, _ in _LAYOUT], axis=1),
        "w_zi": a["w_in"][0][:, 1024:1536].reshape(KD, P, 512).transpose(1, 0, 2),
        "w_tiles": np.concatenate([w_in[0:8], w_in[12:16], w_in[16:30]]),
        "shift0": a["state_shift"][0].reshape(NS, FB, P).transpose(2, 1, 0),
        "state_h": a["state_hgrn"][0].transpose(2, 0, 1, 3),
        "state_r": a["state_rwkv"][0].reshape(NS, 4, 2, HN, HN).transpose(2, 4, 1, 0, 3).reshape(P, 4, NS, HN),
        "lora": np.concatenate([np.concatenate([a["w_w2"][0], a["a_w2"][0]], axis=0), a["g_w2"][0]], axis=1),
        "w_out": a["w_out"][0].reshape(8, P, D).transpose(1, 0, 2),
        "w_q": wq,
        "keysT": a["peer_keys"][0].transpose(2, 0, 1),
        "uT": a["peer_u"][0].reshape(NK, NK, KD, P).transpose(0, 3, 2, 1),
        "v": a["peer_v"][0].reshape(NK, NK, D),
        "norm_f": a["norm_f"].reshape(1, D),
    }
    return {k: np.ascontiguousarray(v) for k, v in out.items()}


def kernel(**inputs):
    import concourse.bacc as bacc
    from concourse.bass_utils import run_bass_kernel_spmd

    arrays = layout(inputs)
    nc = bacc.Bacc("TRN2", target_bir_lowering=False, num_devices=1)
    inp = {k: nc.dram_tensor(f"in_{k}", v.shape, mybir.dt.from_np(v.dtype), kind="ExternalInput").ap()
           for k, v in arrays.items()}
    out = {k: nc.dram_tensor(f"out_{k}", s, F32, kind="ExternalOutput").ap() for k, s in _OUTS.items()}
    build_program(nc, inp, out)
    r = run_bass_kernel_spmd(nc, [{f"in_{k}": v for k, v in arrays.items()}], core_ids=[0]).results[0]
    got = {k: np.asarray(r[f"out_{k}"]) for k in _OUTS}
    y = got["y"]
    shift = got["shift"].transpose(2, 1, 0).reshape(1 + NS, FB * P)
    rwkv = lambda s: s.reshape(2, HN, 4, -1, HN).transpose(3, 2, 0, 4, 1).reshape(-1, HB, HN, HN)
    return (np.ascontiguousarray(y[:SEQ][None]),
            np.ascontiguousarray(y[SEQ:NT].reshape(NS, LS, D)),
            np.ascontiguousarray(got["hgrn_p"].transpose(1, 0, 2)[None, None]),
            np.ascontiguousarray(rwkv(got["rwkv_p"][:, :, None])[None]),
            np.ascontiguousarray(shift[None, 0:1]),
            np.ascontiguousarray(got["hgrn_s"].transpose(1, 2, 0, 3)[None]),
            np.ascontiguousarray(rwkv(got["rwkv_s"])[None]),
            np.ascontiguousarray(shift[None, 1:]))
```

```python
from contextlib import ExitStack

import numpy as np

import concourse.bass as bass
from concourse import mybir

ALU = mybir.AluOpType
ACT = mybir.ActivationFunctionType
AX = mybir.AxisListType.X
F32 = mybir.dt.float32
F32R = mybir.dt.float32r
U32 = mybir.dt.uint32

P = 128
D = 1024
KD = D // P
META, SEQ, NS, LS = 16, 256, 8, 8
PROMPT = META + SEQ
SAMP0 = 288
C = SAMP0 + NS * LS
TW = [128, 128, C - 256]
HA, HB, HN = 4, 8, 64
FB = 14
EPS, GN_EPS = 1e-6, 64e-5
NT = SEQ + NS * LS
PT = [(0, 128), (128, 128), (256, 64)]
PH, NK, TOPK = 8, 128, 16
NBLK = NK
NMASK = 12
(M_ID, M_BU, M_BL, M_EU, M_SU, M_IU, M_TBU, M_TBL, M_TIU, M_HI, M_HO, M_B64) = range(NMASK)


def shape_constants():
    s, t = np.arange(P)[:, None], np.arange(P)[None, :]
    blk = lambda n: s // n == t // n
    seq = np.where(np.arange(P) < 16, 100, np.where(np.arange(P) < 32, 101, np.arange(P) // 8))
    same = seq[:, None] == seq[None, :]
    m = np.zeros((P, NMASK, P), np.float32)
    m[:, M_ID] = s == t
    m[:, M_BU] = blk(16) & (s < t)
    m[:, M_BL] = blk(16) & (s > t)
    m[:, M_EU] = blk(64) & ~blk(16) & (s < t)
    m[:, M_SU] = blk(64) & (s < t)
    m[:, M_IU] = blk(64) & (s <= t)
    m[:, M_TBU] = same & (s < t)
    m[:, M_TBL] = same & (s > t)
    m[:, M_TIU] = same & (s <= t)
    m[:, M_HI] = blk(16) & (s <= t)
    m[:, M_HO] = blk(32) & ~blk(16) & (s < t)
    m[:, M_B64] = blk(64)
    col = np.arange(C)
    start = np.where(col < PROMPT, col % 64 == 0, np.where(col < SAMP0, col == PROMPT, col % 8 == 0))
    restart = np.broadcast_to(np.where(start, 0.0, 1.0), (P, C)).astype(np.float32)
    seq9 = np.zeros((P, 9), np.float32)
    seq9[:16, 8] = 1
    for n in range(NS):
        seq9[32 + 8 * n:40 + 8 * n, n] = 1
    x = np.arange(144)
    pat = np.stack([x % 16 == 0, x % 8 == 0]).astype(np.float32)
    misc = np.concatenate([restart, seq9, np.broadcast_to(np.arange(P, dtype=np.float32), (P, P)),
                           np.broadcast_to(pat.reshape(1, 288), (P, 288)), np.ones((P, P), np.float32)], axis=1)
    return m, np.ascontiguousarray(misc.astype(np.float32))


NMISC = C + 9 + P + 288 + P


def build_program(nc, inp, out):
    with ExitStack() as whole:
        names = [0]

        def sem(name):
            names[0] += 1
            return whole.enter_context(nc.semaphore(f"{name}_{names[0]}"))

        def linker(eng, s):
            n = [0]

            def link(ins):
                n[0] += 1
                ins.then_inc(s, 1)
                eng.wait_ge(s, n[0])
            return link

        class Mem:
            def __init__(self):
                self.ctx = ExitStack()

            def sb(self, name, shape, dt=F32):
                names[0] += 1
                return self.ctx.enter_context(nc.sbuf_tensor(f"{name}_{names[0]}", shape, dt))

            def ps(self, name, shape):
                names[0] += 1
                return self.ctx.enter_context(nc.psum_tensor(f"{name}_{names[0]}", shape, F32))

            def free(self):
                self.ctx.close()

        base = Mem()
        ident = base.sb("identity", [P, P])
        iota = base.sb("iota", [P, P])
        feat = base.sb("feat", [P, NFEAT])
        epsc = base.sb("epsc", [P, 4])
        xh = base.sb("xh", [P, KD, NT], F32R)
        xl = base.sb("xl", [P, KD, NT], F32R)
        mask_mem = Mem()
        masks = mask_mem.sb("masks", [P, NMASK, P])
        misc = mask_mem.sb("misc", [P, NMISC])
        restart = misc[:, 0:C]
        seq9 = misc[:, C:C + 9]
        pat16 = misc[:, C + 9 + P:C + 9 + P + 144]
        pat8 = misc[:, C + 9 + P + 144:C + 9 + P + 288]
        ones = misc[:, C + 9 + P + 288:C + 9 + P + 288 + P]
        x1_dram = nc.dram_tensor("x1_scratch", [NT, D], F32).ap()

        def col(name, i=0, n=1):
            return feat[:, FEAT[name] + i:FEAT[name] + i + n]

        mix_mem = Mem()
        mixT = mix_mem.sb("mixT", [P, 8, C])
        zb_mem = Mem()
        zbT = zb_mem.sb("zbT", [P, FB, 289 + 9 * NS])
        za_mem = Mem()
        qT = za_mem.sb("qT", [P, HA, C])
        fT = za_mem.sb("fT", [P, HA, C])
        kT = za_mem.sb("kT", [P, HA, C])
        zoT = za_mem.sb("zoT", [P, HA, C])
        vtok = za_mem.sb("vtok", [P, 3, HA, P])
        in_mem = Mem()
        xnT = in_mem.sb("xnT", [P, KD, C])
        wslot = in_mem.sb("wslot", [P, 4, KD, P])
        wzi = in_mem.sb("wzi", [P, KD, 512])
        sig = in_mem.sb("sig", [P, 2, 2, C])
        shift0 = in_mem.sb("shift0", [P, FB, NS])
        lbt = in_mem.sb("lbt", [P, 6, HA])
        t1 = Mem()
        x = t1.sb("x", [P, 3, D])
        sq = t1.sb("sq", [P, D])
        rs = t1.sb("rs", [P, 16])
        pst = t1.ps("pst", [P, 2, 4, P])

        x_in, c_in = sem("x_in"), sem("c_in")
        sq_done, rt_done, rstd_done, xn_done, dv1 = (sem(n) for n in ("sq", "rt", "rstd", "xn", "dv1"))
        tr_full, tr_free = sem("tr_full"), sem("tr_free")
        const_ready = sem("const_ready")
        with nc.Block() as block:
            @block.sync
            def _(sp):
                sp.dma_start(x[:], inp["x_rows"].rearrange("k p d -> p k d")).then_inc(x_in, 16)
                sp.dma_start(masks[:], inp["masks"]).then_inc(c_in, 16)
                sp.dma_start(misc[:], inp["misc"]).then_inc(c_in, 16)
                sp.dma_start(feat[:], inp["feat"]).then_inc(c_in, 16)
                sp.dma_start(ident[:], inp["masks"][:, M_ID]).then_inc(c_in, 16)
                sp.dma_start(iota[:], inp["misc"][:, C + 9:C + 9 + P]).then_inc(c_in, 16)

            @block.gpsimd
            def _(pool):
                pool.memset(epsc[:, 0:1], EPS).then_inc(const_ready, 1)
                pool.memset(epsc[:, 1:2], GN_EPS).then_inc(const_ready, 1)
                pool.memset(epsc[:, 2:3], 0.0).then_inc(const_ready, 1)
                pool.memset(zbT[:, :, 0:1], 0.0).then_inc(const_ready, 1)

            @block.scalar
            def _(act):
                act.wait_ge(x_in, 16)
                act.wait_ge(const_ready, 4)
                for i in range(3):
                    if i:
                        act.wait_ge(sq_done, i)
                    act.activation(sq[:], x[:, i], ACT.Square, accum_out=rs[:, i:i + 1]).then_inc(sq_done, 1)
                act.wait_ge(sq_done, 3)
                act.activation(rs[:, 3:6], rs[:, 0:3], ACT.Sqrt, bias=epsc[:, 0:1], scale=1.0 / D).then_inc(rt_done, 1)

            @block.vector
            def _(dve):
                dve.wait_ge(rt_done, 1)
                dve.reciprocal(rs[:, 6:9], rs[:, 3:6]).then_inc(rstd_done, 1)
                dve.wait_ge(rstd_done, 1)
                for i in range(3):
                    dve.tensor_scalar(x[:, i], x[:, i], rs[:, 6 + i:7 + i], None, ALU.mult).then_inc(xn_done, 1)
                dve.wait_ge(c_in, 80)
                for i in range(3):
                    for j in range(KD):
                        n = KD * i + j
                        if n % 4 == 0:
                            dve.wait_ge(tr_full, n // 4 + 1)
                        w = TW[i]
                        ins = dve.tensor_scalar(xnT[:, j, P * i:P * i + w], pst[:, n // 4 % 2, n % 4, 0:w],
                                                col("norm1", j), None, ALU.mult)
                        if n % 4 == 3:
                            ins.then_inc(tr_free, 1)

            @block.tensor
            def _(pe):
                pe.wait_ge(c_in, 80)
                for n in range(3 * KD):
                    i, j = divmod(n, KD)
                    if j == 0:
                        pe.wait_ge(xn_done, i + 1)
                    if n % 4 == 0 and n >= 8:
                        pe.wait_ge(tr_free, n // 4 - 1)
                    ins = pe.transpose(pst[:, n // 4 % 2, n % 4, :], x[:, i, P * j:P * j + P], ident[:])
                    if n % 4 == 3:
                        ins.then_inc(tr_full, 1)
        t1.free()

        tiles = [("q", i) for i in range(4)] + [("f", i) for i in range(4)] + [("o", i) for i in range(4)] + \
                [("b", i) for i in range(FB)]
        NF = len(tiles)
        t2 = Mem()
        pz = t2.ps("pz", [P, 8, 512])
        w_in_slot = [sem(f"w_in_slot{i}") for i in range(4)]
        zi_in, sh_in = sem("zi_in"), sem("sh_in")
        z_full, z_act, z_dve, z_tok, dv2, a2, shift_copied = (
            sem(n) for n in ("z_full", "z_act", "z_dve", "z_tok", "dv2", "a2", "shift_copied"))
        with nc.Block() as block:
            @block.sync
            def _(sp):
                sp.dma_start(wzi[:], inp["w_zi"]).then_inc(zi_in, 16)
                sp.dma_start(shift0[:], inp["shift0"]).then_inc(sh_in, 16)
                for n in range(NF):
                    if n >= 4:
                        sp.wait_ge(z_full, 3 + n - 3)
                    sp.dma_start(wslot[:, n % 4], inp["w_tiles"][n]).then_inc(w_in_slot[n % 4], 16)

            @block.tensor
            def _(pe):
                pe.wait_ge(zi_in, 16)
                for i in range(3):
                    for k in range(KD):
                        ins = pe.matmul(pz[0:TW[i], i, :], xnT[:, k, P * i:P * i + TW[i]], wzi[:, k, :],
                                        start=k == 0, stop=k == KD - 1)
                    ins.then_inc(z_full, 1)
                for n in range(NF):
                    bank = (n + 3) % 8
                    if n >= 5:
                        m = n - 8
                        if m < 0:
                            pe.wait_ge(z_tok, n - 4)
                        elif m < 12:
                            pe.wait_ge(z_dve, m + 1)
                        else:
                            pe.wait_ge(z_act, m + 1)
                    pe.wait_ge(w_in_slot[n % 4], 16 * (n // 4 + 1))
                    for k in range(KD):
                        ins = pe.matmul(pz[:, bank, 0:C], wslot[:, n % 4, k], xnT[:, k],
                                        start=k == 0, stop=k == KD - 1)
                    ins.then_inc(z_full, 1)

            @block.scalar
            def _(act):
                act.wait_ge(a2, 1)
                act.activation(lbt[:, 2:4], lbt[:, 0:2], ACT.Exp).then_inc(a2, 1)
                for n, (kind, i) in enumerate(tiles):
                    bank = (n + 3) % 8
                    act.wait_ge(z_full, 4 + n)
                    if kind in "qfo" and n >= 2:
                        act.wait_ge(z_dve, n - 1)
                    if kind in "qo":
                        act.activation(sig[:, n % 2, 0], pz[:, bank, 0:C], ACT.Sigmoid).then_inc(z_act, 1)
                    elif kind == "f":
                        act.activation(sig[:, n % 2, 0], pz[:, bank, 0:C], ACT.Sigmoid)
                        act.activation(sig[:, n % 2, 1], pz[:, bank, 0:C], ACT.Sigmoid, scale=-1.0).then_inc(z_act, 1)
                    else:
                        act.activation(zbT[:, i, 1:289], pz[:, bank, 0:288], ACT.Copy)
                        act.activation(zbT[:, i, 289:361].rearrange("p (s l) -> p s l", l=9)[:, :, 1:9],
                                       pz[:, bank, 288:C].rearrange("p (s l) -> p s l", l=8),
                                       ACT.Copy).then_inc(z_act, 1)

            @block.vector
            def _(dve):
                link = linker(dve, dv2)
                th0, th1 = col("theta0", 0, 4), col("theta1", 0, 4)
                link(dve.tensor_tensor(lbt[:, 0], th0, th1, ALU.max))
                dve.tensor_tensor(lbt[:, 1], th0, lbt[:, 0], ALU.subtract)
                link(dve.tensor_tensor(lbt[:, 2], th1, lbt[:, 0], ALU.subtract))
                link(dve.tensor_copy(lbt[:, 0], lbt[:, 1]))
                dve.tensor_copy(lbt[:, 1], lbt[:, 2]).then_inc(a2, 1)
                dve.wait_ge(sh_in, 16)
                dve.tensor_copy(zbT[:, :, 289:361].rearrange("p f (s l) -> p f s l", l=9)[:, :, :, 0],
                                shift0[:]).then_inc(shift_copied, 1)
                dve.wait_ge(a2, 2)
                link(dve.tensor_tensor(lbt[:, 4], lbt[:, 2], lbt[:, 3], ALU.add))
                link(dve.reciprocal(lbt[:, 5], lbt[:, 4]))
                link(dve.tensor_tensor(lbt[:, 0], lbt[:, 2], lbt[:, 5], ALU.mult))
                link(dve.tensor_scalar(lbt[:, 1], lbt[:, 0], -1.0, 1.0, ALU.mult, ALU.add))
                for i in range(3):
                    dve.wait_ge(z_full, i + 1)
                    dve.tensor_copy(vtok[0:TW[i], i], pz[0:TW[i], i, :].rearrange("p (h e) -> p h e", e=P)) \
                        .then_inc(z_tok, 1)
                for n, (kind, i) in enumerate(tiles[:12]):
                    bank = (n + 3) % 8
                    dve.wait_ge(z_act, n + 1)
                    if kind in "qo":
                        dst = qT if kind == "q" else zoT
                        dve.tensor_tensor(dst[:, i], pz[:, bank, 0:C], sig[:, n % 2, 0], ALU.mult).then_inc(z_dve, 1)
                    else:
                        dve.tensor_scalar(fT[:, i], sig[:, n % 2, 0], lbt[:, 1, i:i + 1], lbt[:, 0, i:i + 1],
                                          ALU.mult, ALU.add)
                        dve.tensor_scalar(kT[:, i], sig[:, n % 2, 1], lbt[:, 1, i:i + 1], None,
                                          ALU.mult).then_inc(z_dve, 1)
        t2.free()
        in_mem.free()
        NB = SAMP0 // 16
        h_mem = Mem()
        scT = h_mem.sb("scT", [P, 3, HA, P])
        q2 = h_mem.sb("q2", [P, HA, C])
        k2h = h_mem.sb("k2h", [P, HA, C])
        ktok = h_mem.sb("ktok", [P, 3, HA, P])
        f16 = h_mem.sb("f16", [P, HA, NB])
        f8 = h_mem.sb("f8", [P, HA, NS])
        f32c = h_mem.sb("f32c", [P, HA, NB // 2])
        hp_mem = Mem()
        prod16 = hp_mem.sb("prod16", [P, 2, HA, NB, 16])
        prod8 = hp_mem.sb("prod8", [P, 2, HA, NS, LS])
        suf16 = hp_mem.sb("suf16", [P, HA, NB, 16])
        suf8 = hp_mem.sb("suf8", [P, HA, NS, LS])
        offm = hp_mem.sb("offm", [P, 2, HA, P])
        ps_h = Mem()
        psI = ps_h.ps("psI", [P, HA, 512])
        psS = ps_h.ps("psS", [P, 512])
        psO = ps_h.ps("psO", [P, 2, HA, P])
        psK = ps_h.ps("psK", [P, HA, P])
        prod_zero, prod_ready, prod_used, dv3, q_decayed, off_full, kt_full, kt_free, sc_done = (
            sem(n) for n in ("prod_zero", "prod_ready", "prod_used", "dv3", "q_decayed", "off_full", "kt_full",
                             "kt_free", "sc_done"))
        blocks16 = lambda a: a[:, :, 0:SAMP0].rearrange("p h (c j) -> p h c j", j=16)
        blocks8 = lambda a: a[:, :, SAMP0:C].rearrange("p h (c j) -> p h c j", j=8)
        with nc.Block() as block:
            @block.gpsimd
            def _(pool):
                pool.memset(prod16[:], 0.0).then_inc(prod_zero, 1)
                pool.memset(prod8[:], 0.0).then_inc(prod_zero, 1)
                pool.memset(suf16[:], 1.0).then_inc(prod_zero, 1)
                pool.memset(suf8[:], 1.0).then_inc(prod_zero, 1)

            @block.vector
            def _(dve):
                link = linker(dve, dv3)
                q16, f16v, k16 = blocks16(qT), blocks16(fT), blocks16(kT)
                q8, f8v, k8 = blocks8(qT), blocks8(fT), blocks8(kT)
                dve.wait_ge(prod_zero, 4)
                for n in range(16):
                    i, j = 15 - n, 7 - n
                    if n:
                        r16 = q16[:, :, :, i + 1:16]
                        ins = dve.tensor_tensor(r16, r16, f16v[:, :, :, i + 1:i + 2].to_broadcast([P, HA, NB, n]), ALU.mult)
                        if 0 < n < 8:
                            r8 = q8[:, :, :, j + 1:8]
                            ins = dve.tensor_tensor(r8, r8, f8v[:, :, :, j + 1:j + 2].to_broadcast([P, HA, NS, n]), ALU.mult)
                        link(ins)
                    if n >= 2:
                        dve.wait_ge(prod_used, n - 1)
                    ins = dve.tensor_tensor(prod16[:, n % 2, :, :, i:16], q16[:, :, :, i:16],
                                            k16[:, :, :, i:i + 1].to_broadcast([P, HA, NB, n + 1]), ALU.mult)
                    if n < 8:
                        ins = dve.tensor_tensor(prod8[:, n % 2, :, :, j:8], q8[:, :, :, j:8],
                                                k8[:, :, :, j:j + 1].to_broadcast([P, HA, NS, n + 1]), ALU.mult)
                    ins.then_inc(prod_ready, 1)
                dve.tensor_tensor(q16, q16, f16v[:, :, :, 0:1].to_broadcast([P, HA, NB, 16]), ALU.mult)
                link(dve.tensor_tensor(q8, q8, f8v[:, :, :, 0:1].to_broadcast([P, HA, NS, 8]), ALU.mult))
                for i in range(14, -1, -1):
                    ins = dve.tensor_tensor(suf16[:, :, :, i:i + 1], suf16[:, :, :, i + 1:i + 2],
                                            f16v[:, :, :, i + 1:i + 2], ALU.mult)
                    if i < 7:
                        ins = dve.tensor_tensor(suf8[:, :, :, i:i + 1], suf8[:, :, :, i + 1:i + 2],
                                                f8v[:, :, :, i + 1:i + 2], ALU.mult)
                    link(ins)
                dve.tensor_tensor(k16, k16, suf16[:], ALU.mult)
                dve.tensor_tensor(k8, k8, suf8[:], ALU.mult)
                dve.tensor_tensor(f16[:], suf16[:, :, :, 0], f16v[:, :, :, 0], ALU.mult)
                dve.tensor_tensor(f8[:], suf8[:, :, :, 0], f8v[:, :, :, 0], ALU.mult).then_inc(q_decayed, 1)
                dve.wait_ge(q_decayed, 1)
                dve.tensor_copy(q2[:], qT[:])
                link(dve.tensor_copy(k2h[:], kT[:]))
                pairs = lambda a: a[:, :, 0:256].rearrange("p h (c b j) -> p h c b j", b=2, j=16)
                fe = f16[:, :, 0:16].rearrange("p h (c b) -> p h c b", b=2)
                for h in range(HA):
                    dve.tensor_tensor(pairs(q2)[:, h, :, 1], pairs(qT)[:, h, :, 1],
                                      fe[:, h, :, 0:1].to_broadcast([P, 8, 16]), ALU.mult)
                    dve.tensor_tensor(pairs(k2h)[:, h, :, 0], pairs(kT)[:, h, :, 0],
                                      fe[:, h, :, 1:2].to_broadcast([P, 8, 16]), ALU.mult)
                dve.tensor_copy(f32c[:, :, 8:9], f16[:, :, 16:17])
                dve.tensor_tensor(f32c[:, :, 0:8], fe[:, :, :, 0], fe[:, :, :, 1], ALU.mult).then_inc(q_decayed, 1)
                dve.wait_ge(off_full, 1)
                dve.wait_ge(prod_used, 16)
                mask = lambda m, n, w: masks[0:n, m:m + 1, 0:w].to_broadcast([n, HA, w])
                for i in range(2):
                    dve.tensor_tensor(offm[:, i], psO[:, i], mask(M_HO, P, P), ALU.mult)
                    dve.tensor_tensor(scT[:, i], psI[:, :, P * i:P * i + P], mask(M_HI, P, P), ALU.mult)
                dve.tensor_tensor(scT[0:96, 2, :, 0:32], psI[0:96, :, 256:288], mask(M_HI, 96, 32), ALU.mult)
                link(dve.tensor_tensor(scT[0:96, 2, :, 32:96], psS[0:96, 0:256].rearrange("p (h t) -> p h t", h=HA),
                                       masks[0:96, M_TIU:M_TIU + 1, 32:96].to_broadcast([96, HA, 64]), ALU.mult))
                dve.tensor_tensor(scT[:, 0:2], scT[:, 0:2], offm[:], ALU.add).then_inc(sc_done, 1)

            @block.tensor
            def _(pe):
                for n in range(16):
                    i, j = 15 - n, 7 - n
                    pe.wait_ge(prod_ready, n + 1)
                    for h in range(HA):
                        ins = pe.matmul(psI[:, h, 0:SAMP0], pat16[:, 16 - i:144 - i],
                                        prod16[:, n % 2, h].rearrange("p c j -> p (c j)"), start=n == 0, stop=n == 15)
                    if n < 8:
                        ins = pe.matmul(psS[:, 0:256], pat8[:, 8 - j:136 - j],
                                        prod8[:, n % 2].rearrange("p h c j -> p (h c j)"), start=n == 0, stop=n == 7)
                    ins.then_inc(prod_used, 1)
                pe.wait_ge(q_decayed, 1)
                for i in range(2):
                    for h in range(HA):
                        ins = pe.matmul(psO[:, i, h], kT[:, h, P * i:P * i + P], qT[:, h, P * i:P * i + P],
                                        start=True, stop=True)
                ins.then_inc(off_full, 1)
                pe.wait_ge(q_decayed, 2)
                for i in range(3):
                    if i:
                        pe.wait_ge(kt_free, i)
                    for h in range(HA):
                        ins = pe.transpose(psK[0:TW[i], h], k2h[:, h, P * i:P * i + TW[i]], ident[:])
                    ins.then_inc(kt_full, 1)

            @block.scalar
            def _(act):
                for i in range(3):
                    act.wait_ge(kt_full, i + 1)
                    act.activation(ktok[0:TW[i], i], psK[0:TW[i]], ACT.Copy).then_inc(kt_free, 1)
        ps_h.free()
        hp_mem.free()

        NCH = 9
        s_mem = Mem()
        sts = s_mem.sb("sts", [P, NCH, HA, P])
        sth = s_mem.sb("sth", [P, NS, HA, P])
        stn = s_mem.sb("stn", [P, NS, HA, P])
        vexp = s_mem.sb("vexp", [P, 2, NS, P])
        osq = s_mem.sb("osq", [P, HA, C])
        rsh = s_mem.sb("rsh", [P, 2, HA, C])
        ps4 = Mem()
        kv = ps4.ps("kv", [P, 4, 512])
        po = ps4.ps("po", [P, HA, 512])
        hs_in, vexp_ready, vexp_used, kv_full, kv_free, st_ready, o_full, sq_ready, ms_full, rt_h, dv4, hst_out = (
            sem(n) for n in ("hs_in", "vexp_ready", "vexp_used", "kv_full", "kv_free", "st_ready", "o_full",
                             "sq_ready", "ms_full", "rt_h", "dv4", "hst_out"))
        with nc.Block() as block:
            @block.sync
            def _(sp):
                sp.dma_start(sth[:], inp["state_h"]).then_inc(hs_in, 16)
                sp.wait_ge(st_ready, NCH)
                sp.dma_start(out["hgrn_p"], sts[:, NCH - 1]).then_inc(hst_out, 16)
                sp.wait_ge(st_ready, NCH + 2 * HA)
                sp.dma_start(out["hgrn_s"], stn[:]).then_inc(hst_out, 16)
                sp.wait_ge(hst_out, 32)

            @block.tensor
            def _(pe):
                for c in range(NCH):
                    if c >= 4:
                        pe.wait_ge(kv_free, c - 3)
                    b, w = 32 * c % P, 32 if c < 8 else 16
                    for h in range(HA):
                        ins = pe.matmul(kv[:, c % 4, P * h:P * h + P], ktok[b:b + w, c // 4, h], vtok[b:b + w, c // 4, h],
                                        start=True, stop=True)
                    ins.then_inc(kv_full, 1)
                for h in range(HA):
                    pe.wait_ge(vexp_ready, h + 1)
                    for g in range(2):
                        n = NCH + 2 * h + g
                        pe.wait_ge(kv_free, n - 3)
                        ins = pe.matmul(kv[:, n % 4, :], ktok[0:96, 2, h],
                                        vexp[0:96, h % 2, 4 * g:4 * g + 4].rearrange("p s e -> p (s e)"),
                                        start=True, stop=True)
                        ins.then_inc(kv_full, 1)
                pe.wait_ge(hs_in, 16)
                pe.wait_ge(st_ready, NCH)
                for h in range(HA):
                    for i in range(3):
                        pe.matmul(po[:, h, P * i:P * i + TW[i]], vtok[0:TW[i], i, h], scT[0:TW[i], i, h, 0:TW[i]],
                                  start=i == 0, stop=False, skip_group_check=True)
                    for c in range(1, NCH):
                        w = 32 if c < 8 else 16
                        pe.matmul(po[:, h, 32 * c:32 * c + w], sts[:, c - 1, h], q2[:, h, 32 * c:32 * c + w],
                                  start=False, stop=False, skip_group_check=True)
                    for s in range(NS):
                        t = SAMP0 + LS * s
                        ins = pe.matmul(po[:, h, t:t + LS], sth[:, s, h], q2[:, h, t:t + LS],
                                        start=False, stop=s == NS - 1, skip_group_check=True)
                    ins.then_inc(o_full, 1)
                for h in range(HA):
                    if h == 0:
                        pe.wait_ge(kv_free, NCH + 2 * HA)
                    pe.wait_ge(sq_ready, h + 1)
                    pe.matmul(kv[:, h, 0:C], ones, osq[:, h], start=True, stop=True).then_inc(ms_full, 1)

            @block.gpsimd
            def _(pool):
                for h in range(HA):
                    if h >= 2:
                        pool.wait_ge(kv_full, NCH + 2 * (h - 1))
                    pool.tensor_tensor(vexp[0:96, h % 2], vtok[0:96, 2, h:h + 1, :].to_broadcast([96, NS, P]),
                                       seq9[0:96, 0:NS].unsqueeze(2).to_broadcast([96, NS, P]), ALU.mult) \
                        .then_inc(vexp_ready, 1)

            @block.vector
            def _(dve):
                for c in range(NCH):
                    dve.wait_ge(kv_full, c + 1)
                    kvc = kv[:, c % 4, :].rearrange("p (h e) -> p h e", h=HA)
                    if c == 0:
                        ins = dve.tensor_copy(sts[:, 0], kvc)
                    else:
                        dve.wait_ge(st_ready, c)
                        for h in range(HA):
                            ins = dve.scalar_tensor_tensor(out=sts[:, c, h], in0=sts[:, c - 1, h], scalar=f32c[:, h, c:c + 1],
                                                           in1=kvc[:, h], op0=ALU.mult, op1=ALU.add)
                    ins.then_inc(st_ready, 1)
                    dve.wait_ge(st_ready, c + 1)
                    dve.sem_inc(kv_free, 1)
                dve.wait_ge(hs_in, 16)
                for h in range(HA):
                    for g in range(2):
                        n = NCH + 2 * h + g
                        dve.wait_ge(kv_full, n + 1)
                        for s in range(4):
                            ins = dve.scalar_tensor_tensor(out=stn[:, 4 * g + s, h], in0=sth[:, 4 * g + s, h],
                                                           scalar=f8[:, h, 4 * g + s:4 * g + s + 1],
                                                           in1=kv[:, n % 4, P * s:P * s + P], op0=ALU.mult, op1=ALU.add)
                        ins.then_inc(st_ready, 1)
                        dve.wait_ge(st_ready, n + 1)
                        dve.sem_inc(kv_free, 1)
                link = linker(dve, dv4)
                for h in range(HA):
                    dve.wait_ge(rt_h, h + 1)
                    link(dve.reciprocal(rsh[:, 1, h], rsh[:, 0, h]))
                    link(dve.scalar_tensor_tensor(out=rsh[:, 0, h], in0=po[:, h, 0:C], scalar=col("hgrn_norm", h),
                                                  in1=rsh[:, 1, h], op0=ALU.mult, op1=ALU.mult))
                    link(dve.tensor_tensor(mixT[:, h], rsh[:, 0, h], zoT[:, h], ALU.mult))

            @block.scalar
            def _(act):
                for h in range(HA):
                    act.wait_ge(o_full, h + 1)
                    act.activation(osq[:, h], po[:, h, 0:C], ACT.Square).then_inc(sq_ready, 1)
                for h in range(HA):
                    act.wait_ge(ms_full, h + 1)
                    act.activation(rsh[:, 0, h], kv[:, h, 0:C], ACT.Sqrt, bias=epsc[:, 0:1], scale=1.0 / P).then_inc(rt_h, 1)
        ps4.free()
        s_mem.free()
        h_mem.free()
        za_mem.free()
        CEXP = float(np.exp(-0.5))
        y_mem = Mem()
        gT = y_mem.sb("gT", [P, 4, C])
        bonusT = y_mem.sb("bonusT", [P, 4, C])
        ARx = y_mem.sb("ARx", [P, 4, 4, C])
        Bt = y_mem.sb("Bt", [P, 4, C])
        Kt = y_mem.sb("Kt", [P, 4, C])
        pinc = y_mem.sb("pinc", [P, 4, C])
        vr = y_mem.sb("vr", [P, 3, 512])
        bk = y_mem.sb("bk", [P, 2, 5, 512])
        w5 = Mem()
        zm = w5.sb("zm", [P, FB, C])
        lora = w5.sb("lora", [P, 2, 512])
        aT = w5.sb("aT", [P, 4, C])
        Lw = w5.sb("Lw", [P, 4, C])
        cum = w5.sb("cum", [P, 4, C])
        tmpa = w5.sb("tmpa", [P, 4, C])
        kkn = w5.sb("kkn", [P, 4, C])
        k7 = w5.sb("k7", [P, 4, C])
        ex = w5.sb("ex", [P, 4, C])
        At = w5.sb("At", [P, 4, C])
        Bh, Kh = aT, Lw
        sh_out = w5.sb("sh_out", [P, FB, 1 + NS])
        ps5 = Mem()
        psl = ps5.ps("psl", [P, 8, 512])
        lora_in, shout, zm_done, tanh_done, lo_full, lo_used, dv5, kk_sq, kk_full, kk_rt, cum_done, to_exp, exps, zeroed, \
            rk_ready, rk_full, tok_src, tok_full, tok_free, sh_done = (
                sem(n) for n in ("lora_in", "shout", "zm_done", "tanh_done", "lo_full", "lo_used", "dv5", "kk_sq",
                                 "kk_full", "kk_rt", "cum_done", "to_exp", "exps", "zeroed", "rk_ready", "rk_full", "tok_src",
                                 "tok_full", "tok_free", "sh_done"))
        order = [12, 13, 4, 5, 6, 7, 0, 1, 2, 3, 8, 9, 10, 11]
        samp = lambda a: a[:, :, 289:361].rearrange("p f (s l) -> p f s l", l=9)
        zs8 = lambda a: a[:, :, SAMP0:C].rearrange("p f (s l) -> p f s l", l=8)
        with nc.Block() as block:
            @block.sync
            def _(sp):
                sp.dma_start(lora[:], inp["lora"].rearrange("p (a f) -> p a f", a=2)).then_inc(lora_in, 16)
                sp.wait_ge(sh_done, 2)
                sp.dma_start(out["shift"], sh_out[:]).then_inc(shout, 16)
                sp.wait_ge(shout, 16)

            @block.gpsimd
            def _(pool):
                pool.memset(ARx[64:128, :, 0::2], 0.0).then_inc(zeroed, 1)
                pool.wait_ge(zeroed, 1)
                pool.memset(ARx[0:64, :, 1::2], 0.0).then_inc(zeroed, 1)
                pool.wait_ge(zeroed, 2)
                pool.memset(bk[:], 0.0).then_inc(zeroed, 1)
                pool.memset(vr[:], 0.0).then_inc(zeroed, 1)
                pool.tensor_copy(sh_out[:, :, 0:1], zbT[:, :, PROMPT:PROMPT + 1]).then_inc(sh_done, 1)
                pool.tensor_copy(sh_out[:, :, 1:1 + NS], samp(zbT)[:, :, :, 8]).then_inc(sh_done, 1)

            @block.tensor
            def _(pe):
                pe.wait_ge(lora_in, 16)
                pe.wait_ge(tanh_done, 1)
                pe.wait_ge(zm_done, 1)
                for i in range(4):
                    pe.matmul(psl[:, i, 0:C], lora[0:64, 0, P * i:P * i + P], zm[0:64, 12], start=True, stop=True)
                    pe.matmul(psl[:, 4 + i, 0:C], lora[64:128, 0, P * i:P * i + P], zm[64:128, 12],
                              start=True, stop=True).then_inc(lo_full, 1)
                pe.wait_ge(tanh_done, 2)
                for i in range(4):
                    pe.wait_ge(lo_used, i + 1)
                    pe.matmul(psl[:, i, 0:C], lora[:, 1, P * i:P * i + P], zm[:, 13], start=True,
                              stop=True).then_inc(lo_full, 1)
                pe.wait_ge(lo_used, 4)
                for i in range(4):
                    pe.wait_ge(kk_sq, 1)
                    pe.matmul(psl[:, 4 + i, 0:C], masks[:, M_B64], tmpa[:, i], start=True, stop=True).then_inc(kk_full, 1)
                pe.wait_ge(lo_used, 8)
                for i in range(4):
                    pe.wait_ge(rk_ready, 1)
                    pe.matmul(psl[:, i, 0:C], masks[:, M_B64], ex[:, i], start=True, stop=True).then_inc(rk_full, 1)
                for n in range(9):
                    what, i = divmod(n, 3)
                    if what == 0:
                        pe.wait_ge(zm_done, FB)
                    else:
                        pe.wait_ge(tok_src, what)
                    if n >= 2:
                        pe.wait_ge(tok_free, n - 1)
                    else:
                        pe.wait_ge(kk_rt, 4)
                    src = zm[:, 8:12] if what == 0 else (Bh, Kh)[what - 1]
                    for j in range(4):
                        ins = pe.transpose(psl[0:TW[i], 4 + n % 2, P * j:P * j + P], src[:, j, P * i:P * i + TW[i]], ident[:])
                    ins.then_inc(tok_full, 1)

            @block.scalar
            def _(act):
                act.wait_ge(zm_done, 1)
                act.activation(zm[0:64, 12], zm[0:64, 12], ACT.Tanh).then_inc(tanh_done, 1)
                act.wait_ge(zm_done, 2)
                act.activation(zm[:, 13], zm[:, 13], ACT.Sigmoid).then_inc(tanh_done, 1)
                for i in range(4):
                    act.wait_ge(lo_full, i + 1)
                    act.activation(Lw[:, i], psl[:, i, 0:C], ACT.Sigmoid, bias=col("w0", i))
                    act.activation(aT[:, i], psl[:, 4 + i, 0:C], ACT.Sigmoid, bias=col("a0", i)).then_inc(lo_used, 1)
                for i in range(4):
                    act.wait_ge(lo_full, 5 + i)
                    act.activation(gT[:, i], psl[:, i, 0:C], ACT.Copy).then_inc(lo_used, 1)
                for i in range(4):
                    act.wait_ge(kk_full, i + 1)
                    act.activation(ex[:, i], psl[:, 4 + i, 0:C], ACT.Sqrt).then_inc(kk_rt, 1)
                act.wait_ge(cum_done, 1)
                act.activation(pinc[:], cum[:], ACT.Exp).then_inc(exps, 1)
                act.activation(Bt[:], cum[:], ACT.Exp, scale=-1.0).then_inc(exps, 1)
                act.wait_ge(to_exp, 1)
                act.activation(At[:], At[:], ACT.Exp).then_inc(exps, 1)
                act.wait_ge(to_exp, 2)
                act.activation(Kt[:], Kt[:], ACT.Exp).then_inc(exps, 1)
                act.wait_ge(zeroed, 4)
                for n in range(9):
                    what, i = divmod(n, 3)
                    act.wait_ge(tok_full, n + 1)
                    src = psl[:, 4 + n % 2, :]
                    if what == 0:
                        ins = act.activation(vr[0:TW[i], i], src[0:TW[i]], ACT.Copy)
                    elif i == 2:
                        ins = act.activation(bk[0:96, what - 1, 4], src[0:96], ACT.Copy)
                    else:
                        act.activation(bk[0:64, what - 1, 2 * i], src[0:64], ACT.Copy)
                        ins = act.activation(bk[64:128, what - 1, 2 * i + 1], src[64:128], ACT.Copy)
                    ins.then_inc(tok_free, 1)

            @block.vector
            def _(dve):
                link = linker(dve, dv5)
                dve.tensor_tensor(zm[:, :, 0:SAMP0], zbT[:, :, 0:288], zbT[:, :, 1:289], ALU.subtract)
                for s in range(NS):
                    ins = dve.tensor_tensor(zm[:, :, SAMP0 + 8 * s:SAMP0 + 8 * s + 8], samp(zbT)[:, :, s, 0:8],
                                            samp(zbT)[:, :, s, 1:9], ALU.subtract)
                link(ins)
                for f in order:
                    dve.scalar_tensor_tensor(out=zm[:, f, 0:SAMP0], in0=zm[:, f, 0:SAMP0], scalar=col("mu", f),
                                             in1=zbT[:, f, 1:289], op0=ALU.mult, op1=ALU.add)
                    dve.scalar_tensor_tensor(out=zs8(zm)[:, f], in0=zs8(zm)[:, f], scalar=col("mu", f),
                                             in1=samp(zbT)[:, f, :, 1:9], op0=ALU.mult, op1=ALU.add).then_inc(zm_done, 1)
                dve.wait_ge(zm_done, FB)
                r, k, v = zm[:, 0:4], zm[:, 4:8], zm[:, 8:12]
                for i in range(4):
                    ins = dve.tensor_scalar(kkn[:, i], k[:, i], col("k_k", i), None, ALU.mult)
                link(ins)
                dve.tensor_tensor(tmpa[:], kkn[:], kkn[:], ALU.mult).then_inc(kk_sq, 1)
                dve.wait_ge(lo_used, 4)
                link(dve.tensor_scalar(Lw[:], Lw[:], -CEXP, None, ALU.mult))
                for i in range(4):
                    ins = dve.tensor_tensor_scan(cum[:, i], restart, Lw[:, i], 0.0, ALU.mult, ALU.add)
                ins.then_inc(cum_done, 1)
                dve.wait_ge(cum_done, 1)
                link(dve.tensor_tensor(At[:], cum[:], Lw[:], ALU.subtract))
                dve.sem_inc(to_exp, 1)
                pc = lambda a: a[:, :, 0:256].rearrange("p f (c j) -> p f c j", j=64)
                pe2 = lambda a: a[:, :, 256:288].rearrange("p f (c j) -> p f c j", j=16)
                dve.tensor_tensor(pc(Kt), pc(cum)[:, :, :, 63:64].to_broadcast([P, 4, 4, 64]), pc(cum), ALU.subtract)
                dve.tensor_tensor(pe2(Kt), pe2(cum)[:, :, :, 15:16].to_broadcast([P, 4, 2, 16]), pe2(cum), ALU.subtract)
                dve.tensor_tensor(zs8(Kt), zs8(cum)[:, :, :, 7:8].to_broadcast([P, 4, NS, 8]), zs8(cum),
                                  ALU.subtract).then_inc(to_exp, 1)
                for i in range(4):
                    ins = dve.tensor_scalar(k7[:, i], aT[:, i], -1.0, col("k_a", i), ALU.add, ALU.mult)
                link(ins)
                link(dve.scalar_tensor_tensor(out=k7[:], in0=k7[:], scalar=1.0, in1=k, op0=ALU.add, op1=ALU.mult))
                dve.wait_ge(kk_rt, 4)
                link(dve.tensor_scalar(tmpa[:], ex[:], 1e-12, None, ALU.max))
                link(dve.reciprocal(tmpa[:], tmpa[:]))
                link(dve.tensor_tensor(kkn[:], kkn[:], tmpa[:], ALU.mult))
                link(dve.tensor_tensor(tmpa[:], kkn[:], aT[:], ALU.mult))
                for i in range(4):
                    ins = dve.scalar_tensor_tensor(out=ex[:, i], in0=r[:, i], scalar=col("r_k", i), in1=k7[:, i],
                                                   op0=ALU.mult, op1=ALU.mult)
                ins.then_inc(rk_ready, 1)
                dve.wait_ge(exps, 4)
                dve.tensor_tensor(Bh[:], tmpa[:], Kt[:], ALU.mult).then_inc(tok_src, 1)
                dve.tensor_tensor(Kh[:], k7[:], Kt[:], ALU.mult).then_inc(tok_src, 1)
                dve.wait_ge(tok_src, 2)
                dve.wait_ge(zeroed, 2)
                for g in range(2):
                    half = slice(64 * g, 64 * g + 64)
                    dve.scalar_tensor_tensor(out=ARx[half, :, g], in0=At[half], scalar=-1.0, in1=kkn[half],
                                             op0=ALU.mult, op1=ALU.mult)
                    dve.tensor_tensor(ARx[half, :, 2 + g], zm[half, 0:4], pinc[half], ALU.mult)
                link(dve.tensor_tensor(Kt[:], k7[:], Bt[:], ALU.mult))
                dve.tensor_tensor(Bt[:], tmpa[:], Bt[:], ALU.mult)
                for i in range(4):
                    dve.wait_ge(rk_full, i + 1)
                    dve.tensor_tensor(bonusT[:, i], psl[:, i, 0:C], v[:, i], ALU.mult)
        ps5.free()
        w5.free()
        m6 = Mem()
        TT = m6.sb("TT", [P, 3, HB, P])
        Aak = m6.sb("Aak", [P, 3, HB, P])
        Arb = m6.sb("Arb", [P, 3, HB, P])
        Ark = m6.sb("Ark", [P, 3, HB, P])
        t6 = Mem()
        pwt = t6.sb("pwt", [P, HB, P])
        pw = t6.sb("pw", [P, HB, P])
        qwt = t6.sb("qwt", [P, HB, P])
        qw = t6.sb("qw", [P, HB, P])
        Et = t6.sb("Et", [P, HB, P])
        ps6 = Mem()
        pb6 = ps6.ps("pb6", [P, 8, 4, P])
        sc_full, sc_free, mm_full, by_act, by_dve, tt_first = (
            sem(n) for n in ("sc_full", "sc_free", "mm_full", "by_act", "by_dve", "tt_first"))
        def solve_steps(i):
            s = [("N2", pwt, pw, qwt, "a"), ("N2t", pw, pwt, qw, "a"), ("R1", qwt, "TT", "TT", "d"),
                 ("N4", qw, qwt, pw, "a"), ("N4t", qwt, qw, pwt, "a"), ("R2", pw, "TT", "TT", "d"),
                 ("N8", pwt, pw, qwt, "a"), ("R3", qwt, "TT", "TT", "d")]
            if i < 2:
                s += [("R", "TT", "ident", qw, "a"), ("F", Et, qw, pwt, "a"), ("Ft", qw, Et, pw, "a"),
                      ("Z1", pwt, "TT", "TT", "d"), ("F2", pw, pwt, qwt, "a"), ("Z2", qwt, "TT", "TT", "d")]
            return s
        reads = {"N2": [], "N2t": [], "R1": ["N2"], "N4": ["N2", "N2t"], "N4t": ["N2", "N2t"], "R2": ["N4", "R1"],
                 "N8": ["N4", "N4t"], "R3": ["N8", "R2"], "R": ["R3"], "F": ["R"], "Ft": ["R"], "Z1": ["F", "R3"],
                 "F2": ["F", "Ft"], "Z2": ["F2", "Z1"]}
        ops = [(i, q) + step for i in range(3) for step in solve_steps(i) for q in range(2)]
        taken = {}
        n_by = {"a": 0, "d": 0}
        for i, q, name, _, _, _, who in ops:
            n_by[who] += 1
            taken[i, q, name] = (by_act if who == "a" else by_dve, n_by[who])
        order6 = [(i, q, name) for i, q, name, *_ in ops]
        NSC = 10
        with nc.Block() as block:
            @block.tensor
            def _(pe):
                for i in range(3):
                    w, cs = TW[i], slice(P * i, P * i + TW[i])
                    first = order6.index((i, 0, "N2"))
                    for n in range(NSC):
                        if i and n < 8:
                            for q in range(2):
                                pe.wait_ge(*taken[i - 1, q, "Z2"])
                                pe.wait_ge(*taken[i - 1, q, "F2"])
                        if n >= 8:
                            pe.wait_ge(sc_free, NSC * i + n - 7)
                        bank = pb6[:, n % 8]
                        if n < 8:
                            j, kind = divmod(n, 2)
                            lhs = (Bt, Kt)[kind]
                            ins = pe.matmul(bank[0:w, :, 0:w], lhs[:, j, cs], ARx[:, j, :, cs], start=True, stop=True)
                        else:
                            for m in range(4):
                                h = 4 * (n - 8) + m
                                ins = pe.matmul(bank[0:w, m, 0:w], ARx[:, h // 2, h % 2, cs], Bt[:, h // 2, cs],
                                                start=True, stop=True)
                        ins.then_inc(sc_full, 1)
                    for n, (_, q, name, lhs, rhs, dst, who) in enumerate(o for o in ops if o[0] == i):
                        if n < 8:
                            pe.wait_ge(sc_free, NSC * (i + 1))
                        else:
                            pe.wait_ge(*taken[order6[first + n - 8]])
                        for r in reads[name]:
                            pe.wait_ge(*taken[i, q, r])
                        if name == "R1":
                            pe.wait_ge(tt_first, i + 1)
                        for m in range(4):
                            h = 4 * q + m
                            pick = lambda a: TT[0:w, i, h, 0:w] if a == "TT" else ident[0:w, 0:w] if a == "ident" \
                                else a[0:w, h, 0:w]
                            if name == "R":
                                ins = pe.transpose(pb6[0:w, n % 8, m, 0:w], pick(lhs), pick(rhs))
                            else:
                                ins = pe.matmul(pb6[0:w, n % 8, m, 0:w], pick(lhs), pick(rhs), start=True, stop=True)
                        ins.then_inc(mm_full, 1)

            @block.vector
            def _(dve):
                dn = 0
                for i in range(3):
                    w = TW[i]
                    first = order6.index((i, 0, "N2"))
                    msk = lambda m, k: masks[0:w, m:m + 1, 0:w].to_broadcast([w, k, w])
                    if i:
                        dve.wait_ge(mm_full, first)
                    bu, bl, su, iu = (M_BU, M_BL, M_SU, M_IU) if i < 2 else (M_TBU, M_TBL, M_TBU, M_TIU)
                    for n in range(NSC):
                        dve.wait_ge(sc_full, NSC * i + n + 1)
                        bank = pb6[0:w, n % 8, :, 0:w]
                        j, kind = divmod(n, 2)
                        hs = slice(2 * j, 2 * j + 2)
                        if n >= 8:
                            ins = dve.tensor_tensor(pw[0:w, 4 * n - 32:4 * n - 28, 0:w], bank, msk(bl, 4), ALU.mult)
                        elif kind == 0:
                            dve.tensor_tensor(pwt[0:w, hs, 0:w], bank[:, 0:2], msk(bu, 2), ALU.mult)
                            if i < 2:
                                dve.tensor_tensor(Et[0:w, hs, 0:w], bank[:, 0:2], msk(M_EU, 2), ALU.mult)
                            ins = dve.tensor_tensor(Arb[0:w, i, hs, 0:w], bank[:, 2:4], msk(iu, 2), ALU.mult)
                        else:
                            dve.tensor_tensor(Aak[0:w, i, hs, 0:w], bank[:, 0:2], msk(su, 2), ALU.mult)
                            ins = dve.tensor_tensor(Ark[0:w, i, hs, 0:w], bank[:, 2:4], msk(iu, 2), ALU.mult)
                        ins.then_inc(sc_free, 1)
                    dve.wait_ge(sc_free, NSC * (i + 1))
                    dve.tensor_tensor(TT[0:w, i, :, 0:w], pwt[0:w, :, 0:w], msk(M_ID, HB), ALU.add).then_inc(tt_first, 1)
                    dve.wait_ge(tt_first, i + 1)
                    for n, (_, q, name, lhs, rhs, dst, who) in enumerate(o for o in ops if o[0] == i):
                        if who == "d":
                            dve.wait_ge(mm_full, first + n + 1)
                            if dn >= 2:
                                dve.wait_ge(by_dve, dn - 1)
                            acc = TT[0:w, i, 4 * q:4 * q + 4, 0:w]
                            dve.tensor_tensor(acc, acc, pb6[0:w, n % 8, :, 0:w], ALU.add).then_inc(by_dve, 1)
                            dn += 1

            @block.scalar
            def _(act):
                for i in range(3):
                    w = TW[i]
                    first = order6.index((i, 0, "N2"))
                    for n, (_, q, name, lhs, rhs, dst, who) in enumerate(o for o in ops if o[0] == i):
                        if who == "a":
                            act.wait_ge(mm_full, first + n + 1)
                            if name == "N4t":
                                act.wait_ge(tt_first, i + 1)
                            act.activation(dst[0:w, 4 * q:4 * q + 4, 0:w], pb6[0:w, n % 8, :, 0:w], ACT.Copy) \
                                .then_inc(by_act, 1)
        ps6.free()
        t6.free()

        m7 = Mem()
        st = m7.sb("st", [P, 2, 4, HN])
        std = m7.sb("std", [P, 4, HN])
        xb = m7.sb("xb", [P, 512])
        ub = m7.sb("ub", [P, 512])
        ss = m7.sb("ss", [P, 4, NS, HN])
        xm = m7.sb("xm", [P, NS, HN])
        xs = m7.sb("xs", [P, HB, HN])
        uv = zbT[:].rearrange("p f c -> p (f c)")[:, 0:36 * HN].rearrange("p (a b s v) -> p a b s v", a=2, b=2, s=9)
        yT = mixT[:, 4:8]
        ps7 = Mem()
        psX = ps7.ps("psX", [P, 512])
        psU = ps7.ps("psU", [P, 512])
        psSt = ps7.ps("psSt", [P, 512])
        psY = ps7.ps("psY", [P, 512])
        ps2 = ps7.ps("ps2", [P, 4, 512])
        (rs_in, z7, x_full, x_ready, u_full, u_ready, st_full, st_done, std_done, y_full, y_taken, x0_full, x0_free,
         xs_ready, spread, spread_used, ns_full, ns_free, rst_out, spread_u, ns_mul) = (sem(n) for n in (
             "rs_in", "z7", "x_full", "x_ready", "u_full", "u_ready", "st_full", "st_done", "std_done", "y_full",
             "y_taken", "x0_full", "x0_free", "xs_ready", "spread", "spread_used", "ns_full", "ns_free", "rst_out",
             "spread_u", "ns_mul"))
        hv = lambda h: slice(HN * h, HN * h + HN)
        with nc.Block() as block:
            @block.sync
            def _(sp):
                sp.dma_start(ss[:], inp["state_r"]).then_inc(rs_in, 16)
                sp.wait_ge(st_done, 5)
                sp.dma_start(out["rwkv_p"], st[:, 0]).then_inc(rst_out, 16)
                sp.wait_ge(ns_free, 4)
                sp.dma_start(out["rwkv_s"], ss[:]).then_inc(rst_out, 16)
                sp.wait_ge(rst_out, 32)

            @block.gpsimd
            def _(pool):
                pool.memset(xb[:], 0.0).then_inc(z7, 1)
                pool.memset(ub[:], 0.0).then_inc(z7, 1)
                for h in range(HB):
                    if h >= 2:
                        pool.wait_ge(spread_used, h - 1)
                    pool.tensor_tensor(uv[0:96, h % 2, 1], vr[0:96, 2, hv(h)].unsqueeze(1).to_broadcast([96, 9, HN]),
                                       seq9[0:96].unsqueeze(2).to_broadcast([96, 9, HN]), ALU.mult).then_inc(spread, 1)

            @block.tensor
            def _(pe):
                pe.wait_ge(z7, 2)
                for c in range(4):
                    i, pb, col0 = c // 2, 64 * (c % 2), 64 * c
                    rows, ts = slice(pb, pb + 64), slice(64 * c, 64 * c + 64)
                    tl = slice(pb, pb + 64)
                    if c:
                        pe.wait_ge(st_done, c)
                        pe.wait_ge(x_ready, c)
                    for h in range(HB):
                        j, g = divmod(h, 2)
                        ins = pe.matmul(psX[rows, hv(h)], Aak[:, i, h, tl], vr[:, i, hv(h)], start=True, stop=c == 0,
                                        skip_group_check=True)
                        if c:
                            ins = pe.matmul(psX[rows, hv(h)], ARx[:, j, g, ts], st[:, (c - 1) % 2, j], start=False, stop=True,
                                      skip_group_check=True)
                    ins.then_inc(x_full, 1)
                    pe.wait_ge(x_ready, c + 1)
                    if c:
                        pe.wait_ge(u_ready, c)
                    for h in range(HB):
                        ins = pe.matmul(psU[rows, hv(h)], TT[:, i, h, tl], xb[:, hv(h)], start=True, stop=True)
                    ins.then_inc(u_full, 1)
                    pe.wait_ge(u_ready, c + 1)
                    for h in range(HB):
                        j, g = divmod(h, 2)
                        o = psSt[64 * g:64 * g + 64, hv(j)]
                        pe.matmul(o, bk[:, 0, c, hv(h)], ub[:, hv(h)], start=True, stop=False)
                        ins = pe.matmul(o, bk[:, 1, c, hv(h)], vr[:, i, hv(h)], start=False, stop=True)
                    ins.then_inc(st_full, 1)
                    if c:
                        pe.wait_ge(y_taken, c)
                    for h in range(HB):
                        j, g = divmod(h, 2)
                        o = psY[64 * g:64 * g + 64, hv(j)]
                        pe.matmul(o, ub[:, hv(h)], Arb[:, i, h, tl], start=True, stop=False)
                        ins = pe.matmul(o, vr[:, i, hv(h)], Ark[:, i, h, tl], start=False, stop=c == 0)
                        if c:
                            ins = pe.matmul(o, st[:, (c - 1) % 2, j], ARx[:, j, 2 + g, ts], start=False, stop=True)
                    ins.then_inc(y_full, 1)
                t2c = slice(256, C)
                pe.wait_ge(rs_in, 16)
                for h in range(HB):
                    j, g = divmod(h, 2)
                    if h >= 4:
                        pe.wait_ge(x0_free, h - 3)
                    pe.matmul(ps2[0:96, h % 4, :], ARx[:, j, g, t2c], ss[:, j].rearrange("p s v -> p (s v)"),
                              start=True, stop=True).then_inc(x0_full, 1)
                pe.wait_ge(st_done, 4)
                pe.wait_ge(u_ready, 4)
                for h in range(HB):
                    j, g = divmod(h, 2)
                    pe.matmul(psX[0:96, hv(h)], ARx[:, j, g, t2c], st[:, 1, j], start=True, stop=True)
                    ins = pe.matmul(psU[0:96, hv(h)], Aak[0:96, 2, h, 0:96], vr[0:96, 2, hv(h)], start=True, stop=True)
                ins.then_inc(x_full, 1)
                pe.wait_ge(x_ready, 5)
                for h in range(HB):
                    ins = pe.matmul(psU[0:96, hv(h)], TT[0:96, 2, h, 0:96], xb[0:96, hv(h)], start=True, stop=True)
                ins.then_inc(u_full, 1)
                pe.wait_ge(u_ready, 5)
                pe.wait_ge(y_taken, 4)
                yb = psY[:, 0:384].rearrange("p (j t) -> p j t", j=4)
                for h in range(HB):
                    j, g = divmod(h, 2)
                    o = yb[64 * g:64 * g + 64, j]
                    pe.matmul(o, ub[0:96, hv(h)], Arb[0:96, 2, h, 0:96], start=j == 0, stop=False, skip_group_check=True)
                    pe.matmul(o, vr[0:96, 2, hv(h)], Ark[0:96, 2, h, 0:96], start=False, stop=False, skip_group_check=True)
                    pe.matmul(o[:, 0:16], st[:, 1, j], ARx[:, j, 2 + g, 256:272], start=False, stop=False,
                              skip_group_check=True)
                    for s in range(NS):
                        t = 32 + 8 * s
                        ins = pe.matmul(o[:, t:t + 8], ss[:, j, s], ARx[:, j, 2 + g, 256 + t:264 + t], start=False,
                                        stop=s == NS - 1, skip_group_check=True)
                ins.then_inc(y_full, 1)
                pe.wait_ge(x0_free, 8)
                for h in range(HB):
                    j, g = divmod(h, 2)
                    pe.wait_ge(spread, h + 1)
                    pe.wait_ge(spread_u, h + 1)
                    lhs = [bk[0:96, k, 4, hv(h)] for k in range(2)]
                    half = slice(64 * g, 64 * g + 64)
                    for k in range(2):
                        pe.matmul(ps2[half, j, :], lhs[k], uv[0:96, h % 2, k, 0:8].rearrange("p s v -> p (s v)"),
                                  start=k == 0, stop=k == 1)
                    for k in range(2):
                        ins = pe.matmul(psSt[half, hv(j)], lhs[k], uv[0:96, h % 2, k, 8], start=k == 0, stop=k == 1)
                    ins.then_inc(spread_used, 1)

            @block.vector
            def _(dve):
                pend = lambda c: pinc[:, :, c:c + 1].to_broadcast([P, 4, HN])
                for c in range(4):
                    pb = 64 * (c % 2)
                    dve.wait_ge(x_full, c + 1)
                    if c == 0:
                        dve.wait_ge(z7, 2)
                    dve.tensor_copy(xb[pb:pb + 64], psX[pb:pb + 64]).then_inc(x_ready, 1)
                    if c:
                        dve.tensor_tensor(std[:], st[:, (c - 1) % 2], pend(64 * c + 63), ALU.mult).then_inc(std_done, 1)
                        dve.wait_ge(std_done, c)
                    dve.wait_ge(st_full, c + 1)
                    src = psSt[:, 0:256].rearrange("p (j v) -> p j v", j=4)
                    if c:
                        dve.tensor_tensor(st[:, c % 2], src, std[:], ALU.add).then_inc(st_done, 1)
                    else:
                        dve.tensor_copy(st[:, 0], src).then_inc(st_done, 1)
                dve.wait_ge(st_done, 4)
                for h in range(HB):
                    dve.wait_ge(x0_full, h + 1)
                    if h:
                        dve.wait_ge(xs_ready, h)
                    dve.tensor_tensor(xm[0:96], ps2[0:96, h % 4, :].rearrange("p (s v) -> p s v", s=NS),
                                      seq9[0:96, 0:8].unsqueeze(2).to_broadcast([96, NS, HN]), ALU.mult).then_inc(x0_free, 1)
                    dve.wait_ge(x0_free, h + 1)
                    dve.tensor_reduce(xs[0:96, h], xm[0:96].rearrange("p s v -> p v s"), AX, ALU.add).then_inc(xs_ready, 1)
                dve.wait_ge(xs_ready, 8)
                dve.wait_ge(x_full, 5)
                xsf = xs[0:96].rearrange("p h v -> p (h v)")
                dve.scalar_tensor_tensor(out=xsf, in0=psX[0:96], scalar=seq9[0:96, 8:9], in1=xsf, op0=ALU.mult,
                                         op1=ALU.add).then_inc(xs_ready, 1)
                dve.wait_ge(xs_ready, 9)
                dve.tensor_tensor(xb[0:96], psU[0:96], xsf, ALU.add).then_inc(x_ready, 1)
                dve.wait_ge(u_ready, 5)
                for h in range(HB):
                    if h >= 2:
                        dve.wait_ge(spread_used, h - 1)
                    dve.tensor_tensor(uv[0:96, h % 2, 0], ub[0:96, hv(h)].unsqueeze(1).to_broadcast([96, 9, HN]),
                                      seq9[0:96].unsqueeze(2).to_broadcast([96, 9, HN]), ALU.mult).then_inc(spread_u, 1)
                dve.wait_ge(y_full, 5)
                for j in range(4):
                    last = pinc[:, j, SAMP0:C].rearrange("p (s l) -> p s l", l=8)[:, :, 7:8]
                    dve.tensor_tensor(ss[:, j], ss[:, j], last.to_broadcast([P, NS, HN]), ALU.mult).then_inc(ns_mul, 1)
                dve.tensor_tensor(std[:], st[:, 1], pend(PROMPT - 1), ALU.mult).then_inc(ns_mul, 1)
                dve.wait_ge(ns_mul, 5)
                for j in range(4):
                    dve.wait_ge(spread_used, 2 * j + 2)
                    dve.tensor_tensor(ss[:, j], ss[:, j], ps2[:, j, :].rearrange("p (s v) -> p s v", s=NS),
                                      ALU.add).then_inc(ns_free, 1)
                dve.tensor_tensor(st[:, 0], psSt[:, 0:256].rearrange("p (j v) -> p j v", j=4), std[:],
                                  ALU.add).then_inc(st_done, 1)

            @block.scalar
            def _(act):
                for c in range(4):
                    pb = 64 * (c % 2)
                    act.wait_ge(u_full, c + 1)
                    act.activation(ub[pb:pb + 64], psU[pb:pb + 64], ACT.Copy).then_inc(u_ready, 1)
                    act.wait_ge(y_full, c + 1)
                    act.activation(yT[:, :, 64 * c:64 * c + 64], psY[:, 0:256].rearrange("p (j t) -> p j t", j=4),
                                   ACT.Copy).then_inc(y_taken, 1)
                act.wait_ge(u_full, 5)
                act.activation(ub[0:96], psU[0:96], ACT.Copy).then_inc(u_ready, 1)
                act.wait_ge(y_full, 5)
                act.activation(yT[:, :, 256:C], psY[:, 0:384].rearrange("p (j t) -> p j t", j=4), ACT.Copy).then_inc(y_taken, 1)
        ps7.free()

        yc, ysq, sd = Bt, Kt, pinc
        ps8 = Mem()
        pmu = ps8.ps("pmu", [P, 4, 512])
        pvar = ps8.ps("pvar", [P, 4, 512])
        mu_full, c_ready, ysq_ready, var_full, sd_ready, dv8 = (
            sem(n) for n in ("mu_full", "c_ready", "ysq_ready", "var_full", "sd_ready", "dv8"))
        with nc.Block() as block:
            @block.tensor
            def _(pe):
                for j in range(4):
                    pe.matmul(pmu[:, j, 0:C], masks[:, M_B64], yT[:, j], start=True, stop=True).then_inc(mu_full, 1)
                for j in range(4):
                    pe.wait_ge(ysq_ready, j + 1)
                    pe.matmul(pvar[:, j, 0:C], masks[:, M_B64], ysq[:, j], start=True, stop=True).then_inc(var_full, 1)

            @block.scalar
            def _(act):
                for j in range(4):
                    act.wait_ge(c_ready, j + 1)
                    act.activation(ysq[:, j], yc[:, j], ACT.Square).then_inc(ysq_ready, 1)
                for j in range(4):
                    act.wait_ge(var_full, j + 1)
                    act.activation(sd[:, j], pvar[:, j, 0:C], ACT.Sqrt, bias=epsc[:, 1:2], scale=1.0 / HN).then_inc(sd_ready, 1)

            @block.vector
            def _(dve):
                link = linker(dve, dv8)
                for j in range(4):
                    dve.wait_ge(mu_full, j + 1)
                    dve.scalar_tensor_tensor(out=yc[:, j], in0=pmu[:, j, 0:C], scalar=-1.0 / HN, in1=yT[:, j],
                                             op0=ALU.mult, op1=ALU.add).then_inc(c_ready, 1)
                dve.wait_ge(c_ready, 4)
                for j in range(4):
                    dve.wait_ge(sd_ready, j + 1)
                    link(dve.reciprocal(sd[:, j], sd[:, j]))
                    link(dve.tensor_tensor(yc[:, j], yc[:, j], sd[:, j], ALU.mult))
                    link(dve.tensor_scalar(yc[:, j], yc[:, j], col("ln_w", j), col("ln_b", j), ALU.mult, ALU.add))
                    link(dve.tensor_tensor(yc[:, j], yc[:, j], bonusT[:, j], ALU.add))
                    link(dve.tensor_tensor(mixT[:, 4 + j], yc[:, j], gT[:, j], ALU.mult))
        ps8.free()
        m7.free()
        m6.free()
        y_mem.free()
        zb_mem.free()
        m9 = Mem()
        wo = m9.sb("wo", [P, 8, D])
        x1 = m9.sb("x1", [P, 3, D])
        sq9 = m9.sb("sq9", [P, D])
        rs9 = m9.sb("rs9", [P, 16])
        ps9 = Mem()
        pmix = ps9.ps("pmix", [P, 6, 512])
        ptr = ps9.ps("ptr", [P, 2, 4, P])
        x1_in, wo_in, mix_full, x1_ready, sq9d, rt9, rc9, rn9, tr9_full, tr9_free, x1_saved, xh_done = (
            sem(n) for n in ("x1_in", "wo_in", "mix_full", "x1_ready", "sq9d", "rt9", "rc9", "rn9", "tr9_full", "tr9_free",
                             "x1_saved", "xh_done"))
        KEEP = [[(META, P, 0)], [(0, P, P - META)], [(0, 16, 240), (32, 96, 256)]]
        with nc.Block() as block:
            @block.sync
            def _(sp):
                sp.dma_start(wo[:], inp["w_out"]).then_inc(wo_in, 16)
                sp.dma_start(x1[:], inp["x_rows"].rearrange("k p d -> p k d")).then_inc(x1_in, 16)
                for i in range(3):
                    sp.wait_ge(x1_ready, i + 1)
                    for a, b, c0 in KEEP[i]:
                        sp.dma_start(x1_dram[c0:c0 + b - a], x1[a:b, i]).then_inc(x1_saved, 16)
                sp.wait_ge(x1_saved, 64)

            @block.tensor
            def _(pe):
                pe.wait_ge(wo_in, 16)
                for i in range(3):
                    for g in range(2):
                        for f in range(8):
                            ins = pe.matmul(pmix[0:TW[i], 2 * i + g], mixT[:, f, P * i:P * i + TW[i]],
                                            wo[:, f, 512 * g:512 * g + 512], start=f == 0, stop=f == 7)
                    ins.then_inc(mix_full, 1)
                for n in range(3 * KD):
                    i, j = divmod(n, KD)
                    if j == 0:
                        pe.wait_ge(rn9, i + 1)
                    if n % 4 == 0 and n >= 8:
                        pe.wait_ge(tr9_free, n // 4 - 1)
                    w = TW[i]
                    ins = pe.transpose(ptr[:, n // 4 % 2, n % 4, 0:w], x1[0:w, i, P * j:P * j + P], ident[0:w, 0:w])
                    if n % 4 == 3:
                        ins.then_inc(tr9_full, 1)

            @block.scalar
            def _(act):
                for i in range(3):
                    act.wait_ge(x1_ready, i + 1)
                    if i:
                        act.wait_ge(sq9d, i)
                    w = TW[i]
                    act.activation(sq9[0:w], x1[0:w, i], ACT.Square, accum_out=rs9[0:w, i:i + 1]).then_inc(sq9d, 1)
                    act.wait_ge(sq9d, i + 1)
                    act.activation(rs9[0:w, 3 + i:4 + i], rs9[0:w, i:i + 1], ACT.Sqrt, bias=epsc[0:w, 0:1],
                                   scale=1.0 / D).then_inc(rt9, 1)

            @block.vector
            def _(dve):
                dve.wait_ge(x1_in, 16)
                for i in range(3):
                    dve.wait_ge(mix_full, i + 1)
                    w = TW[i]
                    dve.tensor_tensor(x1[0:w, i], x1[0:w, i], pmix[0:w, 2 * i:2 * i + 2].rearrange("p a b -> p (a b)"),
                                      ALU.add).then_inc(x1_ready, 1)
                dve.wait_ge(x1_saved, 64)
                for i in range(3):
                    w = TW[i]
                    dve.wait_ge(rt9, i + 1)
                    dve.reciprocal(rs9[0:w, 6 + i:7 + i], rs9[0:w, 3 + i:4 + i]).then_inc(rc9, 1)
                dve.wait_ge(rc9, 3)
                for i in range(3):
                    w = TW[i]
                    dve.tensor_scalar(x1[0:w, i], x1[0:w, i], rs9[0:w, 6 + i:7 + i], None, ALU.mult).then_inc(rn9, 1)
                for n in range(3 * KD):
                    i, j = divmod(n, KD)
                    if n % 4 == 0:
                        dve.wait_ge(tr9_full, n // 4 + 1)
                    for a, b, c0 in KEEP[i]:
                        ins = dve.tensor_scalar(xh[:, j, c0:c0 + b - a], ptr[:, n // 4 % 2, n % 4, a:b],
                                                col("norm2", j), None, ALU.mult)
                    if n % 4 == 3:
                        ins.then_inc(xh_done, 1)
                        dve.wait_ge(xh_done, n // 4 + 1)
                        for m in range(n - 3, n + 1):
                            for a, b, c0 in KEEP[i]:
                                ins = dve.scalar_tensor_tensor(out=xl[:, m % KD, c0:c0 + b - a],
                                                               in0=ptr[:, m // 4 % 2, m % 4, a:b], scalar=col("norm2", m % KD),
                                                               in1=xh[:, m % KD, c0:c0 + b - a], op0=ALU.mult,
                                                               op1=ALU.subtract)
                        ins.then_inc(tr9_free, 1)
        ps9.free()
        m9.free()
        mix_mem.free()
        mask_mem.free()

        NQ, NA = 16, 48
        NG = NBLK - NA
        assert 4 * NG == NT and NA % 2 == 0
        big_mem = Mem()
        hid = big_mem.sb("hid", [P, NBLK, NT])
        hflat = hid[:].rearrange("p b t -> p (b t)")
        ring = Mem()
        raw = [ring.sb(f"raw{r}", [P, 2, 256]) for r in range(4)]
        hi = [ring.sb(f"hi{u}", [P, 2, P], F32R) for u in range(4)]
        lo = [ring.sb(f"lo{u}", [P, 2, P], F32R) for u in range(4)]
        wide = lambda a: a[:].rearrange("p k n -> p (k n)")
        RT = ring.sb("RT", [P, 3, NT])
        act_h = [ring.sb(f"act_h{q}", [P, NT]) for q in range(2)]
        oh1 = [ring.sb(f"oh1_{s}", [P, 2, NK]) for s in range(2)]
        oh2 = [ring.sb(f"oh2_{s}", [P, 2, NK]) for s in range(2)]
        at = [(NBLK * NT)]

        def scratch(*shape):
            n = int(np.prod(shape))
            at[0] -= n
            names_ = "abcd"[:len(shape)]
            flat = hflat[:, at[0]:at[0] + n]
            if len(shape) == 1:
                return flat
            return flat.rearrange(f"p ({' '.join(names_)}) -> p {' '.join(names_)}", **dict(zip(names_, shape)))

        sc = scratch(3, NQ, NK)
        qpT = scratch(2, NT)
        keysT = scratch(2, NK)
        top = scratch(16, TOPK)
        topi = scratch(16, TOPK).bitcast(U32)
        topf = scratch(16, TOPK)
        cand = scratch(PH, TOPK, TOPK)
        best = scratch(3, PH, TOPK)
        flat = scratch(PH, TOPK).bitcast(U32)
        rank = scratch(2, PH, TOPK).bitcast(U32)
        rankf = scratch(2, PH, TOPK)
        pick = scratch(2, PH, TOPK, TOPK)
        picked = scratch(3, 3, P)
        gsum = scratch(2, PH)
        CLEAN = NA * NT
        DIRTY = at[0]
        assert DIRTY > CLEAN
        ps10 = Mem()
        ph = ps10.ps("ph", [P, 2, 512])
        pss = ps10.ps("pss", [P, 2, 4, P])
        ptp = ps10.ps("ptp", [P, 4, P])
        pg = ps10.ps("pg", [P, 2, 4, NK])
        t_in = [sem(f"t_in{r}") for r in range(4)]
        (keys_in, t_hi, lo_dve, lo_pool, t_mm, q_ready, s_full, s_ready, dv10, e_in, e_out, pk_ready, pt_full, rt_ready,
         ones_set, ones_set_dve, h_done, g_done, h_used, oh_ready, g_mm, g_used) = (sem(n) for n in (
             "keys_in", "t_hi", "lo_dve", "lo_pool", "t_mm", "q_ready", "s_full", "s_ready", "dv10", "e_in", "e_out",
             "pk_ready", "pt_full", "rt_ready", "ones_set", "ones_set_dve", "h_done", "g_done", "h_used", "oh_ready", "g_mm", "g_used"))
        NEG = -3.0e38
        QU = 4 * NQ
        with nc.Block() as block:
            @block.sync
            def _(sp):
                sp.dma_start(keysT, inp["keysT"]).then_inc(keys_in, 16)
                for n in range(2 * NQ):
                    if n >= 4:
                        sp.wait_ge(lo_dve, 2 * (n - 3))
                    sp.dma_start(wide(raw[n % 4]), inp["w_q"][n // 2, :, 4 * (n % 2):4 * (n % 2) + 4, :]
                                 .rearrange("p k n -> p (k n)")).then_inc(t_in[n % 4], 16)

                def block_half(b, r):
                    src = inp["uT"][bass.ds(b, 1), :, 4 * (r % 2):4 * (r % 2) + 4, :]
                    sp.dma_start(wide(raw[r]), src.rearrange("b p k n -> p (b k n)")).then_inc(t_in[r], 16)

                for r in range(4):
                    sp.wait_ge(lo_dve, QU - 6 + 2 * r)
                    block_half(r // 2, r)
                with sp.Fori(1, NA // 2) as i:
                    for r in range(4):
                        sp.wait_ge(lo_pool, 8 * i + (2 * r - 6))
                        block_half(2 * i + r // 2, r)
                for r in range(4):
                    sp.wait_ge(lo_pool, 4 * NA - 6 + 2 * r)
                    block_half(NA + r // 2, r)
                with sp.Fori(1, NG // 2) as i:
                    for r in range(4):
                        sp.wait_ge(t_mm, QU + 4 * NA + 8 * i + (2 * r - 6))
                        block_half(2 * i + (NA + r // 2), r)

            @block.gpsimd
            def _(pool):
                pool.memset(hflat[:, CLEAN:DIRTY], 1.0).then_inc(ones_set, 1)

                def low(u, n):
                    pool.wait_ge(t_hi, n)
                    pool.tensor_tensor(wide(lo[u % 4]), raw[u // 2][:, u % 2], wide(hi[u % 4]),
                                       ALU.subtract).then_inc(lo_pool, 1)
                with pool.Fori(0, NA // 2) as i:
                    for u in range(8):
                        low(u, QU + 8 * i + (u + 1))
                pool.wait_ge(rt_ready, 3)
                pool.memset(hflat[:, DIRTY:DIRTY + (NBLK * NT - DIRTY) // 2], 1.0).then_inc(ones_set, 1)
                with pool.Fori(0, NG // 2) as i:
                    for u in range(1, 8, 2):
                        low(u, QU + 4 * NA + 8 * i + (u + 1))

            @block.scalar
            def _(act):
                def high(u, landed, n, reuse=True):
                    if u % 2 == 0:
                        act.wait_ge(t_in[u // 2], landed)
                    if reuse:
                        act.wait_ge(t_mm, n - 3)
                    act.activation(wide(hi[u % 4]), raw[u // 2][:, u % 2], ACT.Copy).then_inc(t_hi, 1)

                for n in range(NQ + 1):
                    if n < NQ:
                        for u in range(4):
                            m = 4 * n + u
                            high(m % 8, 16 * (n // 2 + 1), m, m >= 4)
                    if n >= 1:
                        m = n - 1
                        act.wait_ge(t_mm, 4 * n)
                        if m >= 2:
                            act.wait_ge(s_full, m - 1)
                        act.activation(qpT[:, m % 2], ph[:, m % 2, 0:NT], ACT.Copy).then_inc(q_ready, 1)
                    if n >= 2:
                        m = n - 2
                        act.wait_ge(s_full, m + 1)
                        act.activation(sc[:, 0:2, m], pss[:, m % 2, 0:2], ACT.Copy)
                        act.activation(sc[0:64, 2, m], pss[0:64, m % 2, 2], ACT.Copy).then_inc(s_ready, 1)
                m = NQ - 1
                act.wait_ge(s_full, m + 1)
                act.activation(sc[:, 0:2, m], pss[:, m % 2, 0:2], ACT.Copy)
                act.activation(sc[0:64, 2, m], pss[0:64, m % 2, 2], ACT.Copy).then_inc(s_ready, 1)

                def gelu(b, q, quarters):
                    act.wait_ge(t_mm, quarters)
                    act.activation(hid[:, bass.ds(b, 1), :].rearrange("p b t -> p (b t)"), ph[:, q, 0:NT],
                                   ACT.Gelu).then_inc(h_done, 1)

                def step_a(i, first):
                    for u in range(8):
                        high(u, 16 * (NQ // 2 + 1) + 16 * i, QU + 8 * i + u)
                        if u == 1 and not first:
                            gelu(2 * i - 1, 1, QU + 8 * i)
                        if u == 5:
                            gelu(2 * i, 0, QU + 8 * i + 4)
                step_a(0, True)
                with act.Fori(1, NA // 2) as i:
                    step_a(i, False)
                gelu(NA - 1, 1, QU + 4 * NA)
                act.wait_ge(e_in, 3)
                act.activation(best, best, ACT.Exp).then_inc(e_out, 1)

                def gelu_b(q, quarters, used):
                    act.wait_ge(t_mm, quarters)
                    if used is not None:
                        act.wait_ge(h_used, used)
                    act.activation(act_h[q][:], ph[:, q, 0:NT], ACT.Gelu).then_inc(g_done, 1)

                def step_b(i, first, second):
                    q0 = QU + 4 * NA
                    for u in range(8):
                        high(u, 16 * (NQ // 2 + 1 + NA // 2) + 16 * i, q0 + 8 * i + u)
                        if u == 1 and not first:
                            gelu_b(1, q0 + 8 * i, None if second else 2 * i - 2)
                        if u == 5:
                            gelu_b(0, q0 + 8 * i + 4, None if first else 2 * i - 1)
                step_b(0, True, False)
                step_b(1, False, True)
                with act.Fori(2, NG // 2) as i:
                    step_b(i, False, False)
                gelu_b(1, QU + 4 * NBLK, NG - 2)

            @block.tensor
            def _(pe):
                def quarter(o, u, sub):
                    s = u % 4
                    for k in range(2):
                        c = 2 * sub + k
                        begin, end = c == 0, c == KD - 1
                        pe.matmul(o, hi[s][:, k], xh[:, c], start=begin, stop=False)
                        pe.matmul(o, hi[s][:, k], xl[:, c], start=False, stop=False)
                        ins = pe.matmul(o, lo[s][:, k], xh[:, c], start=False, stop=end)
                    ins.then_inc(t_mm, 1)

                for n in range(NQ + 1):
                    if n < NQ:
                        if n >= 2:
                            pe.wait_ge(q_ready, n - 1)
                        for u in range(4):
                            pe.wait_ge(lo_dve, 4 * n + u + 1)
                            quarter(ph[:, n % 2, 0:NT], u, u)
                    if n:
                        m = n - 1
                        if m == 0:
                            pe.wait_ge(keys_in, 16)
                        pe.wait_ge(q_ready, m + 1)
                        if m >= 2:
                            pe.wait_ge(s_ready, m - 1)
                        for i, (c0, w) in enumerate(PT):
                            ins = pe.matmul(pss[0:w, m % 2, i], qpT[:, m % 2, c0:c0 + w], keysT[:, m % 2], start=True,
                                            stop=True)
                        ins.then_inc(s_full, 1)

                def step_a(i, first):
                    for u in range(8):
                        if u % 4 == 0 and not first:
                            pe.wait_ge(h_done, 2 * i + (u // 4 - 1))
                        pe.wait_ge(lo_pool, 8 * i + (u + 1))
                        quarter(ph[:, u // 4, 0:NT], u, u % 4)
                step_a(0, True)
                with pe.Fori(1, NA // 2) as i:
                    step_a(i, False)
                pe.wait_ge(pk_ready, 3)
                for i, (c0, w) in enumerate(PT):
                    if i:
                        pe.wait_ge(rt_ready, i)
                    for k in range(3):
                        ins = pe.transpose(ptp[:, k, 0:w], picked[0:w, i, k], ident[0:w, 0:w])
                    ins.then_inc(pt_full, 1)

                def step_b(i, first):
                    for q in range(2):
                        if not first:
                            pe.wait_ge(g_used, 2 * i + (q - 1))
                        for s in range(2):
                            pe.wait_ge(oh_ready, 4 * i + (2 * q + s + 1))
                            for t in range(2):
                                ins = pe.matmul(pg[:, q, 2 * s + t], oh2[s][:, t], oh1[s][:, t], start=True, stop=True)
                            ins.then_inc(g_mm, 1)
                        if first:
                            pe.wait_ge(h_done, NA - 1 + q)
                        else:
                            pe.wait_ge(g_done, 2 * i + (q - 1))
                        for u in range(4):
                            if u % 2 == 0:
                                pe.wait_ge(lo_dve, QU + 4 * i + (2 * q + u // 2 + 1))
                            else:
                                pe.wait_ge(lo_pool, 4 * NA + 4 * i + (2 * q + u // 2 + 1))
                            quarter(ph[:, q, 0:NT], u, u)
                step_b(0, True)
                with pe.Fori(1, NG // 2) as i:
                    step_b(i, False)

            @block.vector
            def _(dve):
                link = linker(dve, dv10)

                def low(u, n):
                    dve.wait_ge(t_hi, n)
                    dve.tensor_tensor(wide(lo[u % 4]), raw[u // 2][:, u % 2], wide(hi[u % 4]),
                                      ALU.subtract).then_inc(lo_dve, 1)
                for n in range(QU):
                    low(n % 8, n + 1)
                dve.wait_ge(s_ready, NQ)

                def top16(values, index, source, groups):
                    for half in range(2):
                        e = slice(8 * half, 8 * half + 8)
                        for g in range(groups):
                            ins = dve.max(values(g)[:, e], source(g))
                        link(ins)
                        for g in range(groups):
                            ins = dve.max_index(index(g)[:, e], values(g)[:, e], source(g))
                        link(ins)
                        if half == 0:
                            for g in range(groups):
                                ins = dve.match_replace(out=source(g), in_to_replace=values(g)[:, e], in_values=source(g),
                                                        imm_value=NEG)
                            link(ins)

                dve.memset(best, 0.0).then_inc(ones_set_dve, 1)
                dve.wait_ge(ones_set_dve, 1)
                for i, (c0, w) in enumerate(PT):
                    top16(lambda g: top[0:w, g], lambda g: topi[0:w, g], lambda g: sc[0:w, i, g], 16)
                    dve.tensor_copy(topf[0:w], topi[0:w])
                    pairs = top[0:w].rearrange("p (h a) k -> p h a k", a=2)
                    link(dve.tensor_tensor(cand[0:w], pairs[:, :, 0, :].unsqueeze(3).to_broadcast([w, PH, TOPK, TOPK]),
                                           pairs[:, :, 1, :].unsqueeze(2).to_broadcast([w, PH, TOPK, TOPK]), ALU.add))
                    top16(lambda g: best[0:w, i, g], lambda g: flat[0:w, g],
                          lambda g: cand[0:w, g].rearrange("p a b -> p (a b)"), PH)
                    link(dve.tensor_copy(gsum[0:w, 0], best[0:w, i, :, 0]))
                    dve.tensor_tensor(best[0:w, i], best[0:w, i], gsum[0:w, 0].unsqueeze(2).to_broadcast([w, PH, TOPK]),
                                      ALU.subtract).then_inc(e_in, 1)
                    dve.tensor_single_scalar(rank[0:w, 0], flat[0:w], 4, ALU.logical_shift_right)
                    link(dve.tensor_single_scalar(rank[0:w, 1], flat[0:w], TOPK - 1, ALU.bitwise_and))
                    link(dve.tensor_copy(rankf[0:w], rank[0:w]))
                    keys = lambda a: topf[0:w].rearrange("p (h a) k -> p h a k", a=2)[:, :, a, :].unsqueeze(2)
                    four = [w, PH, TOPK, TOPK]
                    for a in range(2):
                        ins = dve.tensor_tensor(pick[0:w, a], rankf[0:w, a].unsqueeze(3).to_broadcast(four),
                                                iota[0:w, 0:TOPK].unsqueeze(1).unsqueeze(1).to_broadcast(four), ALU.is_equal)
                    link(ins)
                    for a in range(2):
                        ins = dve.tensor_tensor(pick[0:w, a], pick[0:w, a], keys(a).to_broadcast(four), ALU.mult)
                    link(ins)
                    for a in range(2):
                        ins = dve.tensor_reduce(picked[0:w, i, a].rearrange("p (h k) -> p h k", h=PH), pick[0:w, a], AX, ALU.add)
                    link(ins)
                for i, (c0, w) in enumerate(PT):
                    if i == 0:
                        dve.wait_ge(e_out, 1)
                    link(dve.tensor_reduce(gsum[0:w, 0], best[0:w, i], AX, ALU.add))
                    link(dve.reciprocal(gsum[0:w, 1], gsum[0:w, 0]))
                    dve.tensor_tensor(picked[0:w, i, 2].rearrange("p (h k) -> p h k", h=PH), best[0:w, i],
                                      gsum[0:w, 1].unsqueeze(2).to_broadcast([w, PH, TOPK]), ALU.mult).then_inc(pk_ready, 1)
                for i, (c0, w) in enumerate(PT):
                    dve.wait_ge(pt_full, i + 1)
                    dve.tensor_copy(RT[:, :, c0:c0 + w], ptp[:, 0:3, 0:w]).then_inc(rt_ready, 1)
                dve.wait_ge(rt_ready, 3)
                dve.memset(hflat[:, DIRTY + (NBLK * NT - DIRTY) // 2:], 1.0).then_inc(ones_set_dve, 1)
                dve.wait_ge(ones_set_dve, 2)
                dve.wait_ge(ones_set, 2)
                dve.wait_ge(h_done, NA)

                def times_gates(t0, q, group):
                    dve.wait_ge(g_mm, group)
                    h = hid[:, :, bass.ds(t0, 4)]
                    dve.tensor_tensor(h, h, pg[:, q].rearrange("p t k -> p k t"), ALU.mult).then_inc(g_used, 1)

                def times_hidden(b, q, done):
                    dve.wait_ge(g_done, done)
                    h = hid[:, bass.ds(b, 1), :].rearrange("p b t -> p (b t)")
                    dve.tensor_tensor(h, h, act_h[q][:], ALU.mult).then_inc(h_used, 1)

                def step_b(i, first):
                    for q in range(2):
                        none = first and q == 0
                        for s in range(2):
                            if not none:
                                dve.wait_ge(g_mm, 4 * i + (2 * q + s - 1))
                            t0 = 8 * i + (4 * q + 2 * s)
                            for t in range(2):
                                dve.tensor_scalar(oh1[s][:, t], iota[:], RT[:, 0, bass.ds(t0 + t, 1)],
                                                  RT[:, 2, bass.ds(t0 + t, 1)], ALU.is_equal, ALU.mult)
                            dve.tensor_tensor(oh2[s][:], iota[:].unsqueeze(1).to_broadcast([P, 2, NK]),
                                              RT[:, 1, bass.ds(t0, 2)].unsqueeze(2).to_broadcast([P, 2, NK]),
                                              ALU.is_equal).then_inc(oh_ready, 1)
                        low(4 * q, QU + 4 * NA + 8 * i + (4 * q + 1))
                        if not none:
                            if not (first and q == 1):
                                dve.wait_ge(h_used, 2 * i + (q - 1))
                            times_gates(8 * i + (4 * q - 4), 1 - q, 4 * i + 2 * q)
                        low(4 * q + 2, QU + 4 * NA + 8 * i + (4 * q + 3))
                        if not none:
                            dve.wait_ge(g_used, 2 * i + q)
                            times_hidden(2 * i + (NA + q - 1), 1 - q, 2 * i + q)
                step_b(0, True)
                with dve.Fori(1, NG // 2) as i:
                    step_b(i, False)
                dve.wait_ge(h_used, NG - 1)
                times_gates(NT - 4, 1, 2 * NG)
                dve.wait_ge(g_used, NG)
                times_hidden(NBLK - 1, 1, NG)
        ps10.free()
        ring.free()
        STEPS = NBLK // 2

        ring = Mem()
        raw = [ring.sb(f"raw{u}", [P, 512]) for u in range(4)]
        hi = [ring.sb(f"hi{u}", [P, 4, P], F32R) for u in range(4)]
        lo = [ring.sb(f"lo{u}", [P, 4, P], F32R) for u in range(4)]
        ch = [xh[:, s] for s in range(2)]
        cl = [xl[:, s] for s in range(2)]
        ps13 = Mem()
        acc = ps13.ps("acc", [P, KD, 512])
        v_in = [sem(f"v_in{u}") for u in range(4)]
        v_hi, v_lo, v_mm, c_hi, c_lo = (sem(n) for n in ("v_hi", "v_lo", "v_mm", "c_hi", "c_lo"))
        with nc.Block() as block:
            @block.sync
            def _(sp):
                def step(i, first):
                    for u in range(4):
                        if not first:
                            sp.wait_ge(v_lo, 4 * i + (u - 3))
                        src = inp["v"][bass.ds(2 * i + u // 2, 1), :, 512 * (u % 2):512 * (u % 2) + 512]
                        sp.dma_start(raw[u][:], src.rearrange("b p n -> p (b n)")).then_inc(v_in[u], 16)
                step(0, True)
                with sp.Fori(1, STEPS) as i:
                    step(i, False)

            @block.scalar
            def _(act):
                def step(i, first):
                    for u in range(4):
                        act.wait_ge(v_in[u], 16 * i + 16)
                        if not first:
                            act.wait_ge(v_mm, 4 * i + (u - 2 if u % 2 == 0 else u - 3))
                        if u % 2 == 0:
                            act.activation(ch[u // 2], hid[:, bass.ds(2 * i + u // 2, 1), :].rearrange("p b t -> p (b t)"),
                                           ACT.Copy).then_inc(c_hi, 1)
                        act.activation(wide(hi[u]), raw[u][:], ACT.Copy).then_inc(v_hi, 1)
                step(0, True)
                with act.Fori(1, STEPS) as i:
                    step(i, False)

            @block.vector
            def _(dve):
                def step(i):
                    for u in range(4):
                        if u % 2 == 0:
                            dve.wait_ge(c_hi, 2 * i + (u // 2 + 1))
                            dve.tensor_tensor(cl[u // 2], hid[:, bass.ds(2 * i + u // 2, 1), :].rearrange("p b t -> p (b t)"),
                                              ch[u // 2], ALU.subtract).then_inc(c_lo, 1)
                        dve.wait_ge(v_hi, 4 * i + (u + 1))
                        dve.tensor_tensor(wide(lo[u]), raw[u][:], wide(hi[u]), ALU.subtract).then_inc(v_lo, 1)
                with dve.Fori(0, STEPS) as i:
                    step(i)

            @block.tensor
            def _(pe):
                def step(i, first, last):
                    for u in range(4):
                        if u % 2 == 0:
                            pe.wait_ge(c_lo, 2 * i + (u // 2 + 1))
                        pe.wait_ge(v_lo, 4 * i + (u + 1))
                        begin, end = first and u < 2, last and u >= 2
                        for k in range(4):
                            o, s = acc[:, 4 * (u % 2) + k, 0:NT], u // 2
                            pe.matmul(o, hi[u][:, k], ch[s], start=begin, stop=False)
                            pe.matmul(o, hi[u][:, k], cl[s], start=False, stop=False)
                            ins = pe.matmul(o, lo[u][:, k], ch[s], start=False, stop=end)
                        ins.then_inc(v_mm, 1)
                step(0, True, False)
                with pe.Fori(1, STEPS - 1) as i:
                    step(i, False, False)
                step(STEPS - 1, False, True)
        ring.free()
        big_mem.free()

        m14 = Mem()
        oT = m14.sb("oT", [P, KD, NT])
        x2 = m14.sb("x2", [P, 3, D])
        nf = m14.sb("nf", [P, D])
        sq14 = m14.sb("sq14", [P, D])
        rs14 = m14.sb("rs14", [P, 16])
        x2_in, o_taken, y_full14, y_sum, sq14d, rt14, dv14, y_done, y_out = (
            sem(n) for n in ("x2_in", "o_taken", "y_full14", "y_sum", "sq14d", "rt14", "dv14", "y_done", "y_out"))
        with nc.Block() as block:
            @block.sync
            def _(sp):
                for i, (c0, w) in enumerate(PT):
                    sp.dma_start(x2[0:w, i], x1_dram[c0:c0 + w]).then_inc(x2_in, 16)
                sp.dma_start(nf[:], inp["norm_f"].to_broadcast([P, D])).then_inc(x2_in, 16)
                for i, (c0, w) in enumerate(PT):
                    sp.wait_ge(y_done, i + 1)
                    sp.dma_start(out["y"][c0:c0 + w], x2[0:w, i]).then_inc(y_out, 16)
                sp.wait_ge(y_out, 48)

            @block.scalar
            def _(act):
                for j in range(KD):
                    act.activation(oT[:, j], acc[:, j, 0:NT], ACT.Copy).then_inc(o_taken, 1)
                for i, (c0, w) in enumerate(PT):
                    act.wait_ge(y_sum, i + 1)
                    if i:
                        act.wait_ge(sq14d, i)
                    act.activation(sq14[0:w], x2[0:w, i], ACT.Square, accum_out=rs14[0:w, i:i + 1]).then_inc(sq14d, 1)
                    act.wait_ge(sq14d, i + 1)
                    act.activation(rs14[0:w, 3 + i:4 + i], rs14[0:w, i:i + 1], ACT.Sqrt, bias=epsc[0:w, 0:1],
                                   scale=1.0 / D).then_inc(rt14, 1)

            @block.tensor
            def _(pe):
                pe.wait_ge(o_taken, KD)
                for i, (c0, w) in enumerate(PT):
                    for j in range(KD):
                        ins = pe.transpose(acc[0:w, 2 * i + j // 4, P * (j % 4):P * (j % 4) + P], oT[:, j, c0:c0 + w], ident[:])
                    ins.then_inc(y_full14, 1)

            @block.vector
            def _(dve):
                link = linker(dve, dv14)
                dve.wait_ge(x2_in, 64)
                for i, (c0, w) in enumerate(PT):
                    dve.wait_ge(y_full14, i + 1)
                    dve.tensor_tensor(x2[0:w, i], x2[0:w, i], acc[0:w, 2 * i:2 * i + 2].rearrange("p a b -> p (a b)"),
                                      ALU.add).then_inc(y_sum, 1)
                for i, (c0, w) in enumerate(PT):
                    dve.wait_ge(rt14, i + 1)
                    link(dve.reciprocal(rs14[0:w, 6 + i:7 + i], rs14[0:w, 3 + i:4 + i]))
                    dve.scalar_tensor_tensor(out=x2[0:w, i], in0=x2[0:w, i], scalar=rs14[0:w, 6 + i:7 + i], in1=nf[0:w],
                                             op0=ALU.mult, op1=ALU.mult).then_inc(y_done, 1)
        ps13.free()
        m14.free()
        base.free()


_LAYOUT = [("norm1", 8), ("norm2", 8), ("theta0", 4), ("theta1", 4), ("hgrn_norm", 4), ("mu", FB), ("w0", 4),
           ("a0", 4), ("k_k", 4), ("k_a", 4), ("r_k", 4), ("ln_w", 4), ("ln_b", 4)]
FEAT, NFEAT = {}, 0
for _name, _n in _LAYOUT:
    FEAT[_name] = NFEAT
    NFEAT += _n

_OUTS = {
    "y": (NT, D),
    "hgrn_p": (P, HA, P),
    "hgrn_s": (P, NS, HA, P),
    "rwkv_p": (P, 4, HN),
    "rwkv_s": (P, 4, NS, HN),
    "shift": (P, FB, 1 + NS),
}


def layout(inputs):
    a = {k: np.asarray(v) for k, v in inputs.items()}
    f32 = np.float32
    rows = np.concatenate([a["meta_tokens"], a["x_prompt"][0], np.zeros((SAMP0 - PROMPT, D), f32),
                           a["x_sample"].reshape(-1, D), np.zeros((3 * P - C, D), f32)])
    w_in = a["w_in"][0].reshape(KD, P, 30, P).transpose(2, 1, 0, 3)
    cols = lambda v: v.reshape(-1, P).T
    parts = {"norm1": a["norm1"][0], "norm2": a["norm2"][0], "theta0": a["lb_theta"][0], "theta1": a["lb_theta"][1],
             "hgrn_norm": a["hgrn_norm"][0], "mu": a["mu_shift"][0], "w0": a["w0"][0], "a0": a["a0"][0],
             "k_k": a["k_k"][0], "k_a": a["k_a"][0], "r_k": a["r_k"][0], "ln_w": a["ln_w"][0], "ln_b": a["ln_b"][0]}
    masks, misc = shape_constants()
    wq = a["peer_wq"][0].reshape(KD, P, 16, P).transpose(2, 1, 0, 3)
    out = {
        "x_rows": rows.reshape(3, P, D),
        "masks": masks,
        "misc": misc,
        "feat": np.concatenate([cols(parts[n]) for n, _ in _LAYOUT], axis=1),
        "w_zi": a["w_in"][0][:, 1024:1536].reshape(KD, P, 512).transpose(1, 0, 2),
        "w_tiles": np.concatenate([w_in[0:8], w_in[12:16], w_in[16:30]]),
        "shift0": a["state_shift"][0].reshape(NS, FB, P).transpose(2, 1, 0),
        "state_h": a["state_hgrn"][0].transpose(2, 0, 1, 3),
        "state_r": a["state_rwkv"][0].reshape(NS, 4, 2, HN, HN).transpose(2, 4, 1, 0, 3).reshape(P, 4, NS, HN),
        "lora": np.concatenate([np.concatenate([a["w_w2"][0], a["a_w2"][0]], axis=0), a["g_w2"][0]], axis=1),
        "w_out": a["w_out"][0].reshape(8, P, D).transpose(1, 0, 2),
        "w_q": wq,
        "keysT": a["peer_keys"][0].transpose(2, 0, 1),
        "uT": a["peer_u"][0].reshape(NK, NK, KD, P).transpose(0, 3, 2, 1),
        "v": a["peer_v"][0].reshape(NK, NK, D),
        "norm_f": a["norm_f"].reshape(1, D),
    }
    return {k: np.ascontiguousarray(v) for k, v in out.items()}


def kernel(**inputs):
    import concourse.bacc as bacc
    from concourse.bass_utils import run_bass_kernel_spmd

    arrays = layout(inputs)
    nc = bacc.Bacc("TRN2", target_bir_lowering=False, num_devices=1)
    inp = {k: nc.dram_tensor(f"in_{k}", v.shape, mybir.dt.from_np(v.dtype), kind="ExternalInput").ap()
           for k, v in arrays.items()}
    out = {k: nc.dram_tensor(f"out_{k}", s, F32, kind="ExternalOutput").ap() for k, s in _OUTS.items()}
    build_program(nc, inp, out)
    r = run_bass_kernel_spmd(nc, [{f"in_{k}": v for k, v in arrays.items()}], core_ids=[0]).results[0]
    got = {k: np.asarray(r[f"out_{k}"]) for k in _OUTS}
    y = got["y"]
    shift = got["shift"].transpose(2, 1, 0).reshape(1 + NS, FB * P)
    rwkv = lambda s: s.reshape(2, HN, 4, -1, HN).transpose(3, 2, 0, 4, 1).reshape(-1, HB, HN, HN)
    return (np.ascontiguousarray(y[:SEQ][None]),
            np.ascontiguousarray(y[SEQ:NT].reshape(NS, LS, D)),
            np.ascontiguousarray(got["hgrn_p"].transpose(1, 0, 2)[None, None]),
            np.ascontiguousarray(rwkv(got["rwkv_p"][:, :, None])[None]),
            np.ascontiguousarray(shift[None, 0:1]),
            np.ascontiguousarray(got["hgrn_s"].transpose(1, 2, 0, 3)[None]),
            np.ascontiguousarray(rwkv(got["rwkv_s"])[None]),
            np.ascontiguousarray(shift[None, 1:]))
```

```python
from contextlib import ExitStack

import numpy as np

import concourse.bass as bass
from concourse import mybir

ALU = mybir.AluOpType
ACT = mybir.ActivationFunctionType
AX = mybir.AxisListType.X
F32 = mybir.dt.float32
F32R = mybir.dt.float32r
U32 = mybir.dt.uint32

P = 128
D = 1024
KD = D // P
META, SEQ, NS, LS = 16, 256, 8, 8
PROMPT = META + SEQ
SAMP0 = 288
C = SAMP0 + NS * LS
TW = [128, 128, C - 256]
HA, HB, HN = 4, 8, 64
FB = 14
EPS, GN_EPS = 1e-6, 64e-5
NT = SEQ + NS * LS
PT = [(0, 128), (128, 128), (256, 64)]
PH, NK, TOPK = 8, 128, 16
NBLK = NK
NMASK = 12
(M_ID, M_BU, M_BL, M_EU, M_SU, M_IU, M_TBU, M_TBL, M_TIU, M_HI, M_HO, M_B64) = range(NMASK)


def shape_constants():
    s, t = np.arange(P)[:, None], np.arange(P)[None, :]
    blk = lambda n: s // n == t // n
    seq = np.where(np.arange(P) < 16, 100, np.where(np.arange(P) < 32, 101, np.arange(P) // 8))
    same = seq[:, None] == seq[None, :]
    m = np.zeros((P, NMASK, P), np.float32)
    m[:, M_ID] = s == t
    m[:, M_BU] = blk(16) & (s < t)
    m[:, M_BL] = blk(16) & (s > t)
    m[:, M_EU] = blk(64) & ~blk(16) & (s < t)
    m[:, M_SU] = blk(64) & (s < t)
    m[:, M_IU] = blk(64) & (s <= t)
    m[:, M_TBU] = same & (s < t)
    m[:, M_TBL] = same & (s > t)
    m[:, M_TIU] = same & (s <= t)
    m[:, M_HI] = blk(16) & (s <= t)
    m[:, M_HO] = blk(32) & ~blk(16) & (s < t)
    m[:, M_B64] = blk(64)
    col = np.arange(C)
    start = np.where(col < PROMPT, col % 64 == 0, np.where(col < SAMP0, col == PROMPT, col % 8 == 0))
    restart = np.broadcast_to(np.where(start, 0.0, 1.0), (P, C)).astype(np.float32)
    seq9 = np.zeros((P, 9), np.float32)
    seq9[:16, 8] = 1
    for n in range(NS):
        seq9[32 + 8 * n:40 + 8 * n, n] = 1
    one_hot = np.zeros((P, 63), np.float32)
    one_hot[:, 31] = 1
    expand = np.concatenate([s % 32 == t % 16, s % 32 == t % 8 + 8], axis=1).astype(np.float32)
    sum_h, sum_r = np.zeros((2, P, 14), np.float32)
    sum_h[:, 6:8] = 1
    sum_r[:64, 6] = sum_r[64:, 7] = 1
    spread8 = np.zeros((P, 4, P), np.float32)
    for j in range(4):
        spread8[2 * j, j, :64] = spread8[2 * j + 1, j, 64:] = 1
    misc = np.concatenate([restart, seq9, np.broadcast_to(np.arange(P, dtype=np.float32), (P, P)),
                           one_hot, expand, sum_h, sum_r, spread8.reshape(P, 4 * P)], axis=1)
    return m, np.ascontiguousarray(misc.astype(np.float32))


NMISC = C + 9 + P + 63 + 2 * P + 28 + 4 * P


def build_program(nc, inp, out):
    with ExitStack() as whole:
        names = [0]

        def sem(name):
            names[0] += 1
            return whole.enter_context(nc.semaphore(f"{name}_{names[0]}"))

        links = [0]
        dve_chain = sem("dve_chain")

        def linker(eng, s):
            def link(ins):
                links[0] += 1
                ins.then_inc(s, 1)
                eng.wait_ge(s, links[0])
            return link

        class Mem:
            def __init__(self):
                self.ctx = ExitStack()

            def sb(self, name, shape, dt=F32):
                names[0] += 1
                return self.ctx.enter_context(nc.sbuf_tensor(f"{name}_{names[0]}", shape, dt))

            def ps(self, name, shape):
                names[0] += 1
                return self.ctx.enter_context(nc.psum_tensor(f"{name}_{names[0]}", shape, F32))

            def free(self):
                self.ctx.close()

        base = Mem()
        ident = base.sb("identity", [P, P])
        iota = base.sb("iota", [P, P])
        feat = base.sb("feat", [P, NFEAT])
        epsc = base.sb("epsc", [P, 4])
        xh = base.sb("xh", [P, KD, NT], F32R)
        xl = base.sb("xl", [P, KD, NT], F32R)
        mask_mem = Mem()
        masks = mask_mem.sb("masks", [P, NMASK, P])
        misc = mask_mem.sb("misc", [P, NMISC])
        restart = misc[:, 0:C]
        seq9 = misc[:, C:C + 9]
        one_hot = lambda i: misc[:, C + 9 + P + 31 - i:C + 9 + P + 63 - i]
        expand = misc[:, C + 9 + P + 63:C + 9 + P + 63 + 2 * P].rearrange("p (a s) -> p a s", a=2)
        own = C + 9 + P + 63 + 2 * P
        row_sum_h = lambda j: misc[:, own + 6 - 2 * j:own + 14 - 2 * j]
        row_sum_r = lambda j: misc[:, own + 20 - 2 * j:own + 28 - 2 * j]
        spread8 = lambda j: misc[0:8, own + 28 + P * j:own + 28 + P * j + P]
        rows_in, rows_out = sem("rows_in"), sem("rows_out")
        states_in, states_out = sem("states_in"), sem("states_out")
        x1_dram = nc.dram_tensor("x1_scratch", [NT, D], F32).ap()

        def col(name, i=0, n=1):
            return feat[:, FEAT[name] + i:FEAT[name] + i + n]

        mix_mem = Mem()
        mixT = mix_mem.sb("mixT", [P, 8, C])
        zb_mem = Mem()
        zbT = zb_mem.sb("zbT", [P, FB, 289 + 9 * NS])
        zm = zb_mem.sb("zm", [P, FB, C])
        zflat = zm[:].rearrange("p f c -> p (f c)")
        za_mem = Mem()
        qT = za_mem.sb("qT", [P, HA, C])
        fT = za_mem.sb("fT", [P, HA, C])
        kT = za_mem.sb("kT", [P, HA, C])
        zoT = za_mem.sb("zoT", [P, HA, C])
        vtok = za_mem.sb("vtok", [P, 3, HA, P])
        NB = SAMP0 // 16
        h_mem = Mem()
        scT = h_mem.sb("scT", [P, 3, HA, P])
        q2 = h_mem.sb("q2", [P, HA, C])
        k2h = h_mem.sb("k2h", [P, HA, C])
        ktok = h_mem.sb("ktok", [P, 3, HA, P])
        f16 = h_mem.sb("f16", [P, HA, NB])
        f8 = h_mem.sb("f8", [P, HA, NS])
        f32c = h_mem.sb("f32c", [P, HA, NB // 2])
        suf = h_mem.sb("suf", [P, HA, C])
        compact = h_mem.sb("compact", [P, C])
        blocks16 = lambda a: a[:, :, 0:SAMP0].rearrange("p h (c j) -> p h c j", j=16)
        blocks8 = lambda a: a[:, :, SAMP0:C].rearrange("p h (c j) -> p h c j", j=8)
        in_mem = Mem()
        xnh = in_mem.sb("xnh", [P, KD, C], F32R)
        xnl = in_mem.sb("xnl", [P, KD, C], F32R)
        wraw = in_mem.sb("wraw", [P, 4, D])
        whi = in_mem.sb("whi", [P, 2, D], F32R)
        wlo = in_mem.sb("wlo", [P, 2, D], F32R)
        sig = in_mem.sb("sig", [P, 2, 2, C])
        shift0 = in_mem.sb("shift0", [P, FB, NS])
        lbt = in_mem.sb("lbt", [P, 6, HA])
        x = zflat[:, 0:3 * D].rearrange("p (i d) -> p i d", i=3)
        norm_row = zflat[:, 3 * D:4 * D]
        sq = in_mem.sb("sq", [P, D])
        rs = in_mem.sb("rs", [P, 16])
        prod = x[:].rearrange("p i d -> p (i d)")[:, 0:2 * HA * C].rearrange("p (b h t) -> p b h t", b=2, h=HA)
        t2 = Mem()
        pz = t2.ps("pz", [P, 6, 512])
        pst = t2.ps("pst", [P, 2, 4, P])
        tiles = [("q", i) for i in range(4)] + [("f", i) for i in range(4)] + [("o", i) for i in range(4)] + \
                [("b", i) for i in range(FB)]
        NF = len(tiles)
        NZI = 4
        ITEMS = NZI + NF
        NBANK = 6
        STEP0 = 8
        pC = pst[:, 0].rearrange("p a b -> p (a b)")[:, 0:C]
        w_in_slot = [sem(f"w_in_slot{i}") for i in range(4)]
        x_in = [sem(f"x_in{i}") for i in range(3)]
        (norm_in, c_in, m_in, sh_in, sq_done, rt_done, rstd_done, xn_done, tr_full, tr_hi, tr_lo, const_ready,
         w_hi, w_lo, item_done, z_act, z_dve, z_tok, a2, shift_copied, prod_zero, prod_ready, prod_used, suf_done,
         compact_done) = (sem(n) for n in (
             "norm_in", "c_in", "m_in", "sh_in", "sq_done", "rt_done", "rstd_done", "xn_done", "tr_full", "tr_hi",
             "tr_lo", "const_ready", "w_hi", "w_lo", "item_done", "z_act", "z_dve", "z_tok", "a2", "shift_copied",
             "prod_zero", "prod_ready", "prod_used", "suf_done", "compact_done"))
        with nc.Block() as block:
            @block.sync
            def _(sp):
                sp.dma_start(x[:, 0], inp["x_rows"][0]).then_inc(x_in[0], 16)
                sp.dma_start(norm_row, inp["norm1"].to_broadcast([P, D])).then_inc(norm_in, 16)
                sp.dma_start(ident[:], inp["masks"][:, M_ID]).then_inc(c_in, 16)
                sp.dma_start(feat[:], inp["feat"]).then_inc(c_in, 16)
                for i in (1, 2):
                    sp.dma_start(x[:, i], inp["x_rows"][i]).then_inc(x_in[i], 16)
                for n in range(ITEMS):
                    if n >= 4:
                        sp.wait_ge(w_lo, n - 3)
                    sp.dma_start(wraw[:, n % 4], inp["w_in"][n]).then_inc(w_in_slot[n % 4], 16)
                    if n == 3:
                        sp.dma_start(shift0[:], inp["shift0"]).then_inc(sh_in, 16)
                        sp.dma_start(masks[:], inp["masks"]).then_inc(m_in, 16)
                        sp.dma_start(misc[:], inp["misc"]).then_inc(m_in, 16)
                        sp.dma_start(iota[:], inp["misc"][:, C + 9:C + 9 + P]).then_inc(m_in, 16)
                sp.wait_ge(m_in, 48)

            @block.gpsimd
            def _(pool):
                pool.memset(epsc[:, 0:1], EPS).then_inc(const_ready, 1)
                pool.memset(epsc[:, 1:2], GN_EPS).then_inc(const_ready, 1)
                pool.memset(epsc[:, 2:3], 0.0).then_inc(const_ready, 1)
                pool.memset(zbT[:, :, 0:1], 0.0).then_inc(const_ready, 1)
                pool.memset(suf[:], 1.0).then_inc(prod_zero, 1)
                pool.wait_ge(tr_full, 6)
                pool.memset(prod, 0.0).then_inc(prod_zero, 1)
                pool.wait_ge(z_dve, STEP0)
                s16, s8, g16, g8 = blocks16(suf), blocks8(suf), blocks16(fT), blocks8(fT)
                pool.wait_ge(prod_zero, 2)
                for n, i in enumerate(range(14, -1, -1)):
                    if n:
                        pool.wait_ge(suf_done, n)
                    if i < 7:
                        pool.tensor_tensor(s8[:, :, :, i:i + 1], s8[:, :, :, i + 1:i + 2], g8[:, :, :, i + 1:i + 2], ALU.mult)
                    pool.tensor_tensor(s16[:, :, :, i:i + 1], s16[:, :, :, i + 1:i + 2], g16[:, :, :, i + 1:i + 2],
                                       ALU.mult).then_inc(suf_done, 1)
                pool.wait_ge(suf_done, 15)
                pool.tensor_tensor(f16[:], s16[:, :, :, 0], g16[:, :, :, 0], ALU.mult)
                pool.tensor_tensor(f8[:], s8[:, :, :, 0], g8[:, :, :, 0], ALU.mult).then_inc(suf_done, 1)

            @block.tensor
            def _(pe):
                pe.wait_ge(c_in, 32)
                for n in range(6):
                    i, g = divmod(n, 2)
                    if g == 0:
                        pe.wait_ge(xn_done, i + 1)
                    if n >= 2:
                        pe.wait_ge(tr_lo, n - 1)
                    for j in range(4):
                        ins = pe.transpose(pst[:, g, j, :], x[:, i, 512 * g + P * j:512 * g + P * j + P], ident[:])
                    ins.then_inc(tr_full, 1)
                for m in range(NZI):
                    pe.wait_ge(w_hi, m + 1)
                    for a, b in ((xnh, whi), (xnl, whi), (xnh, wlo)):
                        if m == 0 and a is xnl:
                            pe.wait_ge(tr_lo, 6)
                        if b is wlo:
                            pe.wait_ge(w_lo, m + 1)
                        for i in range(3):
                            if m == 0 and a is xnh and b is whi:
                                pe.wait_ge(tr_hi, 2 * i + 2)
                            for k in range(2):
                                ins = pe.matmul(pz[0:TW[i], i, :], a[:, 2 * m + k, P * i:P * i + TW[i]],
                                                b[:, m % 2, 512 * k:512 * k + 512], start=m == 0 and b is whi and a is xnh
                                                and k == 0, stop=m == NZI - 1 and b is wlo and k == 1)
                    ins.then_inc(item_done, 1)
                for n in range(NF):
                    m, bank = NZI + n, (n + 3) % NBANK
                    if n >= NBANK:
                        if n - NBANK < 12:
                            pe.wait_ge(z_dve, n - NBANK + 1)
                        else:
                            pe.wait_ge(z_act, n - NBANK + 1)
                    elif n >= 3:
                        pe.wait_ge(z_tok, n - 2)
                    pe.wait_ge(w_hi, m + 1)
                    for k in range(KD):
                        for a in (xnh, xnl):
                            pe.matmul(pz[:, bank, 0:C], whi[:, m % 2, P * k:P * k + P], a[:, k], start=k == 0 and a is xnh,
                                      stop=False)
                    pe.wait_ge(w_lo, m + 1)
                    for k in range(KD):
                        ins = pe.matmul(pz[:, bank, 0:C], wlo[:, m % 2, P * k:P * k + P], xnh[:, k], start=False,
                                        stop=k == KD - 1)
                    ins.then_inc(item_done, 1)
                    step = n - STEP0 - 2
                    if step >= 0:
                        if step == 0:
                            pe.wait_ge(m_in, 48)
                        pe.wait_ge(prod_ready, step + 1)
                        for h in range(HA):
                            ins = pe.matmul(pC[32 * h:32 * h + 32], one_hot(15 - step), prod[:, step % 2, h],
                                            start=step == 0, stop=step == 15, skip_group_check=True)
                        ins.then_inc(prod_used, 1)

            @block.scalar
            def _(act):
                def high(m):
                    act.wait_ge(w_in_slot[m % 4], 16 * (m // 4 + 1))
                    if m >= 2:
                        act.wait_ge(item_done, m - 1)
                    act.activation(whi[:, m % 2], wraw[:, m % 4], ACT.Copy).then_inc(w_hi, 1)

                def root(i):
                    act.wait_ge(x_in[i], 16)
                    if i:
                        act.wait_ge(sq_done, i)
                    act.activation(sq[:], x[:, i], ACT.Square, accum_out=rs[:, i:i + 1]).then_inc(sq_done, 1)
                    act.wait_ge(sq_done, i + 1)
                    act.activation(rs[:, 3 + i:4 + i], rs[:, i:i + 1], ACT.Sqrt, bias=epsc[:, 0:1], scale=1.0 / D) \
                        .then_inc(rt_done, 1)

                def x_high(i):
                    for g in range(2):
                        act.wait_ge(tr_full, 2 * i + g + 1)
                        act.activation(xnh[:, 4 * g:4 * g + 4, P * i:P * i + TW[i]], pst[:, g, :, 0:TW[i]],
                                       ACT.Copy).then_inc(tr_hi, 1)

                act.wait_ge(const_ready, 4)
                root(0)
                root(1)
                x_high(0)
                root(2)
                x_high(1)
                high(0)
                x_high(2)
                act.wait_ge(a2, 1)
                act.activation(lbt[:, 2:4], lbt[:, 0:2], ACT.Exp).then_inc(a2, 1)
                high(1)
                for m in range(2, ITEMS + 2):
                    if m < ITEMS:
                        high(m)
                    n = m - 2 - NZI
                    if n < 0:
                        continue
                    kind, i = tiles[n]
                    bank = (n + 3) % NBANK
                    act.wait_ge(item_done, NZI + n + 1)
                    if kind in "qfo" and n >= 2:
                        act.wait_ge(z_dve, n - 1)
                    if kind in "qo":
                        act.activation(sig[:, n % 2, 0], pz[:, bank, 0:C], ACT.Sigmoid).then_inc(z_act, 1)
                    elif kind == "f":
                        act.activation(sig[:, n % 2, 0], pz[:, bank, 0:C], ACT.Sigmoid)
                        act.activation(sig[:, n % 2, 1], pz[:, bank, 0:C], ACT.Sigmoid, scale=-1.0).then_inc(z_act, 1)
                    else:
                        act.activation(zbT[:, i, 1:289], pz[:, bank, 0:288], ACT.Copy)
                        act.activation(zbT[:, i, 289:361].rearrange("p (s l) -> p s l", l=9)[:, :, 1:9],
                                       pz[:, bank, 288:C].rearrange("p (s l) -> p s l", l=8),
                                       ACT.Copy).then_inc(z_act, 1)
                act.wait_ge(prod_used, 16)
                act.activation(compact[:], pC, ACT.Copy).then_inc(compact_done, 1)

            @block.vector
            def _(dve):
                link = linker(dve, dve_chain)

                def score_step(n):
                    q16, f16v, k16, p16 = (blocks16(a) for a in (qT, fT, kT, prod[:, n % 2]))
                    q8, f8v, k8, p8 = (blocks8(a) for a in (qT, fT, kT, prod[:, n % 2]))
                    i, j = 15 - n, 7 - n
                    if n:
                        r16 = q16[:, :, :, i + 1:16]
                        ins = dve.tensor_tensor(r16, r16, f16v[:, :, :, i + 1:i + 2].to_broadcast([P, HA, NB, n]), ALU.mult)
                        if n < 8:
                            r8 = q8[:, :, :, j + 1:8]
                            ins = dve.tensor_tensor(r8, r8, f8v[:, :, :, j + 1:j + 2].to_broadcast([P, HA, NS, n]), ALU.mult)
                        link(ins)
                    else:
                        dve.wait_ge(z_dve, STEP0)
                        dve.wait_ge(prod_zero, 2)
                    if n >= 2:
                        dve.wait_ge(prod_used, n - 1)
                    ins = dve.tensor_tensor(p16[:, :, :, i:16], q16[:, :, :, i:16],
                                            k16[:, :, :, i:i + 1].to_broadcast([P, HA, NB, n + 1]), ALU.mult)
                    if n < 8:
                        ins = dve.tensor_tensor(p8[:, :, :, j:8], q8[:, :, :, j:8],
                                                k8[:, :, :, j:j + 1].to_broadcast([P, HA, NS, n + 1]), ALU.mult)
                    ins.then_inc(prod_ready, 1)

                def low(m):
                    dve.wait_ge(w_hi, m + 1)
                    if m >= 2:
                        dve.wait_ge(item_done, m - 1)
                    dve.tensor_tensor(wlo[:, m % 2], wraw[:, m % 4], whi[:, m % 2], ALU.subtract).then_inc(w_lo, 1)

                dve.wait_ge(c_in, 32)
                th0, th1 = col("theta0", 0, 4), col("theta1", 0, 4)
                link(dve.tensor_tensor(lbt[:, 0], th0, th1, ALU.max))
                dve.tensor_tensor(lbt[:, 1], th0, lbt[:, 0], ALU.subtract)
                link(dve.tensor_tensor(lbt[:, 2], th1, lbt[:, 0], ALU.subtract))
                link(dve.tensor_copy(lbt[:, 0], lbt[:, 1]))
                dve.tensor_copy(lbt[:, 1], lbt[:, 2]).then_inc(a2, 1)
                dve.wait_ge(norm_in, 16)

                def normalise(i):
                    dve.wait_ge(rt_done, i + 1)
                    dve.reciprocal(rs[:, 6 + i:7 + i], rs[:, 3 + i:4 + i]).then_inc(rstd_done, 1)
                    dve.wait_ge(rstd_done, i + 1)
                    dve.scalar_tensor_tensor(out=x[:, i], in0=x[:, i], scalar=rs[:, 6 + i:7 + i], in1=norm_row,
                                             op0=ALU.mult, op1=ALU.mult).then_inc(xn_done, 1)

                def x_low(i):
                    for g in range(2):
                        dve.wait_ge(tr_hi, 2 * i + g + 1)
                        dve.tensor_tensor(xnl[:, 4 * g:4 * g + 4, P * i:P * i + TW[i]], pst[:, g, :, 0:TW[i]],
                                          xnh[:, 4 * g:4 * g + 4, P * i:P * i + TW[i]], ALU.subtract).then_inc(tr_lo, 1)

                normalise(0)
                normalise(1)
                x_low(0)
                normalise(2)
                x_low(1)
                x_low(2)
                low(0)
                low(1)
                dve.wait_ge(a2, 2)
                link(dve.tensor_tensor(lbt[:, 4], lbt[:, 2], lbt[:, 3], ALU.add))
                link(dve.reciprocal(lbt[:, 5], lbt[:, 4]))
                link(dve.tensor_tensor(lbt[:, 0], lbt[:, 2], lbt[:, 5], ALU.mult))
                link(dve.tensor_scalar(lbt[:, 1], lbt[:, 0], -1.0, 1.0, ALU.mult, ALU.add))
                dve.wait_ge(sh_in, 16)
                dve.tensor_copy(zbT[:, :, 289:361].rearrange("p f (s l) -> p f s l", l=9)[:, :, :, 0],
                                shift0[:]).then_inc(shift_copied, 1)
                for m in range(2, ITEMS + 2):
                    if m < ITEMS:
                        low(m)
                    n = m - 2 - NZI
                    if n == -1:
                        dve.wait_ge(item_done, NZI)
                        for i in range(3):
                            dve.tensor_copy(vtok[0:TW[i], i], pz[0:TW[i], i, :].rearrange("p (h e) -> p h e", e=P)) \
                                .then_inc(z_tok, 1)
                    if 0 <= n < 12:
                        kind, i = tiles[n]
                        bank = (n + 3) % NBANK
                        dve.wait_ge(z_act, n + 1)
                        if kind in "qo":
                            dst = qT if kind == "q" else zoT
                            dve.tensor_tensor(dst[:, i], pz[:, bank, 0:C], sig[:, n % 2, 0], ALU.mult).then_inc(z_dve, 1)
                        else:
                            dve.tensor_scalar(fT[:, i], sig[:, n % 2, 0], lbt[:, 1, i:i + 1], lbt[:, 0, i:i + 1],
                                              ALU.mult, ALU.add)
                            dve.tensor_scalar(kT[:, i], sig[:, n % 2, 1], lbt[:, 1, i:i + 1], None,
                                              ALU.mult).then_inc(z_dve, 1)
                    if STEP0 <= n < STEP0 + 16:
                        score_step(n - STEP0)
        t2.free()
        in_mem.free()
        hp_mem = Mem()
        offm = hp_mem.sb("offm", [P, 2, HA, P])
        ps_h = Mem()
        psI = ps_h.ps("psI", [P, HA, 512])
        psO = ps_h.ps("psO", [P, 2, HA, P])
        psK = ps_h.ps("psK", [P, HA, P])
        q_decayed, inner_full, off_full, half_copied, kt_full, kt_free, sc_done = (
            sem(n) for n in ("q_decayed", "inner_full", "off_full", "half_copied", "kt_full", "kt_free", "sc_done"))
        pairs = lambda a: a[:, :, 0:256].rearrange("p h (c b j) -> p h c b j", b=2, j=16)
        with nc.Block() as block:
            @block.vector
            def _(dve):
                q16, g16, q8, g8 = blocks16(qT), blocks16(fT), blocks8(qT), blocks8(fT)
                dve.tensor_tensor(q16, q16, g16[:, :, :, 0:1].to_broadcast([P, HA, NB, 16]), ALU.mult)
                dve.tensor_tensor(q8, q8, g8[:, :, :, 0:1].to_broadcast([P, HA, NS, 8]), ALU.mult)
                dve.tensor_tensor(kT[:], kT[:], suf[:], ALU.mult).then_inc(q_decayed, 1)
                dve.wait_ge(q_decayed, 1)
                fe = f16[:, :, 0:16].rearrange("p h (c b) -> p h c b", b=2)
                for h in range(HA):
                    dve.tensor_tensor(pairs(q2)[:, h, :, 1], pairs(qT)[:, h, :, 1],
                                      fe[:, h, :, 0:1].to_broadcast([P, 8, 16]), ALU.mult)
                    dve.tensor_tensor(pairs(k2h)[:, h, :, 0], pairs(kT)[:, h, :, 0],
                                      fe[:, h, :, 1:2].to_broadcast([P, 8, 16]), ALU.mult)
                dve.tensor_copy(f32c[:, :, 8:9], f16[:, :, 16:17])
                dve.tensor_tensor(f32c[:, :, 0:8], fe[:, :, :, 0], fe[:, :, :, 1], ALU.mult).then_inc(q_decayed, 1)
                mask = lambda m, n, w: masks[0:n, m:m + 1, 0:w].to_broadcast([n, HA, w])
                dve.wait_ge(inner_full, 1)
                for i in range(2):
                    dve.tensor_tensor(scT[:, i], psI[:, :, P * i:P * i + P], mask(M_HI, P, P), ALU.mult)
                dve.tensor_tensor(scT[0:96, 2, :, 0:32], psI[0:96, :, 256:288], mask(M_HI, 96, 32), ALU.mult)
                dve.tensor_tensor(scT[0:96, 2, :, 32:96], psI[0:96, :, SAMP0:C],
                                  masks[0:96, M_TIU:M_TIU + 1, 32:96].to_broadcast([96, HA, 64]), ALU.mult)
                dve.wait_ge(off_full, 1)
                for i in range(2):
                    dve.tensor_tensor(offm[:, i], psO[:, i], mask(M_HO, P, P), ALU.mult).then_inc(sc_done, 1)
                dve.wait_ge(sc_done, 2)
                dve.tensor_tensor(scT[:, 0:2], scT[:, 0:2], offm[:], ALU.add).then_inc(sc_done, 1)

            @block.tensor
            def _(pe):
                for h in range(HA):
                    rows = slice(32 * h, 32 * h + 32)
                    pe.matmul(psI[:, h, 0:SAMP0], expand[rows, 0], compact[rows, 0:SAMP0], start=True, stop=True)
                    ins = pe.matmul(psI[:, h, SAMP0:C], expand[rows, 1], compact[rows, SAMP0:C], start=True, stop=True)
                ins.then_inc(inner_full, 1)
                pe.wait_ge(q_decayed, 1)
                for i in range(2):
                    for h in range(HA):
                        ins = pe.matmul(psO[:, i, h], kT[:, h, P * i:P * i + P], qT[:, h, P * i:P * i + P],
                                        start=True, stop=True)
                ins.then_inc(off_full, 1)
                pe.wait_ge(q_decayed, 2)
                pe.wait_ge(half_copied, 1)
                for i in range(3):
                    if i:
                        pe.wait_ge(kt_free, i)
                    for h in range(HA):
                        ins = pe.transpose(psK[0:TW[i], h], k2h[:, h, P * i:P * i + TW[i]], ident[:])
                    ins.then_inc(kt_full, 1)

            @block.scalar
            def _(act):
                act.wait_ge(q_decayed, 1)
                for h in range(HA):
                    act.activation(pairs(k2h)[:, h, :, 1], pairs(kT)[:, h, :, 1], ACT.Copy)
                act.activation(k2h[:, :, 256:C], kT[:, :, 256:C], ACT.Copy).then_inc(half_copied, 1)
                for h in range(HA):
                    act.activation(pairs(q2)[:, h, :, 0], pairs(qT)[:, h, :, 0], ACT.Copy)
                act.activation(q2[:, :, 256:C], qT[:, :, 256:C], ACT.Copy).then_inc(half_copied, 1)
                for i in range(3):
                    act.wait_ge(kt_full, i + 1)
                    act.activation(ktok[0:TW[i], i], psK[0:TW[i]], ACT.Copy).then_inc(kt_free, 1)
        ps_h.free()
        hp_mem.free()

        order = [12, 13, 4, 5, 6, 7, 0, 1, 2, 3, 8, 9, 10, 11]
        samp = lambda a: a[:, :, 289:361].rearrange("p f (s l) -> p f s l", l=9)
        zs8 = lambda a: a[:, :, SAMP0:C].rearrange("p f (s l) -> p f s l", l=8)
        zm_done = sem("zm_done")
        NCH = 9
        s_mem = Mem()
        sts = s_mem.sb("sts", [P, NCH, HA, P])
        sth = s_mem.sb("sth", [P, NS, HA, P])
        stn = s_mem.sb("stn", [P, NS, HA, P])
        vexp = s_mem.sb("vexp", [P, 2, NS, P])
        osq = s_mem.sb("osq", [P, HA, C])
        rsh = s_mem.sb("rsh", [8, 2, 1, C])
        ps4 = Mem()
        kv = ps4.ps("kv", [P, 4, 512])
        po = ps4.ps("po", [P, HA, 512])
        vexp_ready, kv_full, kv_free, st_ready, o_full, sq_ready, ms_full, rt_h, inv_made, gated, inv_full = (
            sem(n) for n in ("vexp_ready", "kv_full", "kv_free", "st_ready", "o_full",
                             "sq_ready", "ms_full", "rt_h", "inv_made", "gated", "inv_full"))
        with nc.Block() as block:
            @block.sync
            def _(sp):
                sp.dma_start(sth[:], inp["state_h"]).then_inc(states_in, 16)
                sp.wait_ge(st_ready, NCH)
                sp.dma_start(out["hgrn_p"], sts[:, NCH - 1]).then_inc(states_out, 16)
                sp.wait_ge(st_ready, NCH + 2 * HA)
                sp.dma_start(out["hgrn_s"], stn[:]).then_inc(states_out, 16)
                sp.wait_ge(states_out, 32)

            @block.tensor
            def _(pe):
                for c in range(NCH):
                    if c >= 4:
                        pe.wait_ge(kv_free, c - 3)
                    b, w = 32 * c % P, 32 if c < 8 else 16
                    for h in range(HA):
                        ins = pe.matmul(kv[:, c % 4, P * h:P * h + P], ktok[b:b + w, c // 4, h], vtok[b:b + w, c // 4, h],
                                        start=True, stop=True)
                    ins.then_inc(kv_full, 1)
                for h in range(HA):
                    pe.wait_ge(vexp_ready, h + 1)
                    for g in range(2):
                        n = NCH + 2 * h + g
                        pe.wait_ge(kv_free, n - 3)
                        ins = pe.matmul(kv[:, n % 4, :], ktok[0:96, 2, h],
                                        vexp[0:96, h % 2, 4 * g:4 * g + 4].rearrange("p s e -> p (s e)"),
                                        start=True, stop=True)
                        ins.then_inc(kv_full, 1)
                pe.wait_ge(states_in, 16)
                pe.wait_ge(st_ready, NCH)
                for h in range(HA):
                    for i in range(3):
                        pe.matmul(po[:, h, P * i:P * i + TW[i]], vtok[0:TW[i], i, h], scT[0:TW[i], i, h, 0:TW[i]],
                                  start=i == 0, stop=False, skip_group_check=True)
                    reads = [(sts[:, c - 1, h], 32 * c, 32 if c < 8 else 16) for c in range(1, NCH)] + \
                            [(sth[:, s, h], SAMP0 + LS * s, LS) for s in range(NS)]
                    for n, (state, t, w) in enumerate(reads):
                        for m in range(0, P, 32):
                            ins = pe.matmul(po[m:m + 32, h, t:t + w], state[:, m:m + 32], q2[:, h, t:t + w],
                                            start=False, stop=n == len(reads) - 1, skip_group_check=True)
                    ins.then_inc(o_full, 1)
                for h in range(HA):
                    if h == 0:
                        pe.wait_ge(kv_free, NCH + 2 * HA)
                    pe.wait_ge(sq_ready, h + 1)
                    ins = pe.matmul(kv[0:8, 0, 0:C], row_sum_h(h), osq[:, h], start=h == 0, stop=h == HA - 1)
                ins.then_inc(ms_full, 1)
                pe.wait_ge(inv_made, 1)
                for h in range(HA):
                    pe.matmul(kv[:, h, 0:C], spread8(h), rsh[0:8, 1, 0], start=True, stop=True).then_inc(inv_full, 1)

            @block.gpsimd
            def _(pool):
                for h in range(HA):
                    if h >= 2:
                        pool.wait_ge(kv_full, NCH + 2 * (h - 1))
                    pool.tensor_tensor(vexp[0:96, h % 2], vtok[0:96, 2, h:h + 1, :].to_broadcast([96, NS, P]),
                                       seq9[0:96, 0:NS].unsqueeze(2).to_broadcast([96, NS, P]), ALU.mult) \
                        .then_inc(vexp_ready, 1)

            @block.vector
            def _(dve):
                for c in range(NCH):
                    dve.wait_ge(kv_full, c + 1)
                    kvc = kv[:, c % 4, :].rearrange("p (h e) -> p h e", h=HA)
                    if c == 0:
                        ins = dve.tensor_copy(sts[:, 0], kvc)
                    else:
                        dve.wait_ge(st_ready, c)
                        for h in range(HA):
                            ins = dve.scalar_tensor_tensor(out=sts[:, c, h], in0=sts[:, c - 1, h], scalar=f32c[:, h, c:c + 1],
                                                           in1=kvc[:, h], op0=ALU.mult, op1=ALU.add)
                    ins.then_inc(st_ready, 1)
                    dve.wait_ge(st_ready, c + 1)
                    dve.sem_inc(kv_free, 1)
                dve.wait_ge(states_in, 16)
                for h in range(HA):
                    for g in range(2):
                        n = NCH + 2 * h + g
                        dve.wait_ge(kv_full, n + 1)
                        for s in range(4):
                            ins = dve.scalar_tensor_tensor(out=stn[:, 4 * g + s, h], in0=sth[:, 4 * g + s, h],
                                                           scalar=f8[:, h, 4 * g + s:4 * g + s + 1],
                                                           in1=kv[:, n % 4, P * s:P * s + P], op0=ALU.mult, op1=ALU.add)
                        ins.then_inc(st_ready, 1)
                        dve.wait_ge(st_ready, n + 1)
                        dve.sem_inc(kv_free, 1)
                link = linker(dve, dve_chain)
                dve.tensor_tensor(zm[:, :, 0:SAMP0], zbT[:, :, 0:288], zbT[:, :, 1:289], ALU.subtract)
                for s in range(NS):
                    ins = dve.tensor_tensor(zm[:, :, SAMP0 + 8 * s:SAMP0 + 8 * s + 8], samp(zbT)[:, :, s, 0:8],
                                            samp(zbT)[:, :, s, 1:9], ALU.subtract)
                link(ins)
                for f in order:
                    dve.scalar_tensor_tensor(out=zm[:, f, 0:SAMP0], in0=zm[:, f, 0:SAMP0], scalar=col("mu", f),
                                             in1=zbT[:, f, 1:289], op0=ALU.mult, op1=ALU.add)
                    dve.scalar_tensor_tensor(out=zs8(zm)[:, f], in0=zs8(zm)[:, f], scalar=col("mu", f),
                                             in1=samp(zbT)[:, f, :, 1:9], op0=ALU.mult, op1=ALU.add).then_inc(zm_done, 1)
                for h in range(HA):
                    dve.wait_ge(sq_ready, h + 1)
                    dve.scalar_tensor_tensor(out=zoT[:, h], in0=po[:, h, 0:C], scalar=col("hgrn_norm", h),
                                             in1=zoT[:, h], op0=ALU.mult, op1=ALU.mult).then_inc(gated, 1)
                dve.wait_ge(rt_h, 1)
                dve.reciprocal(rsh[0:8, 1, 0], rsh[0:8, 0, 0]).then_inc(inv_made, 1)
                dve.wait_ge(gated, HA)
                for h in range(HA):
                    dve.wait_ge(inv_full, h + 1)
                    dve.tensor_tensor(mixT[:, h], zoT[:, h], kv[:, h, 0:C], ALU.mult)

            @block.scalar
            def _(act):
                for h in range(HA):
                    act.wait_ge(o_full, h + 1)
                    act.activation(osq[:, h], po[:, h, 0:C], ACT.Square).then_inc(sq_ready, 1)
                act.wait_ge(ms_full, 1)
                act.activation(rsh[0:8, 0, 0], kv[0:8, 0, 0:C], ACT.Sqrt, bias=epsc[0:8, 0:1], scale=1.0 / P) \
                    .then_inc(rt_h, 1)
        ps4.free()
        s_mem.free()
        h_mem.free()
        za_mem.free()
        CEXP = float(np.exp(-0.5))
        y_mem = Mem()
        gT = y_mem.sb("gT", [P, 4, C])
        bonusT = y_mem.sb("bonusT", [P, 4, C])
        ARx = y_mem.sb("ARx", [P, 4, 4, C])
        Bt = y_mem.sb("Bt", [P, 4, C])
        Kt = y_mem.sb("Kt", [P, 4, C])
        pinc = y_mem.sb("pinc", [P, 4, C])
        vr = y_mem.sb("vr", [P, 3, 512])
        bk = y_mem.sb("bk", [P, 2, 5, 512])
        w5 = Mem()
        lora = w5.sb("lora", [P, 2, 512])
        lo_in = mixT[:, 6:8]
        aT = w5.sb("aT", [P, 4, C])
        Lw = w5.sb("Lw", [P, 4, C])
        cum = w5.sb("cum", [P, 4, C])
        tmpa = w5.sb("tmpa", [P, 4, C])
        kkn = w5.sb("kkn", [P, 4, C])
        k7 = w5.sb("k7", [P, 4, C])
        ex = w5.sb("ex", [P, 4, C])
        At = w5.sb("At", [P, 4, C])
        Bh, Kh = aT, Lw
        inv8 = mixT[0:8, 4:6]
        sh_out = w5.sb("sh_out", [P, FB, 1 + NS])
        ps5 = Mem()
        psl = ps5.ps("psl", [P, 8, 512])
        lora_in, tanh_done, lo_full, lo_used, kk_sq, kk_full, kk_rt, cum_done, to_exp, exps, zeroed, \
            rk_ready, rk_full, tok_src, tok_full, tok_free, sh_done, kk_inv, \
            kk_used, rt_made = (
                sem(n) for n in ("lora_in", "tanh_done", "lo_full", "lo_used", "kk_sq",
                                 "kk_full", "kk_rt", "cum_done", "to_exp", "exps", "zeroed", "rk_ready", "rk_full", "tok_src",
                                 "tok_full", "tok_free", "sh_done", "kk_inv", "kk_used", "rt_made"))
        with nc.Block() as block:
            @block.sync
            def _(sp):
                sp.dma_start(lora[:], inp["lora"].rearrange("p (a f) -> p a f", a=2)).then_inc(lora_in, 16)
                sp.wait_ge(sh_done, 2)
                sp.dma_start(out["shift"], sh_out[:]).then_inc(states_out, 16)
                sp.wait_ge(states_out, 48)

            @block.gpsimd
            def _(pool):
                pool.memset(lo_in[0:64, 1], 0.0).then_inc(zeroed, 1)
                pool.wait_ge(zeroed, 1)
                pool.memset(lo_in[64:128, 0], 0.0).then_inc(zeroed, 1)
                pool.memset(ARx[64:128, :, 0::2], 0.0).then_inc(zeroed, 1)
                pool.wait_ge(zeroed, 3)
                pool.memset(ARx[0:64, :, 1::2], 0.0).then_inc(zeroed, 1)
                pool.wait_ge(zeroed, 4)
                pool.memset(bk[:], 0.0).then_inc(zeroed, 1)
                pool.memset(vr[:], 0.0).then_inc(zeroed, 1)
                pool.tensor_copy(sh_out[:, :, 0:1], zbT[:, :, PROMPT:PROMPT + 1]).then_inc(sh_done, 1)
                pool.tensor_copy(sh_out[:, :, 1:1 + NS], samp(zbT)[:, :, :, 8]).then_inc(sh_done, 1)
                pool.wait_ge(exps, 1)
                for g in range(2):
                    half = slice(64 * g, 64 * g + 64)
                    if g:
                        pool.wait_ge(rt_made, 1)
                    pool.tensor_tensor(ARx[half, :, 2 + g], zm[half, 0:4], pinc[half], ALU.mult).then_inc(rt_made, 1)

            @block.tensor
            def _(pe):
                pe.wait_ge(lora_in, 16)
                pe.wait_ge(tanh_done, 1)
                pe.wait_ge(zeroed, 2)
                for i in range(4):
                    pe.matmul(psl[:, i, 0:C], lora[:, 0, P * i:P * i + P], lo_in[:, 0], start=True, stop=True)
                    pe.matmul(psl[:, 4 + i, 0:C], lora[:, 0, P * i:P * i + P], lo_in[:, 1], start=True,
                              stop=True).then_inc(lo_full, 1)
                pe.wait_ge(tanh_done, 2)
                for i in range(4):
                    pe.wait_ge(lo_used, i + 1)
                    pe.matmul(psl[:, i, 0:C], lora[:, 1, P * i:P * i + P], zm[:, 13], start=True,
                              stop=True).then_inc(lo_full, 1)
                pe.wait_ge(lo_used, 4)
                pe.wait_ge(kk_sq, 1)
                for i in range(4):
                    ins = pe.matmul(psl[0:8, 4, 0:C], row_sum_r(i), tmpa[:, i], start=i == 0, stop=i == 3)
                ins.then_inc(kk_full, 1)
                pe.wait_ge(lo_used, 8)
                for i in range(3):
                    for j in range(4):
                        ins = pe.transpose(psl[0:TW[i], i, P * j:P * j + P], zm[:, 8 + j, P * i:P * i + TW[i]], ident[:])
                    ins.then_inc(tok_full, 1)
                pe.wait_ge(kk_inv, 2)
                for i in range(4):
                    ins = pe.matmul(psl[:, 4 + i, 0:C], spread8(i), inv8[:, 1], start=True, stop=True)
                ins.then_inc(kk_full, 1)
                pe.wait_ge(tok_free, 3)
                for i in range(4):
                    pe.wait_ge(rk_ready, 1)
                    pe.matmul(psl[:, i, 0:C], masks[:, M_B64], ex[:, i], start=True, stop=True).then_inc(rk_full, 1)
                for n in range(3, 9):
                    what, i = divmod(n, 3)
                    pe.wait_ge(tok_src, what)
                    if n >= 5:
                        pe.wait_ge(tok_free, n - 1)
                    else:
                        pe.wait_ge(kk_used, 1)
                    src = (Bh, Kh)[what - 1]
                    for j in range(4):
                        ins = pe.transpose(psl[0:TW[i], 4 + n % 2, P * j:P * j + P], src[:, j, P * i:P * i + TW[i]], ident[:])
                    ins.then_inc(tok_full, 1)

            @block.scalar
            def _(act):
                act.activation(lo_in[0:64, 0], zm[0:64, 12], ACT.Tanh)
                act.activation(lo_in[64:128, 1], zm[64:128, 12], ACT.Copy).then_inc(tanh_done, 1)
                act.activation(zm[:, 13], zm[:, 13], ACT.Sigmoid).then_inc(tanh_done, 1)
                for i in range(4):
                    act.wait_ge(lo_full, i + 1)
                    act.activation(Lw[:, i], psl[:, i, 0:C], ACT.Sigmoid, bias=col("w0", i))
                    act.activation(aT[:, i], psl[:, 4 + i, 0:C], ACT.Sigmoid, bias=col("a0", i)).then_inc(lo_used, 1)
                for i in range(4):
                    act.wait_ge(lo_full, 5 + i)
                    act.activation(gT[:, i], psl[:, i, 0:C], ACT.Copy).then_inc(lo_used, 1)
                act.wait_ge(kk_full, 1)
                act.activation(inv8[:, 0], psl[0:8, 4, 0:C], ACT.Sqrt).then_inc(kk_rt, 1)
                act.wait_ge(zeroed, 6)
                for i in range(3):
                    act.wait_ge(tok_full, i + 1)
                    act.activation(vr[0:TW[i], i], psl[0:TW[i], i, :], ACT.Copy).then_inc(tok_free, 1)
                act.wait_ge(cum_done, 1)
                act.activation(pinc[:], cum[:], ACT.Exp).then_inc(exps, 1)
                act.activation(Bt[:], cum[:], ACT.Exp, scale=-1.0).then_inc(exps, 1)
                act.wait_ge(to_exp, 1)
                act.activation(At[:], At[:], ACT.Exp).then_inc(exps, 1)
                act.wait_ge(to_exp, 2)
                act.activation(Kt[:], Kt[:], ACT.Exp).then_inc(exps, 1)
                for n in range(3, 9):
                    what, i = divmod(n, 3)
                    act.wait_ge(tok_full, n + 1)
                    src = psl[:, 4 + n % 2, :]
                    if i == 2:
                        ins = act.activation(bk[0:96, what - 1, 4], src[0:96], ACT.Copy)
                    else:
                        act.activation(bk[0:64, what - 1, 2 * i], src[0:64], ACT.Copy)
                        ins = act.activation(bk[64:128, what - 1, 2 * i + 1], src[64:128], ACT.Copy)
                    ins.then_inc(tok_free, 1)

            @block.vector
            def _(dve):
                link = linker(dve, dve_chain)
                dve.wait_ge(zm_done, FB)
                r, k, v = zm[:, 0:4], zm[:, 4:8], zm[:, 8:12]
                for i in range(4):
                    ins = dve.tensor_scalar(kkn[:, i], k[:, i], col("k_k", i), None, ALU.mult)
                link(ins)
                dve.tensor_tensor(tmpa[:], kkn[:], kkn[:], ALU.mult).then_inc(kk_sq, 1)
                for i in range(4):
                    ins = dve.tensor_scalar(ex[:, i], r[:, i], col("r_k", i), None, ALU.mult)
                link(ins)
                dve.wait_ge(lo_used, 4)
                link(dve.tensor_scalar(Lw[:], Lw[:], -CEXP, None, ALU.mult))
                for i in range(4):
                    ins = dve.tensor_tensor_scan(cum[:, i], restart, Lw[:, i], 0.0, ALU.mult, ALU.add)
                ins.then_inc(cum_done, 1)
                dve.wait_ge(cum_done, 1)
                link(dve.tensor_tensor(At[:], cum[:], Lw[:], ALU.subtract))
                dve.sem_inc(to_exp, 1)
                pc = lambda a: a[:, :, 0:256].rearrange("p f (c j) -> p f c j", j=64)
                pe2 = lambda a: a[:, :, 256:288].rearrange("p f (c j) -> p f c j", j=16)
                dve.tensor_tensor(pc(Kt), pc(cum)[:, :, :, 63:64].to_broadcast([P, 4, 4, 64]), pc(cum), ALU.subtract)
                dve.tensor_tensor(pe2(Kt), pe2(cum)[:, :, :, 15:16].to_broadcast([P, 4, 2, 16]), pe2(cum), ALU.subtract)
                dve.tensor_tensor(zs8(Kt), zs8(cum)[:, :, :, 7:8].to_broadcast([P, 4, NS, 8]), zs8(cum),
                                  ALU.subtract).then_inc(to_exp, 1)
                dve.wait_ge(kk_rt, 1)
                dve.tensor_scalar(inv8[:, 0], inv8[:, 0], 1e-12, None, ALU.max).then_inc(kk_inv, 1)
                dve.wait_ge(kk_inv, 1)
                dve.reciprocal(inv8[:, 1], inv8[:, 0]).then_inc(kk_inv, 1)
                for i in range(4):
                    ins = dve.tensor_scalar(k7[:, i], aT[:, i], -1.0, col("k_a", i), ALU.add, ALU.mult)
                link(ins)
                link(dve.scalar_tensor_tensor(out=k7[:], in0=k7[:], scalar=1.0, in1=k, op0=ALU.add, op1=ALU.mult))
                dve.wait_ge(kk_full, 2)
                for i in range(4):
                    ins = dve.tensor_tensor(kkn[:, i], kkn[:, i], psl[:, 4 + i, 0:C], ALU.mult)
                ins.then_inc(kk_used, 1)
                dve.wait_ge(kk_used, 1)
                link(dve.tensor_tensor(tmpa[:], kkn[:], aT[:], ALU.mult))
                dve.tensor_tensor(ex[:], ex[:], k7[:], ALU.mult).then_inc(rk_ready, 1)
                dve.wait_ge(exps, 4)
                dve.tensor_tensor(Bh[:], tmpa[:], Kt[:], ALU.mult).then_inc(tok_src, 1)
                dve.tensor_tensor(Kh[:], k7[:], Kt[:], ALU.mult).then_inc(tok_src, 1)
                dve.wait_ge(tok_src, 2)
                dve.wait_ge(zeroed, 4)
                for g in range(2):
                    half = slice(64 * g, 64 * g + 64)
                    dve.scalar_tensor_tensor(out=ARx[half, :, g], in0=At[half], scalar=-1.0, in1=kkn[half],
                                             op0=ALU.mult, op1=ALU.mult)
                link(dve.tensor_tensor(Kt[:], k7[:], Bt[:], ALU.mult))
                dve.tensor_tensor(Bt[:], tmpa[:], Bt[:], ALU.mult)
                for i in range(4):
                    dve.wait_ge(rk_full, i + 1)
                    dve.tensor_tensor(bonusT[:, i], psl[:, i, 0:C], v[:, i], ALU.mult)
        ps5.free()
        w5.free()
        m6 = Mem()
        TT = zflat[:, 0:3 * HB * P].rearrange("p (i h s) -> p i h s", i=3, h=HB)
        Et = zflat[:, 3 * HB * P:4 * HB * P].rearrange("p (h s) -> p h s", h=HB)
        Aak = m6.sb("Aak", [P, 3, HB, P])
        Arb = m6.sb("Arb", [P, 3, HB, P])
        Ark = m6.sb("Ark", [P, 3, HB, P])
        t6 = [zbT[:].rearrange("p f c -> p (f c)")[:, HB * P * i:HB * P * (i + 1)].rearrange("p (h s) -> p h s", h=HB)
              for i in range(4)]
        pwt = t6[0]
        pw = t6[1]
        qwt = t6[2]
        qw = t6[3]
        ps6 = Mem()
        pb6 = ps6.ps("pb6", [P, 8, 4, P])
        sc_full, sc_free, mm_full, by_act, by_dve, tt_first = (
            sem(n) for n in ("sc_full", "sc_free", "mm_full", "by_act", "by_dve", "tt_first"))
        def solve_steps(i):
            s = [("N2", pwt, pw, qwt, "a"), ("N2t", pw, pwt, qw, "a"), ("R1", qwt, "TT", "TT", "d"),
                 ("N4", qw, qwt, pw, "a"), ("N4t", qwt, qw, pwt, "a"), ("R2", pw, "TT", "TT", "d"),
                 ("N8", pwt, pw, qwt, "a"), ("R3", qwt, "TT", "TT", "d")]
            if i < 2:
                s += [("R", "TT", "ident", qw, "a"), ("F", Et, qw, pwt, "a"), ("Ft", qw, Et, pw, "a"),
                      ("Z1", pwt, "TT", "TT", "d"), ("F2", pw, pwt, qwt, "a"), ("Z2", qwt, "TT", "TT", "d")]
            return s
        reads = {"N2": [], "N2t": [], "R1": ["N2"], "N4": ["N2", "N2t"], "N4t": ["N2", "N2t"], "R2": ["N4", "R1"],
                 "N8": ["N4", "N4t"], "R3": ["N8", "R2"], "R": ["R3"], "F": ["R"], "Ft": ["R"], "Z1": ["F", "R3"],
                 "F2": ["F", "Ft"], "Z2": ["F2", "Z1"]}
        ops = [(i, q) + step for i in range(3) for step in solve_steps(i) for q in range(2)]
        taken = {}
        n_by = {"a": 0, "d": 0}
        for i, q, name, _, _, _, who in ops:
            n_by[who] += 1
            taken[i, q, name] = (by_act if who == "a" else by_dve, n_by[who])
        order6 = [(i, q, name) for i, q, name, *_ in ops]
        NSC = 10
        with nc.Block() as block:
            @block.tensor
            def _(pe):
                for i in range(3):
                    w, cs = TW[i], slice(P * i, P * i + TW[i])
                    first = order6.index((i, 0, "N2"))
                    for n in range(NSC):
                        if i and n < 8:
                            for q in range(2):
                                pe.wait_ge(*taken[i - 1, q, "Z2"])
                                pe.wait_ge(*taken[i - 1, q, "F2"])
                        if n >= 8:
                            pe.wait_ge(sc_free, NSC * i + n - 7)
                        bank = pb6[:, n % 8]
                        if n < 8:
                            j, kind = divmod(n, 2)
                            lhs = (Bt, Kt)[kind]
                            ins = pe.matmul(bank[0:w, :, 0:w], lhs[:, j, cs], ARx[:, j, :, cs], start=True, stop=True)
                        else:
                            for m in range(4):
                                h = 4 * (n - 8) + m
                                ins = pe.matmul(bank[0:w, m, 0:w], ARx[:, h // 2, h % 2, cs], Bt[:, h // 2, cs],
                                                start=True, stop=True)
                        ins.then_inc(sc_full, 1)
                    for n, (_, q, name, lhs, rhs, dst, who) in enumerate(o for o in ops if o[0] == i):
                        if n < 8:
                            pe.wait_ge(sc_free, NSC * (i + 1))
                        else:
                            pe.wait_ge(*taken[order6[first + n - 8]])
                        for r in reads[name]:
                            pe.wait_ge(*taken[i, q, r])
                        if name == "R1":
                            pe.wait_ge(tt_first, i + 1)
                        for m in range(4):
                            h = 4 * q + m
                            pick = lambda a: TT[0:w, i, h, 0:w] if a == "TT" else ident[0:w, 0:w] if a == "ident" \
                                else a[0:w, h, 0:w]
                            if name == "R":
                                ins = pe.transpose(pb6[0:w, n % 8, m, 0:w], pick(lhs), pick(rhs))
                            else:
                                ins = pe.matmul(pb6[0:w, n % 8, m, 0:w], pick(lhs), pick(rhs), start=True, stop=True)
                        ins.then_inc(mm_full, 1)

            @block.vector
            def _(dve):
                dn = 0
                for i in range(3):
                    w = TW[i]
                    first = order6.index((i, 0, "N2"))
                    msk = lambda m, k: masks[0:w, m:m + 1, 0:w].to_broadcast([w, k, w])
                    if i:
                        dve.wait_ge(mm_full, first)
                    bu, bl, su, iu = (M_BU, M_BL, M_SU, M_IU) if i < 2 else (M_TBU, M_TBL, M_TBU, M_TIU)
                    for n in range(NSC):
                        dve.wait_ge(sc_full, NSC * i + n + 1)
                        bank = pb6[0:w, n % 8, :, 0:w]
                        j, kind = divmod(n, 2)
                        hs = slice(2 * j, 2 * j + 2)
                        if n >= 8:
                            ins = dve.tensor_tensor(pw[0:w, 4 * n - 32:4 * n - 28, 0:w], bank, msk(bl, 4), ALU.mult)
                        elif kind == 0:
                            dve.tensor_tensor(pwt[0:w, hs, 0:w], bank[:, 0:2], msk(bu, 2), ALU.mult)
                            if i < 2:
                                dve.tensor_tensor(Et[0:w, hs, 0:w], bank[:, 0:2], msk(M_EU, 2), ALU.mult)
                            ins = dve.tensor_tensor(Arb[0:w, i, hs, 0:w], bank[:, 2:4], msk(iu, 2), ALU.mult)
                        else:
                            dve.tensor_tensor(Aak[0:w, i, hs, 0:w], bank[:, 0:2], msk(su, 2), ALU.mult)
                            ins = dve.tensor_tensor(Ark[0:w, i, hs, 0:w], bank[:, 2:4], msk(iu, 2), ALU.mult)
                        ins.then_inc(sc_free, 1)
                    dve.wait_ge(sc_free, NSC * (i + 1))
                    dve.tensor_tensor(TT[0:w, i, :, 0:w], pwt[0:w, :, 0:w], msk(M_ID, HB), ALU.add).then_inc(tt_first, 1)
                    dve.wait_ge(tt_first, i + 1)
                    for n, (_, q, name, lhs, rhs, dst, who) in enumerate(o for o in ops if o[0] == i):
                        if who == "d":
                            dve.wait_ge(mm_full, first + n + 1)
                            if dn >= 2:
                                dve.wait_ge(by_dve, dn - 1)
                            acc = TT[0:w, i, 4 * q:4 * q + 4, 0:w]
                            dve.tensor_tensor(acc, acc, pb6[0:w, n % 8, :, 0:w], ALU.add).then_inc(by_dve, 1)
                            dn += 1

            @block.scalar
            def _(act):
                for i in range(3):
                    w = TW[i]
                    first = order6.index((i, 0, "N2"))
                    for n, (_, q, name, lhs, rhs, dst, who) in enumerate(o for o in ops if o[0] == i):
                        if who == "a":
                            act.wait_ge(mm_full, first + n + 1)
                            if name == "N4t":
                                act.wait_ge(tt_first, i + 1)
                            act.activation(dst[0:w, 4 * q:4 * q + 4, 0:w], pb6[0:w, n % 8, :, 0:w], ACT.Copy) \
                                .then_inc(by_act, 1)
        ps6.free()

        m7 = Mem()
        st = m7.sb("st", [P, 2, 4, HN])
        std = m7.sb("std", [P, 4, HN])
        spare = zflat[:, 3 * HB * P:3 * HB * P + 1536].rearrange("p (a b) -> p a b", a=3)
        xb = spare[:, 0]
        ub = m7.sb("ub", [P, 512])
        ss = m7.sb("ss", [P, 4, NS, HN])
        xm = spare[:, 1].rearrange("p (s v) -> p s v", s=NS)
        xs = spare[:, 2].rearrange("p (h v) -> p h v", h=HB)
        uv = zbT[:].rearrange("p f c -> p (f c)")[:, 0:72 * HN].rearrange("p (a b s v) -> p a b s v", a=4, b=2, s=9)
        yT = mixT[:, 4:8]
        ps7 = Mem()
        psX = ps7.ps("psX", [P, 512])
        psU = ps7.ps("psU", [P, 512])
        psSt = ps7.ps("psSt", [P, 512])
        psY = ps7.ps("psY", [P, 512])
        ps2 = ps7.ps("ps2", [P, 4, 512])
        (z7, x_full, x_ready, u_full, u_ready, st_full, st_done, std_done, y_full, y_taken, x0_full, x0_free,
         xs_ready, spread, spread_used, ns_free, spread_u, ns_mul) = (sem(n) for n in (
             "z7", "x_full", "x_ready", "u_full", "u_ready", "st_full", "st_done", "std_done", "y_full",
             "y_taken", "x0_full", "x0_free", "xs_ready", "spread", "spread_used", "ns_free", "spread_u", "ns_mul"))
        hv = lambda h: slice(HN * h, HN * h + HN)
        with nc.Block() as block:
            @block.sync
            def _(sp):
                sp.dma_start(ss[:], inp["state_r"]).then_inc(states_in, 16)
                sp.wait_ge(st_done, 5)
                sp.dma_start(out["rwkv_p"], st[:, 0]).then_inc(states_out, 16)
                sp.wait_ge(ns_free, 4)
                sp.dma_start(out["rwkv_s"], ss[:]).then_inc(states_out, 16)

            @block.gpsimd
            def _(pool):
                pool.memset(xb, 0.0).then_inc(z7, 1)
                pool.memset(ub[:], 0.0).then_inc(z7, 1)
                for h in range(HB):
                    if h >= 4:
                        pool.wait_ge(spread_used, (h - 4) // 2 + 1)
                    pool.tensor_tensor(uv[:, h % 4, 1], vr[:, 2, hv(h)].unsqueeze(1).to_broadcast([P, 9, HN]),
                                       seq9.unsqueeze(2).to_broadcast([P, 9, HN]), ALU.mult).then_inc(spread, 1)

            @block.tensor
            def _(pe):
                pe.wait_ge(z7, 2)
                t2c = slice(256, C)
                yo = lambda h: psY[64 * (h % 2):64 * (h % 2) + 64, hv(h // 2)]
                for c in range(4):
                    i, pb, col0 = c // 2, 64 * (c % 2), 64 * c
                    rows, ts = slice(pb, pb + 64), slice(64 * c, 64 * c + 64)
                    tl = slice(pb, pb + 64)
                    if c:
                        pe.wait_ge(st_done, c)
                        pe.wait_ge(x_ready, c)
                    for h in range(HB):
                        j, g = divmod(h, 2)
                        ins = pe.matmul(psX[rows, hv(h)], Aak[:, i, h, tl], vr[:, i, hv(h)], start=True, stop=c == 0,
                                        skip_group_check=True)
                        if c:
                            ins = pe.matmul(psX[rows, hv(h)], ARx[:, j, g, ts], st[:, (c - 1) % 2, j], start=False, stop=True,
                                      skip_group_check=True)
                    ins.then_inc(x_full, 1)
                    if c:
                        pe.wait_ge(y_taken, c)
                    for h in range(HB):
                        pe.matmul(yo(h), vr[:, i, hv(h)], Ark[:, i, h, tl], start=h < 2, stop=False,
                                  skip_group_check=True)
                    pe.wait_ge(x_ready, c + 1)
                    if c:
                        pe.wait_ge(u_ready, c)
                    for h in range(HB):
                        ins = pe.matmul(psU[rows, hv(h)], TT[:, i, h, tl], xb[:, hv(h)], start=True, stop=True)
                    ins.then_inc(u_full, 1)
                    for h in range(HB if c else 0):
                        j, g = divmod(h, 2)
                        pe.matmul(yo(h), st[:, (c - 1) % 2, j], ARx[:, j, 2 + g, ts], start=False, stop=False,
                                  skip_group_check=True)
                    pe.wait_ge(u_ready, c + 1)
                    for h in range(HB):
                        j, g = divmod(h, 2)
                        o = psSt[64 * g:64 * g + 64, hv(j)]
                        pe.matmul(o, bk[:, 0, c, hv(h)], ub[:, hv(h)], start=True, stop=False)
                        ins = pe.matmul(o, bk[:, 1, c, hv(h)], vr[:, i, hv(h)], start=False, stop=True)
                    ins.then_inc(st_full, 1)
                    if c == 0:
                        pe.wait_ge(states_in, 32)
                    for h in (2 * c, 2 * c + 1):
                        j, g = divmod(h, 2)
                        if h >= 4:
                            pe.wait_ge(x0_free, h - 3)
                        pe.matmul(ps2[0:96, h % 4, :], ARx[:, j, g, t2c], ss[:, j].rearrange("p s v -> p (s v)"),
                                  start=True, stop=True).then_inc(x0_full, 1)
                    for h in range(HB):
                        ins = pe.matmul(yo(h), ub[:, hv(h)], Arb[:, i, h, tl], start=False, stop=True,
                                        skip_group_check=True)
                    ins.then_inc(y_full, 1)
                pe.wait_ge(st_done, 4)
                pe.wait_ge(u_ready, 4)
                for h in range(HB):
                    j, g = divmod(h, 2)
                    pe.matmul(psX[0:96, hv(h)], ARx[:, j, g, t2c], st[:, 1, j], start=True, stop=True)
                    ins = pe.matmul(psU[0:96, hv(h)], Aak[0:96, 2, h, 0:96], vr[0:96, 2, hv(h)], start=True, stop=True)
                ins.then_inc(x_full, 1)
                pe.wait_ge(y_taken, 4)
                yb = psY[:, 0:384].rearrange("p (j t) -> p j t", j=4)
                yo2 = lambda h: yb[64 * (h % 2):64 * (h % 2) + 64, h // 2]
                reads = [(lambda j: st[:, 1, j], 0, 16)] + [(lambda j, s=s: ss[:, j, s], 32 + 8 * s, 8) for s in range(NS)]
                for n, (state, t, w) in enumerate(reads):
                    for j in range(4):
                        for m in range(0, P, 32):
                            g = m // 64
                            pe.matmul(yb[m:m + 32, j, t:t + w], state(j)[:, m % 64:m % 64 + 32],
                                      ARx[:, j, 2 + g, 256 + t:256 + t + w], start=n == 0 and j == 0, stop=False,
                                      skip_group_check=True)
                pe.wait_ge(x_ready, 5)
                for h in range(HB):
                    ins = pe.matmul(psU[0:96, hv(h)], TT[0:96, 2, h, 0:96], xb[0:96, hv(h)], start=True, stop=True)
                ins.then_inc(u_full, 1)
                for h in range(HB):
                    pe.matmul(yo2(h), vr[0:96, 2, hv(h)], Ark[0:96, 2, h, 0:96], start=False, stop=False,
                              skip_group_check=True)
                pe.wait_ge(u_ready, 5)
                for h in range(HB):
                    ins = pe.matmul(yo2(h), ub[0:96, hv(h)], Arb[0:96, 2, h, 0:96], start=False, stop=True,
                                    skip_group_check=True)
                ins.then_inc(y_full, 1)
                pe.wait_ge(x0_free, 8)
                for j in range(4):
                    pe.wait_ge(spread, 2 * j + 2)
                    pe.wait_ge(spread_u, 2 * j + 2)
                    for k in range(2):
                        for h in (2 * j, 2 * j + 1):
                            half = slice(64 * (h % 2), 64 * (h % 2) + 64)
                            pe.matmul(ps2[half, j, :], bk[:, k, 4, hv(h)], uv[:, h % 4, k, 0:8].rearrange("p s v -> p (s v)"),
                                      start=k == 0, stop=k == 1)
                    for h in (2 * j, 2 * j + 1):
                        half = slice(64 * (h % 2), 64 * (h % 2) + 64)
                        for k in range(2):
                            ins = pe.matmul(psSt[half, hv(j)], bk[:, k, 4, hv(h)], uv[:, h % 4, k, 8], start=k == 0,
                                            stop=k == 1)
                    ins.then_inc(spread_used, 1)

            @block.vector
            def _(dve):
                pend = lambda c: pinc[:, :, c:c + 1].to_broadcast([P, 4, HN])
                for c in range(4):
                    pb = 64 * (c % 2)
                    dve.wait_ge(x_full, c + 1)
                    if c == 0:
                        dve.wait_ge(z7, 2)
                    dve.tensor_copy(xb[pb:pb + 64], psX[pb:pb + 64]).then_inc(x_ready, 1)
                    if c:
                        dve.tensor_tensor(std[:], st[:, (c - 1) % 2], pend(64 * c + 63), ALU.mult).then_inc(std_done, 1)
                        dve.wait_ge(std_done, c)
                    dve.wait_ge(st_full, c + 1)
                    src = psSt[:, 0:256].rearrange("p (j v) -> p j v", j=4)
                    if c:
                        dve.tensor_tensor(st[:, c % 2], src, std[:], ALU.add).then_inc(st_done, 1)
                    else:
                        dve.tensor_copy(st[:, 0], src).then_inc(st_done, 1)
                    for h in (2 * c, 2 * c + 1):
                        dve.wait_ge(x0_full, h + 1)
                        if h:
                            dve.wait_ge(xs_ready, h)
                        dve.tensor_tensor(xm[0:96], ps2[0:96, h % 4, :].rearrange("p (s v) -> p s v", s=NS),
                                          seq9[0:96, 0:8].unsqueeze(2).to_broadcast([96, NS, HN]), ALU.mult).then_inc(x0_free, 1)
                        dve.wait_ge(x0_free, h + 1)
                        dve.tensor_reduce(xs[0:96, h], xm[0:96].rearrange("p s v -> p v s"), AX, ALU.add).then_inc(xs_ready, 1)
                dve.wait_ge(st_done, 4)
                dve.wait_ge(xs_ready, 8)
                dve.wait_ge(x_full, 5)
                xsf = xs[0:96].rearrange("p h v -> p (h v)")
                dve.scalar_tensor_tensor(out=xsf, in0=psX[0:96], scalar=seq9[0:96, 8:9], in1=xsf, op0=ALU.mult,
                                         op1=ALU.add).then_inc(xs_ready, 1)
                dve.wait_ge(xs_ready, 9)
                dve.tensor_tensor(xb[0:96], psU[0:96], xsf, ALU.add).then_inc(x_ready, 1)
                dve.wait_ge(u_ready, 5)
                for h in range(HB):
                    if h >= 4:
                        dve.wait_ge(spread_used, (h - 4) // 2 + 1)
                    dve.tensor_tensor(uv[:, h % 4, 0], ub[:, hv(h)].unsqueeze(1).to_broadcast([P, 9, HN]),
                                      seq9.unsqueeze(2).to_broadcast([P, 9, HN]), ALU.mult).then_inc(spread_u, 1)
                dve.wait_ge(y_full, 5)
                for j in range(4):
                    last = pinc[:, j, SAMP0:C].rearrange("p (s l) -> p s l", l=8)[:, :, 7:8]
                    dve.tensor_tensor(ss[:, j], ss[:, j], last.to_broadcast([P, NS, HN]), ALU.mult).then_inc(ns_mul, 1)
                dve.tensor_tensor(std[:], st[:, 1], pend(PROMPT - 1), ALU.mult).then_inc(ns_mul, 1)
                dve.wait_ge(ns_mul, 5)
                for j in range(4):
                    dve.wait_ge(spread_used, j + 1)
                    dve.tensor_tensor(ss[:, j], ss[:, j], ps2[:, j, :].rearrange("p (s v) -> p s v", s=NS),
                                      ALU.add).then_inc(ns_free, 1)
                dve.tensor_tensor(st[:, 0], psSt[:, 0:256].rearrange("p (j v) -> p j v", j=4), std[:],
                                  ALU.add).then_inc(st_done, 1)

            @block.scalar
            def _(act):
                for c in range(4):
                    pb = 64 * (c % 2)
                    act.wait_ge(u_full, c + 1)
                    act.activation(ub[pb:pb + 64], psU[pb:pb + 64], ACT.Copy).then_inc(u_ready, 1)
                    act.wait_ge(y_full, c + 1)
                    act.activation(yT[:, :, 64 * c:64 * c + 64], psY[:, 0:256].rearrange("p (j t) -> p j t", j=4),
                                   ACT.Copy).then_inc(y_taken, 1)
                act.wait_ge(u_full, 5)
                act.activation(ub[0:96], psU[0:96], ACT.Copy).then_inc(u_ready, 1)
                act.wait_ge(y_full, 5)
                act.activation(yT[:, :, 256:C], psY[:, 0:384].rearrange("p (j t) -> p j t", j=4), ACT.Copy).then_inc(y_taken, 1)
        ps7.free()
        m7.free()
        m6.free()

        yc, ysq = Bt, Kt
        m9 = Mem()
        wo = m9.sb("wo", [P, 8, D])
        x1 = zflat[:, 0:3 * D].rearrange("p (i d) -> p i d", i=3)
        rs9 = m9.sb("rs9", [P, 16])
        r8 = m9.sb("r8", [8, 2, C])
        xn9 = m9.sb("xn9", [P, 3, D])
        norm2_row = zflat[:, 3 * D:4 * D]
        ps9 = Mem()
        pmix = ps9.ps("pmix", [P, 6, 512])
        ptr = ps9.ps("ptr", [P, 2, 4, P])
        pstat = ptr[:].rearrange("p a b c -> p a (b c)")
        wo_in = [16 * (len(range(g, ITEMS, 4)) + 1) for g in range(4)]
        (mu_full, c_ready, ysq_ready, var_full, sd_ready, mix_ready, mix_full, x1_ready, sq9d, rt9, rc9, rn9,
         tr9_full, xh_done, xl_done, inv_ready, y_scaled, spread_full) = (sem(n) for n in (
             "mu_full", "c_ready", "ysq_ready", "var_full", "sd_ready", "mix_ready", "mix_full", "x1_ready",
             "sq9d", "rt9", "rc9", "rn9", "tr9_full", "xh_done", "xl_done", "inv_ready", "y_scaled", "spread_full"))
        KEEP = [[(META, P, 0)], [(0, P, P - META)], [(0, 16, 240), (32, 96, 256)]]
        with nc.Block() as block:
            @block.sync
            def _(sp):
                for g in range(4):
                    sp.dma_start(wo[:, 2 * g:2 * g + 2], inp["w_out"][:, 2 * g:2 * g + 2]).then_inc(w_in_slot[g], 16)
                sp.dma_start(x1, inp["x_rows"].rearrange("k p d -> p k d")).then_inc(rows_in, 16)
                sp.dma_start(norm2_row, inp["norm2"].to_broadcast([P, D])).then_inc(rows_in, 16)
                for i in range(3):
                    sp.wait_ge(x1_ready, i + 1)
                    for a, b, c0 in KEEP[i]:
                        sp.dma_start(x1_dram[c0:c0 + b - a], x1[a:b, i]).then_inc(rows_out, 16)
                sp.wait_ge(rows_out, 64)

            @block.tensor
            def _(pe):
                def product(i, g, f):
                    return pe.matmul(pmix[0:TW[i], 2 * i + g], mixT[:, f, P * i:P * i + TW[i]],
                                     wo[:, f, 512 * g:512 * g + 512], start=f == 0, stop=f == 7)

                for j in range(4):
                    if j >= 2:
                        pe.wait_ge(c_ready, j - 1)
                    pe.matmul(pstat[:, j % 2, 0:C], masks[:, M_B64], yT[:, j], start=True, stop=True).then_inc(mu_full, 1)
                for f in range(4):
                    if f % 2 == 0:
                        pe.wait_ge(w_in_slot[f // 2], wo_in[f // 2])
                    for i in range(3):
                        for g in range(2):
                            product(i, g, f)
                    if f == 0:
                        pe.wait_ge(c_ready, 4)
                        pe.wait_ge(ysq_ready, 4)
                        for j in range(4):
                            ins = pe.matmul(pstat[0:8, 0, 0:C], row_sum_r(j), ysq[:, j], start=j == 0, stop=j == 3)
                        ins.then_inc(var_full, 1)
                    if f == 1:
                        pe.wait_ge(inv_ready, 1)
                        for j in range(4):
                            if j >= 2:
                                pe.wait_ge(y_scaled, j - 1)
                            pe.matmul(pstat[:, j % 2, 0:C], spread8(j), r8[:, 1], start=True, stop=True).then_inc(spread_full, 1)
                def transposes(i):
                    w = TW[i]
                    pe.wait_ge(rn9, i + 1)
                    for n in range(KD * i, KD * i + KD):
                        if n == 0:
                            pe.wait_ge(y_scaled, 4)
                        if n % 4 == 0 and n >= 8:
                            pe.wait_ge(xl_done, n // 4 - 1)
                        ins = pe.transpose(ptr[:, n // 4 % 2, n % 4, 0:w], xn9[0:w, i, P * (n % KD):P * (n % KD) + P],
                                           ident[0:w, 0:w])
                        if n % 4 == 3:
                            ins.then_inc(tr9_full, 1)

                for i in range(3):
                    for f in range(4, 8):
                        if i == 0:
                            pe.wait_ge(mix_ready, f - 3)
                            if f % 2 == 0:
                                pe.wait_ge(w_in_slot[f // 2], wo_in[f // 2])
                        for g in range(2):
                            ins = product(i, g, f)
                    ins.then_inc(mix_full, 1)
                    if i:
                        transposes(i - 1)
                transposes(2)

            @block.scalar
            def _(act):
                for j in range(4):
                    act.wait_ge(c_ready, j + 1)
                    act.activation(ysq[:, j], yc[:, j], ACT.Square).then_inc(ysq_ready, 1)
                act.wait_ge(var_full, 1)
                act.activation(r8[:, 0], pstat[0:8, 0, 0:C], ACT.Sqrt, bias=epsc[0:8, 1:2], scale=1.0 / HN).then_inc(sd_ready, 1)

                def root(i):
                    w = TW[i]
                    act.wait_ge(x1_ready, i + 1)
                    if i == 0:
                        act.wait_ge(states_out, 80)
                    act.activation(xn9[0:w, i], x1[0:w, i], ACT.Square, accum_out=rs9[0:w, i:i + 1]).then_inc(sq9d, 1)
                    act.wait_ge(sq9d, i + 1)
                    act.activation(rs9[0:w, 3 + i:4 + i], rs9[0:w, i:i + 1], ACT.Sqrt, bias=epsc[0:w, 0:1],
                                   scale=1.0 / D).then_inc(rt9, 1)

                def high(i):
                    for g in range(2):
                        act.wait_ge(tr9_full, 2 * i + g + 1)
                        for a, b, c0 in KEEP[i]:
                            ins = act.activation(xh[:, 4 * g:4 * g + 4, c0:c0 + b - a], ptr[:, g, :, a:b], ACT.Copy)
                        ins.then_inc(xh_done, 1)

                for i in range(3):
                    root(i)
                    high(i)

            @block.vector
            def _(dve):
                link = linker(dve, dve_chain)
                for j in range(4):
                    dve.wait_ge(mu_full, j + 1)
                    dve.scalar_tensor_tensor(out=yc[:, j], in0=pstat[:, j % 2, 0:C], scalar=-1.0 / HN, in1=yT[:, j],
                                             op0=ALU.mult, op1=ALU.add).then_inc(c_ready, 1)
                dve.wait_ge(sd_ready, 1)
                dve.reciprocal(r8[:, 1], r8[:, 0]).then_inc(inv_ready, 1)
                for j in range(4):
                    dve.tensor_scalar(yc[:, j], yc[:, j], col("ln_w", j), None, ALU.mult)
                    ins = dve.tensor_scalar(bonusT[:, j], bonusT[:, j], col("ln_b", j), None, ALU.add)
                link(ins)
                for j in range(4):
                    dve.wait_ge(spread_full, j + 1)
                    dve.tensor_tensor(yc[:, j], yc[:, j], pstat[:, j % 2, 0:C], ALU.mult).then_inc(y_scaled, 1)
                dve.wait_ge(y_scaled, 4)
                link(dve.tensor_tensor(yc[:], yc[:], bonusT[:], ALU.add))
                for j in range(4):
                    dve.tensor_tensor(mixT[:, 4 + j], yc[:, j], gT[:, j], ALU.mult).then_inc(mix_ready, 1)
                dve.wait_ge(rows_in, 32)

                def add_and_scale(i):
                    w = TW[i]
                    dve.wait_ge(mix_full, i + 1)
                    dve.tensor_tensor(x1[0:w, i], x1[0:w, i], pmix[0:w, 2 * i:2 * i + 2].rearrange("p a b -> p (a b)"),
                                      ALU.add).then_inc(x1_ready, 1)
                    dve.wait_ge(rt9, i + 1)
                    dve.reciprocal(rs9[0:w, 6 + i:7 + i], rs9[0:w, 3 + i:4 + i]).then_inc(rc9, 1)
                    dve.wait_ge(rc9, i + 1)
                    dve.scalar_tensor_tensor(out=xn9[0:w, i], in0=x1[0:w, i], scalar=rs9[0:w, 6 + i:7 + i],
                                             in1=norm2_row[0:w], op0=ALU.mult, op1=ALU.mult).then_inc(rn9, 1)

                def low(i):
                    for g in range(2):
                        dve.wait_ge(xh_done, 2 * i + g + 1)
                        for a, b, c0 in KEEP[i]:
                            ins = dve.tensor_tensor(xl[:, 4 * g:4 * g + 4, c0:c0 + b - a], ptr[:, g, :, a:b],
                                                    xh[:, 4 * g:4 * g + 4, c0:c0 + b - a], ALU.subtract)
                        ins.then_inc(xl_done, 1)

                for i in range(3):
                    add_and_scale(i)
                    low(i)
        ps9.free()
        m9.free()
        y_mem.free()
        zb_mem.free()
        mix_mem.free()
        mask_mem.free()

        NQ, NA = 16, 48
        NG = NBLK - NA
        assert 4 * NG == NT and NA % 2 == 0
        PICKED = NA // 2 - 3
        big_mem = Mem()
        hid = big_mem.sb("hid", [P, NBLK, NT])
        hflat = hid[:].rearrange("p b t -> p (b t)")
        raw_mem = Mem()
        raw = [raw_mem.sb(f"raw{r}", [P, 2, 256]) for r in range(4)]
        ring = Mem()
        hi = [ring.sb(f"hi{u}", [P, 2, P], F32R) for u in range(4)]
        lo = [ring.sb(f"lo{u}", [P, 2, P], F32R) for u in range(4)]
        wide = lambda a: a[:].rearrange("p k n -> p (k n)")
        RT = ring.sb("RT", [P, 3, NT])
        act_h = [ring.sb(f"act_h{q}", [P, NT]) for q in range(2)]
        oh1 = [ring.sb(f"oh1_{s}", [P, 2, NK]) for s in range(2)]
        oh2 = [ring.sb(f"oh2_{s}", [P, 2, NK]) for s in range(2)]
        at = [(NBLK * NT)]

        def scratch(*shape):
            n = int(np.prod(shape))
            at[0] -= n
            names_ = "abcd"[:len(shape)]
            flat = hflat[:, at[0]:at[0] + n]
            if len(shape) == 1:
                return flat
            return flat.rearrange(f"p ({' '.join(names_)}) -> p {' '.join(names_)}", **dict(zip(names_, shape)))

        sc = scratch(3, NQ, NK)
        qpT = scratch(2, NT)
        keysT = scratch(2, NK)
        top = scratch(16, TOPK)
        topi = scratch(16, TOPK).bitcast(U32)
        topf = scratch(16, TOPK)
        cand = scratch(PH, TOPK, TOPK)
        best = scratch(3, PH, TOPK)
        flat = scratch(PH, TOPK).bitcast(U32)
        rank = scratch(2, PH, TOPK).bitcast(U32)
        rankf = scratch(2, PH, TOPK)
        pick = scratch(2, PH, TOPK, TOPK)
        picked = scratch(3, 3, P)
        gsum = scratch(2, PH)
        CLEAN = NA * NT
        DIRTY = at[0]
        PIECE = (NBLK * NT - DIRTY) // 3 // 16
        LAST = NBLK * NT - 16 * PIECE
        assert DIRTY > CLEAN + PIECE
        ps10 = Mem()
        ph = ps10.ps("ph", [P, 2, 512])
        pss = ps10.ps("pss", [P, 2, 4, P])
        pg = ps10.ps("pg", [P, 2, 4, NK])
        ptp = [ps10.ps("ptp", [P, 4, P])] + [pg[:, q] for q in range(2)]
        t_in = [sem(f"t_in{r}") for r in range(4)]
        (keys_in, t_hi, lo_dve, lo_pool, t_mm, q_ready, s_full, s_ready, e_in, e_out, pk_ready, pt_full, rt_ready,
         ones_set, ones_set_dve, ones_set_act, h_done, g_done, h_used, oh_ready, g_mm, g_used) = (sem(n) for n in (
             "keys_in", "t_hi", "lo_dve", "lo_pool", "t_mm", "q_ready", "s_full", "s_ready", "e_in", "e_out",
             "pk_ready", "pt_full", "rt_ready", "ones_set", "ones_set_dve", "ones_set_act", "h_done", "g_done", "h_used",
             "oh_ready", "g_mm", "g_used"))
        NEG = -3.0e38
        QU = 4 * NQ
        with nc.Block() as block:
            @block.sync
            def _(sp):
                for n in range(2 * NQ):
                    if n >= 4:
                        sp.wait_ge(lo_dve, 2 * (n - 3))
                    sp.dma_start(wide(raw[n % 4]), inp["w_q"][n // 2, :, 4 * (n % 2):4 * (n % 2) + 4, :]
                                 .rearrange("p k n -> p (k n)")).then_inc(t_in[n % 4], 16)
                    if n == 3:
                        sp.dma_start(keysT, inp["keysT"]).then_inc(keys_in, 16)

                def block_half(b, r):
                    src = inp["uT"][bass.ds(b, 1), :, 4 * (r % 2):4 * (r % 2) + 4, :]
                    sp.dma_start(wide(raw[r]), src.rearrange("b p k n -> p (b k n)")).then_inc(t_in[r], 16)

                for r in range(4):
                    sp.wait_ge(lo_dve, QU - 6 + 2 * r)
                    block_half(r // 2, r)
                with sp.Fori(1, NA // 2) as i:
                    for r in range(4):
                        sp.wait_ge(lo_pool, 8 * i + (2 * r - 6))
                        block_half(2 * i + r // 2, r)
                for r in range(4):
                    sp.wait_ge(lo_pool, 4 * NA - 6 + 2 * r)
                    block_half(NA + r // 2, r)
                with sp.Fori(1, NG // 2) as i:
                    for r in range(4):
                        sp.wait_ge(t_mm, QU + 4 * NA + 8 * i + (2 * r - 6))
                        block_half(2 * i + (NA + r // 2), r)
                for r in range(4):
                    sp.wait_ge(t_mm, QU + 4 * NBLK - 6 + 2 * r)
                    sp.dma_start(wide(raw[r]), inp["v"][r // 2, :, 512 * (r % 2):512 * (r % 2) + 512]).then_inc(t_in[r], 16)

            @block.gpsimd
            def _(pool):
                pool.memset(hflat[:, CLEAN:DIRTY], 1.0).then_inc(ones_set, 1)

                def low(u, n):
                    pool.wait_ge(t_hi, n)
                    pool.tensor_tensor(wide(lo[u % 4]), raw[u // 2][:, u % 2], wide(hi[u % 4]),
                                       ALU.subtract).then_inc(lo_pool, 1)
                with pool.Fori(0, NA // 2) as i:
                    for u in range(8):
                        low(u, QU + 8 * i + (u + 1))
                with pool.Fori(0, NG // 2) as i:
                    for u in range(1, 8, 2):
                        low(u, QU + 4 * NA + 8 * i + (u + 1))

            @block.scalar
            def _(act):
                def high(u, landed, n, reuse=True):
                    if u % 2 == 0:
                        act.wait_ge(t_in[u // 2], landed)
                    if reuse:
                        act.wait_ge(t_mm, n - 3)
                    act.activation(wide(hi[u % 4]), raw[u // 2][:, u % 2], ACT.Copy).then_inc(t_hi, 1)

                for n in range(NQ + 1):
                    if n < NQ:
                        for u in range(4):
                            m = 4 * n + u
                            high(m % 8, 16 * (n // 2 + 1), m, m >= 4)
                    if n >= 1:
                        m = n - 1
                        act.wait_ge(t_mm, 4 * n)
                        if m >= 2:
                            act.wait_ge(s_full, m - 1)
                        act.activation(qpT[:, m % 2], ph[:, m % 2, 0:NT], ACT.Copy).then_inc(q_ready, 1)
                    if n >= 2:
                        m = n - 2
                        act.wait_ge(s_full, m + 1)
                        act.activation(sc[:, 0:2, m], pss[:, m % 2, 0:2], ACT.Copy)
                        act.activation(sc[0:64, 2, m], pss[0:64, m % 2, 2], ACT.Copy).then_inc(s_ready, 1)
                m = NQ - 1
                act.wait_ge(s_full, m + 1)
                act.activation(sc[:, 0:2, m], pss[:, m % 2, 0:2], ACT.Copy)
                act.activation(sc[0:64, 2, m], pss[0:64, m % 2, 2], ACT.Copy).then_inc(s_ready, 1)

                def gelu(b, q, quarters):
                    act.wait_ge(t_mm, quarters)
                    act.activation(hid[:, bass.ds(b, 1), :].rearrange("p b t -> p (b t)"), ph[:, q, 0:NT],
                                   ACT.Gelu).then_inc(h_done, 1)

                def step_a(i, first, pieces=None):
                    for u in range(8):
                        high(u, 16 * (NQ // 2 + 1) + 16 * i, QU + 8 * i + u)
                        for p in pieces[u] if pieces else ():
                            if p == 0:
                                act.wait_ge(ones_set, 1)
                                act.wait_ge(rt_ready, 3)
                            act.activation(hflat[:, LAST + p * PIECE:LAST + (p + 1) * PIECE], hflat[:, CLEAN:CLEAN + PIECE],
                                           ACT.Copy).then_inc(ones_set_act, 1)
                        if u == 3 and not first:
                            gelu(2 * i - 1, 1, QU + 8 * i)
                        if u == 7:
                            gelu(2 * i, 0, QU + 8 * i + 4)
                step_a(0, True)
                with act.Fori(1, PICKED) as i:
                    step_a(i, False)
                act.wait_ge(e_in, 3)
                act.activation(best, best, ACT.Exp).then_inc(e_out, 1)
                with act.Fori(PICKED, NA // 2 - 2) as i:
                    step_a(i, False)
                step_a(NA // 2 - 2, False, [(), (), (), (), (0,), (1,), (2, 3), (4, 5)])
                step_a(NA // 2 - 1, False, [(6,), (7,), (8,), (9,), (10,), (11,), (12, 13), (14, 15)])
                gelu(NA - 1, 1, QU + 4 * NA)

                def gelu_b(q, quarters, used):
                    act.wait_ge(t_mm, quarters)
                    if used is not None:
                        act.wait_ge(h_used, used)
                    act.activation(act_h[q][:], ph[:, q, 0:NT], ACT.Gelu).then_inc(g_done, 1)

                def step_b(i, first, second):
                    q0 = QU + 4 * NA
                    for u in range(8):
                        high(u, 16 * (NQ // 2 + 1 + NA // 2) + 16 * i, q0 + 8 * i + u)
                        if u == 1 and not first:
                            gelu_b(1, q0 + 8 * i, None if second else 2 * i - 2)
                        if u == 5:
                            gelu_b(0, q0 + 8 * i + 4, None if first else 2 * i - 1)
                step_b(0, True, False)
                step_b(1, False, True)
                with act.Fori(2, NG // 2) as i:
                    step_b(i, False, False)
                gelu_b(1, QU + 4 * NBLK, NG - 2)

            @block.tensor
            def _(pe):
                def quarter(o, u, sub):
                    s = u % 4
                    for k in range(2):
                        c = 2 * sub + k
                        begin, end = c == 0, c == KD - 1
                        pe.matmul(o, hi[s][:, k], xh[:, c], start=begin, stop=False)
                        pe.matmul(o, hi[s][:, k], xl[:, c], start=False, stop=False)
                        ins = pe.matmul(o, lo[s][:, k], xh[:, c], start=False, stop=end)
                    ins.then_inc(t_mm, 1)

                for n in range(NQ + 1):
                    if n < NQ:
                        if n >= 2:
                            pe.wait_ge(q_ready, n - 1)
                        for u in range(4):
                            pe.wait_ge(lo_dve, 4 * n + u + 1)
                            quarter(ph[:, n % 2, 0:NT], u, u)
                    if n:
                        m = n - 1
                        if m == 0:
                            pe.wait_ge(keys_in, 16)
                        pe.wait_ge(q_ready, m + 1)
                        if m >= 2:
                            pe.wait_ge(s_ready, m - 1)
                        for i, (c0, w) in enumerate(PT):
                            ins = pe.matmul(pss[0:w, m % 2, i], qpT[:, m % 2, c0:c0 + w], keysT[:, m % 2], start=True,
                                            stop=True)
                        ins.then_inc(s_full, 1)

                def step_a(i, first):
                    for u in range(8):
                        if u % 4 == 0 and not first:
                            pe.wait_ge(h_done, 2 * i + (u // 4 - 1))
                        pe.wait_ge(lo_pool, 8 * i + (u + 1))
                        quarter(ph[:, u // 4, 0:NT], u, u % 4)
                step_a(0, True)
                with pe.Fori(1, PICKED + 1) as i:
                    step_a(i, False)
                pe.wait_ge(pk_ready, 3)
                for i, (c0, w) in enumerate(PT):
                    for k in range(3):
                        ins = pe.transpose(ptp[i][:, k, 0:w], picked[0:w, i, k], ident[0:w, 0:w])
                    ins.then_inc(pt_full, 1)
                with pe.Fori(PICKED + 1, NA // 2) as i:
                    step_a(i, False)

                def step_b(i, first):
                    for q in range(2):
                        if not first:
                            pe.wait_ge(g_used, 2 * i + (q - 1))
                        for s in range(2):
                            pe.wait_ge(oh_ready, 4 * i + (2 * q + s + 1))
                            for t in range(2):
                                ins = pe.matmul(pg[:, q, 2 * s + t], oh2[s][:, t], oh1[s][:, t], start=True, stop=True)
                            ins.then_inc(g_mm, 1)
                        if first:
                            pe.wait_ge(h_done, NA - 1 + q)
                        else:
                            pe.wait_ge(g_done, 2 * i + (q - 1))
                        for u in range(4):
                            if u % 2 == 0:
                                pe.wait_ge(lo_dve, QU + 4 * i + (2 * q + u // 2 + 1))
                            else:
                                pe.wait_ge(lo_pool, 4 * NA + 4 * i + (2 * q + u // 2 + 1))
                            quarter(ph[:, q, 0:NT], u, u)
                step_b(0, True)
                with pe.Fori(1, NG // 2) as i:
                    step_b(i, False)

            @block.vector
            def _(dve):
                link = linker(dve, dve_chain)

                def low(u, n):
                    dve.wait_ge(t_hi, n)
                    dve.tensor_tensor(wide(lo[u % 4]), raw[u // 2][:, u % 2], wide(hi[u % 4]),
                                      ALU.subtract).then_inc(lo_dve, 1)
                for n in range(QU):
                    low(n % 8, n + 1)
                dve.wait_ge(s_ready, NQ)

                def top16(values, index, source, groups):
                    for half in range(2):
                        e = slice(8 * half, 8 * half + 8)
                        for g in range(groups):
                            ins = dve.max(values(g)[:, e], source(g))
                        link(ins)
                        for g in range(groups):
                            ins = dve.max_index(index(g)[:, e], values(g)[:, e], source(g))
                        link(ins)
                        if half == 0:
                            for g in range(groups):
                                ins = dve.match_replace(out=source(g), in_to_replace=values(g)[:, e], in_values=source(g),
                                                        imm_value=NEG)
                            link(ins)

                dve.memset(best, 0.0).then_inc(ones_set_dve, 1)
                dve.wait_ge(ones_set_dve, 1)
                for i, (c0, w) in enumerate(PT):
                    top16(lambda g: top[0:w, g], lambda g: topi[0:w, g], lambda g: sc[0:w, i, g], 16)
                    dve.tensor_copy(topf[0:w], topi[0:w])
                    pairs = top[0:w].rearrange("p (h a) k -> p h a k", a=2)
                    link(dve.tensor_tensor(cand[0:w], pairs[:, :, 0, :].unsqueeze(3).to_broadcast([w, PH, TOPK, TOPK]),
                                           pairs[:, :, 1, :].unsqueeze(2).to_broadcast([w, PH, TOPK, TOPK]), ALU.add))
                    top16(lambda g: best[0:w, i, g], lambda g: flat[0:w, g],
                          lambda g: cand[0:w, g].rearrange("p a b -> p (a b)"), PH)
                    link(dve.tensor_copy(gsum[0:w, 0], best[0:w, i, :, 0]))
                    dve.tensor_tensor(best[0:w, i], best[0:w, i], gsum[0:w, 0].unsqueeze(2).to_broadcast([w, PH, TOPK]),
                                      ALU.subtract).then_inc(e_in, 1)
                    dve.tensor_single_scalar(rank[0:w, 0], flat[0:w], 4, ALU.logical_shift_right)
                    link(dve.tensor_single_scalar(rank[0:w, 1], flat[0:w], TOPK - 1, ALU.bitwise_and))
                    link(dve.tensor_copy(rankf[0:w], rank[0:w]))
                    keys = lambda a: topf[0:w].rearrange("p (h a) k -> p h a k", a=2)[:, :, a, :].unsqueeze(2)
                    four = [w, PH, TOPK, TOPK]
                    for a in range(2):
                        ins = dve.tensor_tensor(pick[0:w, a], rankf[0:w, a].unsqueeze(3).to_broadcast(four),
                                                iota[0:w, 0:TOPK].unsqueeze(1).unsqueeze(1).to_broadcast(four), ALU.is_equal)
                    link(ins)
                    for a in range(2):
                        ins = dve.tensor_tensor(pick[0:w, a], pick[0:w, a], keys(a).to_broadcast(four), ALU.mult)
                    link(ins)
                    for a in range(2):
                        ins = dve.tensor_reduce(picked[0:w, i, a].rearrange("p (h k) -> p h k", h=PH), pick[0:w, a], AX, ALU.add)
                    link(ins)
                for i, (c0, w) in enumerate(PT):
                    if i == 0:
                        dve.wait_ge(e_out, 1)
                    link(dve.tensor_reduce(gsum[0:w, 0], best[0:w, i], AX, ALU.add))
                    link(dve.reciprocal(gsum[0:w, 1], gsum[0:w, 0]))
                    dve.tensor_tensor(picked[0:w, i, 2].rearrange("p (h k) -> p h k", h=PH), best[0:w, i],
                                      gsum[0:w, 1].unsqueeze(2).to_broadcast([w, PH, TOPK]), ALU.mult).then_inc(pk_ready, 1)
                for i, (c0, w) in enumerate(PT):
                    dve.wait_ge(pt_full, i + 1)
                    dve.tensor_copy(RT[:, :, c0:c0 + w], ptp[i][:, 0:3, 0:w]).then_inc(rt_ready, 1)
                dve.wait_ge(rt_ready, 3)
                dve.memset(hflat[:, DIRTY:LAST], 1.0).then_inc(ones_set_dve, 1)
                dve.wait_ge(ones_set_dve, 2)
                dve.wait_ge(ones_set_act, 16)
                dve.wait_ge(ones_set, 1)
                dve.wait_ge(h_done, NA)

                def times_gates(t0, q, group):
                    dve.wait_ge(g_mm, group)
                    h = hid[:, :, bass.ds(t0, 4)]
                    dve.tensor_tensor(h, h, pg[:, q].rearrange("p t k -> p k t"), ALU.mult).then_inc(g_used, 1)

                def times_hidden(b, q, done):
                    dve.wait_ge(g_done, done)
                    h = hid[:, bass.ds(b, 1), :].rearrange("p b t -> p (b t)")
                    dve.tensor_tensor(h, h, act_h[q][:], ALU.mult).then_inc(h_used, 1)

                def step_b(i, first):
                    for q in range(2):
                        none = first and q == 0
                        for s in range(2):
                            if not none:
                                dve.wait_ge(g_mm, 4 * i + (2 * q + s - 1))
                            t0 = 8 * i + (4 * q + 2 * s)
                            for t in range(2):
                                dve.tensor_scalar(oh1[s][:, t], iota[:], RT[:, 0, bass.ds(t0 + t, 1)],
                                                  RT[:, 2, bass.ds(t0 + t, 1)], ALU.is_equal, ALU.mult)
                            dve.tensor_tensor(oh2[s][:], iota[:].unsqueeze(1).to_broadcast([P, 2, NK]),
                                              RT[:, 1, bass.ds(t0, 2)].unsqueeze(2).to_broadcast([P, 2, NK]),
                                              ALU.is_equal).then_inc(oh_ready, 1)
                        low(4 * q, QU + 4 * NA + 8 * i + (4 * q + 1))
                        if not none:
                            if not (first and q == 1):
                                dve.wait_ge(h_used, 2 * i + (q - 1))
                            times_gates(8 * i + (4 * q - 4), 1 - q, 4 * i + 2 * q)
                        low(4 * q + 2, QU + 4 * NA + 8 * i + (4 * q + 3))
                        if not none:
                            dve.wait_ge(g_used, 2 * i + q)
                            times_hidden(2 * i + (NA + q - 1), 1 - q, 2 * i + q)
                step_b(0, True)
                with dve.Fori(1, NG // 2) as i:
                    step_b(i, False)
                dve.wait_ge(h_used, NG - 1)
                times_gates(NT - 4, 1, 2 * NG)
                dve.wait_ge(g_used, NG)
                times_hidden(NBLK - 1, 1, NG)
        ps10.free()
        ring.free()

        ring = Mem()
        hi = [ring.sb(f"hi{u}", [P, 4, P], F32R) for u in range(4)]
        lo = [ring.sb(f"lo{u}", [P, 4, P], F32R) for u in range(4)]
        x2 = hflat[:, 0:3 * D].rearrange("p (i d) -> p i d", i=3)
        nf = hflat[:, 3 * D:4 * D]
        assert 9 * D + 16 <= NBLK // 2 * NT
        ch = [xh[:, s] for s in range(2)]
        cl = [xl[:, s] for s in range(2)]
        ps13 = Mem()
        acc = ps13.ps("acc", [P, KD, 512])
        STEPS = NBLK // 2
        V0 = 16 * (NQ // 2 + NBLK // 2)
        v_hi, v_lo, v_mm, c_hi, c_lo = (sem(n) for n in ("v_hi", "v_lo", "v_mm", "c_hi", "c_lo"))
        with nc.Block() as block:
            @block.sync
            def _(sp):
                def step(i):
                    for u in range(4):
                        sp.wait_ge(v_lo, 4 * i + (u - 3))
                        src = inp["v"][bass.ds(2 * i + u // 2, 1), :, 512 * (u % 2):512 * (u % 2) + 512]
                        sp.dma_start(wide(raw[u]), src.rearrange("b p n -> p (b n)")).then_inc(t_in[u], 16)
                with sp.Fori(1, STEPS) as i:
                    step(i)
                sp.wait_ge(c_lo, NBLK // 2)
                for i, (c0, w) in enumerate(PT):
                    sp.dma_start(x2[0:w, i], x1_dram[c0:c0 + w]).then_inc(rows_in, 16)
                sp.dma_start(nf, inp["norm_f"].to_broadcast([P, D])).then_inc(rows_in, 16)

            @block.scalar
            def _(act):
                def step(i, first):
                    for u in range(4):
                        act.wait_ge(t_in[u], 16 * i + (V0 + 16))
                        if not first:
                            act.wait_ge(v_mm, 4 * i + (u - 2 if u % 2 == 0 else u - 3))
                        if u % 2 == 0:
                            act.activation(ch[u // 2], hid[:, bass.ds(2 * i + u // 2, 1), :].rearrange("p b t -> p (b t)"),
                                           ACT.Copy).then_inc(c_hi, 1)
                        act.activation(wide(hi[u]), wide(raw[u]), ACT.Copy).then_inc(v_hi, 1)
                step(0, True)
                with act.Fori(1, STEPS) as i:
                    step(i, False)

            @block.vector
            def _(dve):
                def step(i):
                    for u in range(4):
                        if u % 2 == 0:
                            dve.wait_ge(c_hi, 2 * i + (u // 2 + 1))
                            dve.tensor_tensor(cl[u // 2], hid[:, bass.ds(2 * i + u // 2, 1), :].rearrange("p b t -> p (b t)"),
                                              ch[u // 2], ALU.subtract).then_inc(c_lo, 1)
                        dve.wait_ge(v_hi, 4 * i + (u + 1))
                        dve.tensor_tensor(wide(lo[u]), wide(raw[u]), wide(hi[u]), ALU.subtract).then_inc(v_lo, 1)
                with dve.Fori(0, STEPS) as i:
                    step(i)

            @block.tensor
            def _(pe):
                def step(i, first, last):
                    for u in range(4):
                        if u % 2 == 0:
                            pe.wait_ge(c_lo, 2 * i + (u // 2 + 1))
                        pe.wait_ge(v_lo, 4 * i + (u + 1))
                        begin, end = first and u < 2, last and u >= 2
                        for k in range(4):
                            o, s = acc[:, 4 * (u % 2) + k, 0:NT], u // 2
                            pe.matmul(o, hi[u][:, k], ch[s], start=begin, stop=False)
                            pe.matmul(o, hi[u][:, k], cl[s], start=False, stop=False)
                            ins = pe.matmul(o, lo[u][:, k], ch[s], start=False, stop=end)
                        ins.then_inc(v_mm, 1)
                step(0, True, False)
                with pe.Fori(1, STEPS - 1) as i:
                    step(i, False, False)
                step(STEPS - 1, False, True)
        ring.free()
        raw_mem.free()

        oT = hflat[:, 4 * D:4 * D + KD * NT].rearrange("p (k t) -> p k t", k=KD)
        sq14 = hflat[:, 8 * D:9 * D]
        rs14 = hflat[:, 9 * D:9 * D + 16]
        o_taken, o_taken_dve, y_full14, y_sum, sq14d, rt14, y_done = (
            sem(n) for n in ("o_taken", "o_taken_dve", "y_full14", "y_sum", "sq14d", "rt14", "y_done"))
        with nc.Block() as block:
            @block.sync
            def _(sp):
                for i, (c0, w) in enumerate(PT):
                    sp.wait_ge(y_done, i + 1)
                    sp.dma_start(out["y"][c0:c0 + w], x2[0:w, i]).then_inc(rows_out, 16)
                sp.wait_ge(rows_out, 64 + 48)

            @block.scalar
            def _(act):
                for j in range(0, KD, 2):
                    act.activation(oT[:, j], acc[:, j, 0:NT], ACT.Copy).then_inc(o_taken, 1)
                for i, (c0, w) in enumerate(PT):
                    act.wait_ge(y_sum, i + 1)
                    if i:
                        act.wait_ge(sq14d, i)
                    act.activation(sq14[0:w], x2[0:w, i], ACT.Square, accum_out=rs14[0:w, i:i + 1]).then_inc(sq14d, 1)
                    act.wait_ge(sq14d, i + 1)
                    act.activation(rs14[0:w, 3 + i:4 + i], rs14[0:w, i:i + 1], ACT.Sqrt, bias=epsc[0:w, 0:1],
                                   scale=1.0 / D).then_inc(rt14, 1)

            @block.tensor
            def _(pe):
                pe.wait_ge(o_taken, KD // 2)
                pe.wait_ge(o_taken_dve, KD // 2)
                for i, (c0, w) in enumerate(PT):
                    for j in range(KD):
                        ins = pe.transpose(acc[0:w, 2 * i + j // 4, P * (j % 4):P * (j % 4) + P], oT[:, j, c0:c0 + w], ident[:])
                    ins.then_inc(y_full14, 1)

            @block.vector
            def _(dve):
                link = linker(dve, dve_chain)
                for j in range(1, KD, 2):
                    dve.tensor_copy(oT[:, j], acc[:, j, 0:NT]).then_inc(o_taken_dve, 1)
                dve.wait_ge(rows_in, 96)
                for i, (c0, w) in enumerate(PT):
                    dve.wait_ge(y_full14, i + 1)
                    dve.tensor_tensor(x2[0:w, i], x2[0:w, i], acc[0:w, 2 * i:2 * i + 2].rearrange("p a b -> p (a b)"),
                                      ALU.add).then_inc(y_sum, 1)
                for i, (c0, w) in enumerate(PT):
                    dve.wait_ge(rt14, i + 1)
                    link(dve.reciprocal(rs14[0:w, 6 + i:7 + i], rs14[0:w, 3 + i:4 + i]))
                    dve.scalar_tensor_tensor(out=x2[0:w, i], in0=x2[0:w, i], scalar=rs14[0:w, 6 + i:7 + i], in1=nf[0:w],
                                             op0=ALU.mult, op1=ALU.mult).then_inc(y_done, 1)
        ps13.free()
        big_mem.free()
        base.free()


_LAYOUT = [("theta0", 4), ("theta1", 4), ("hgrn_norm", 4), ("mu", FB), ("w0", 4),
           ("a0", 4), ("k_k", 4), ("k_a", 4), ("r_k", 4), ("ln_w", 4), ("ln_b", 4)]
FEAT, NFEAT = {}, 0
for _name, _n in _LAYOUT:
    FEAT[_name] = NFEAT
    NFEAT += _n

_OUTS = {
    "y": (NT, D),
    "hgrn_p": (P, HA, P),
    "hgrn_s": (P, NS, HA, P),
    "rwkv_p": (P, 4, HN),
    "rwkv_s": (P, 4, NS, HN),
    "shift": (P, FB, 1 + NS),
}


def layout(inputs):
    a = {k: np.asarray(v) for k, v in inputs.items()}
    f32 = np.float32
    rows = np.concatenate([a["meta_tokens"], a["x_prompt"][0], np.zeros((SAMP0 - PROMPT, D), f32),
                           a["x_sample"].reshape(-1, D), np.zeros((3 * P - C, D), f32)])
    w_in = a["w_in"][0].reshape(KD, P, 30, P).transpose(2, 1, 0, 3)
    cols = lambda v: v.reshape(-1, P).T
    parts = {"theta0": a["lb_theta"][0], "theta1": a["lb_theta"][1],
             "hgrn_norm": a["hgrn_norm"][0], "mu": a["mu_shift"][0], "w0": a["w0"][0], "a0": a["a0"][0],
             "k_k": a["k_k"][0], "k_a": a["k_a"][0], "r_k": a["r_k"][0], "ln_w": a["ln_w"][0], "ln_b": a["ln_b"][0]}
    masks, misc = shape_constants()
    wq = a["peer_wq"][0].reshape(KD, P, 16, P).transpose(2, 1, 0, 3)
    out = {
        "x_rows": rows.reshape(3, P, D),
        "masks": masks,
        "misc": misc,
        "feat": np.concatenate([cols(parts[n]) for n, _ in _LAYOUT], axis=1),
        "norm1": a["norm1"].reshape(1, D),
        "norm2": a["norm2"].reshape(1, D),
        "w_in": np.concatenate([a["w_in"][0][:, 1024:1536].reshape(4, 2, P, 512).transpose(0, 2, 1, 3).reshape(4, P, D),
                                w_in[0:8].reshape(8, P, D), w_in[12:30].reshape(18, P, D)]),
        "shift0": a["state_shift"][0].reshape(NS, FB, P).transpose(2, 1, 0),
        "state_h": a["state_hgrn"][0].transpose(2, 0, 1, 3),
        "state_r": a["state_rwkv"][0].reshape(NS, 4, 2, HN, HN).transpose(2, 4, 1, 0, 3).reshape(P, 4, NS, HN),
        "lora": np.concatenate([np.concatenate([a["w_w2"][0], a["a_w2"][0]], axis=0), a["g_w2"][0]], axis=1),
        "w_out": a["w_out"][0].reshape(8, P, D).transpose(1, 0, 2),
        "w_q": wq,
        "keysT": a["peer_keys"][0].transpose(2, 0, 1),
        "uT": a["peer_u"][0].reshape(NK, NK, KD, P).transpose(0, 3, 2, 1),
        "v": a["peer_v"][0].reshape(NK, NK, D),
        "norm_f": a["norm_f"].reshape(1, D),
    }
    return {k: np.ascontiguousarray(v) for k, v in out.items()}


def kernel(**inputs):
    import concourse.bacc as bacc
    from concourse.bass_utils import run_bass_kernel_spmd

    arrays = layout(inputs)
    nc = bacc.Bacc("TRN2", target_bir_lowering=False, num_devices=1)
    inp = {k: nc.dram_tensor(f"in_{k}", v.shape, mybir.dt.from_np(v.dtype), kind="ExternalInput").ap()
           for k, v in arrays.items()}
    out = {k: nc.dram_tensor(f"out_{k}", s, F32, kind="ExternalOutput").ap() for k, s in _OUTS.items()}
    build_program(nc, inp, out)
    r = run_bass_kernel_spmd(nc, [{f"in_{k}": v for k, v in arrays.items()}], core_ids=[0]).results[0]
    got = {k: np.asarray(r[f"out_{k}"]) for k in _OUTS}
    y = got["y"]
    shift = got["shift"].transpose(2, 1, 0).reshape(1 + NS, FB * P)
    rwkv = lambda s: s.reshape(2, HN, 4, -1, HN).transpose(3, 2, 0, 4, 1).reshape(-1, HB, HN, HN)
    return (np.ascontiguousarray(y[:SEQ][None]),
            np.ascontiguousarray(y[SEQ:NT].reshape(NS, LS, D)),
            np.ascontiguousarray(got["hgrn_p"].transpose(1, 0, 2)[None, None]),
            np.ascontiguousarray(rwkv(got["rwkv_p"][:, :, None])[None]),
            np.ascontiguousarray(shift[None, 0:1]),
            np.ascontiguousarray(got["hgrn_s"].transpose(1, 2, 0, 3)[None]),
            np.ascontiguousarray(rwkv(got["rwkv_s"])[None]),
            np.ascontiguousarray(shift[None, 1:]))
```
